# Optimizing a Trainium2 kernel written in Bass

```python
import jax, jax.numpy as jnp
from jax import lax
import numpy as np
import math

D_MODEL = 1024
BATCH = 1
SEQ = 1024
DEPTH = 1

CHUNK = 64
N_MIXERS = 3
N_HEADS = 16
HEAD_DIM = D_MODEL // N_HEADS
Q_BLOCK = 128
SG_CHUNK = 128
SG_WIDTH = D_MODEL
SG_GROUPS = 8
SG_GROUP_DIM = SG_WIDTH // SG_GROUPS
CONV_WIDTH = 31
D_FF = 4 * D_MODEL
N_A = (DEPTH + 2) // N_MIXERS
N_B = (DEPTH + 1) // N_MIXERS
N_C = DEPTH // N_MIXERS
EPS = 1e-6


def rms_norm(x, g):
    xf = x.astype(jnp.float32)
    y = xf * lax.rsqrt(jnp.mean(xf * xf, axis=-1, keepdims=True) + EPS)
    return (y * g.astype(jnp.float32)).astype(x.dtype)

def layer_norm(x, g, b):
    xf = x.astype(jnp.float32)
    mu = jnp.mean(xf, axis=-1, keepdims=True)
    xc = xf - mu
    y = xc * lax.rsqrt(jnp.mean(xc * xc, axis=-1, keepdims=True) + EPS)
    return (y * g.astype(jnp.float32) + b.astype(jnp.float32)).astype(x.dtype)

def fox_mixer(h, w_in, b_f, q_g, k_g, w_out):
    B, S, D = h.shape
    proj = h @ w_in
    q, k, v, f_pre = jnp.split(proj, [D, 2 * D, 3 * D], axis=-1)
    q = rms_norm(q.reshape(B, S, N_HEADS, HEAD_DIM), q_g)
    k = rms_norm(k.reshape(B, S, N_HEADS, HEAD_DIM), k_g)
    v = v.reshape(B, S, N_HEADS, HEAD_DIM)
    log_f = jax.nn.log_sigmoid(f_pre.astype(jnp.float32) + b_f.astype(jnp.float32))
    F = jnp.cumsum(log_f, axis=1).transpose(0, 2, 1)
    nb = S // Q_BLOCK
    qb = q.reshape(B, nb, Q_BLOCK, N_HEADS, HEAD_DIM).swapaxes(0, 1)
    Fq = F.reshape(B, N_HEADS, nb, Q_BLOCK).transpose(2, 0, 1, 3)
    k_pos = jnp.arange(S)
    scale = HEAD_DIM ** -0.5

    def block(args):
        q_i, F_i, b_i = args
        logits = (jnp.einsum('bqhd,bkhd->bhqk', q_i, k).astype(jnp.float32) * scale
                  + (F_i[..., :, None] - F[..., None, :]))
        q_pos = b_i * Q_BLOCK + jnp.arange(Q_BLOCK)
        logits = jnp.where(k_pos[None, :] <= q_pos[:, None], logits, -jnp.inf)
        p = jax.nn.softmax(logits, axis=-1).astype(v.dtype)
        return jnp.einsum('bhqk,bkhd->bqhd', p, v)

    o = lax.map(block, (qb, Fq, jnp.arange(nb)))
    o = o.swapaxes(0, 1).reshape(B, S, D)
    return o @ w_out

def gmlp_mixer(h, w_in, ln_g, ln_b, w_s, b_s, w_out):
    B, S, _ = h.shape
    uv = jax.nn.gelu(h @ w_in)
    u, v = jnp.split(uv, 2, axis=-1)
    v = layer_norm(v, ln_g, ln_b)
    v = v.reshape(B, S // SG_CHUNK, SG_CHUNK, SG_GROUPS, SG_GROUP_DIM)
    cid = jnp.arange(SG_CHUNK) // CHUNK
    mask = cid[None, :] <= cid[:, None]
    ws = jnp.where(mask[None], w_s, jnp.zeros_like(w_s))
    v = jnp.einsum('gts,bnsgc->bntgc', ws, v) + b_s.T[:, :, None]
    v = v.reshape(B, S, SG_WIDTH)
    return (u * v) @ w_out

def conv_mixer(h, w_pw1, b_pw1, w_dw, b_dw, ln_g, ln_b, w_pw2, b_pw2):
    D = h.shape[-1]
    y = jax.nn.glu(h @ w_pw1 + b_pw1, axis=-1)
    y = lax.conv_general_dilated(y, w_dw[:, None, :], window_strides=(1,),
                                 padding=[(CONV_WIDTH - 1, 0)],
                                 dimension_numbers=('NWC', 'WIO', 'NWC'),
                                 feature_group_count=D) + b_dw
    y = jax.nn.silu(layer_norm(y, ln_g, ln_b))
    return y @ w_pw2 + b_pw2

def first_inputs(seed: int = 0) -> dict:
    key = jax.random.key(seed)
    ks = iter(jax.random.split(key, 40))
    D = D_MODEL

    def nrm(shape, scale):
        return jax.random.normal(next(ks), shape, jnp.float32) * scale

    def gain(shape):
        return 1.0 + nrm(shape, 0.05)

    return {
        "x": nrm((BATCH, SEQ, D), 1.0),
        "c": nrm((BATCH, D), 1.0),
        "norm_mix": gain((DEPTH, D)),
        "norm_mlp": gain((DEPTH, D)),
        "w_ada": nrm((DEPTH, D, 6 * D), 0.5 * D ** -0.5),
        "b_ada": nrm((DEPTH, 6 * D), 0.02),
        "w_mlp_in": nrm((DEPTH, D, D_FF), D ** -0.5),
        "w_mlp_out": nrm((DEPTH, D_FF, D), D_FF ** -0.5),
        "fox_w_in": nrm((N_A, D, 3 * D + N_HEADS), D ** -0.5),
        "fox_b_f": jax.random.uniform(next(ks), (N_A, N_HEADS), jnp.float32, 1.0, 6.0),
        "fox_q_norm": gain((N_A, HEAD_DIM)),
        "fox_k_norm": gain((N_A, HEAD_DIM)),
        "fox_w_out": nrm((N_A, D, D), D ** -0.5),
        "sg_w_in": nrm((N_B, D, 2 * SG_WIDTH), D ** -0.5),
        "sg_ln_g": gain((N_B, SG_WIDTH)),
        "sg_ln_b": nrm((N_B, SG_WIDTH), 0.02),
        "sg_w_s": nrm((N_B, SG_GROUPS, SG_CHUNK, SG_CHUNK), 0.5 * SG_CHUNK ** -0.5),
        "sg_b_s": 1.0 + nrm((N_B, SG_GROUPS, SG_CHUNK), 0.02),
        "sg_w_out": nrm((N_B, SG_WIDTH, D), SG_WIDTH ** -0.5),
        "cv_w_pw1": nrm((N_C, D, 2 * D), D ** -0.5),
        "cv_b_pw1": nrm((N_C, 2 * D), 0.02),
        "cv_w_dw": nrm((N_C, CONV_WIDTH, D), CONV_WIDTH ** -0.5),
        "cv_b_dw": nrm((N_C, D), 0.02),
        "cv_ln_g": gain((N_C, D)),
        "cv_ln_b": nrm((N_C, D), 0.02),
        "cv_w_pw2": nrm((N_C, D, D), D ** -0.5),
        "cv_b_pw2": nrm((N_C, D), 0.02),
    }

def first_block(x, c, norm_mix, norm_mlp, w_ada, b_ada, w_mlp_in, w_mlp_out,
              fox_w_in, fox_b_f, fox_q_norm, fox_k_norm, fox_w_out,
              sg_w_in, sg_ln_g, sg_ln_b, sg_w_s, sg_b_s, sg_w_out,
              cv_w_pw1, cv_b_pw1, cv_w_dw, cv_b_dw, cv_ln_g, cv_ln_b, cv_w_pw2, cv_b_pw2):
    c_act = jax.nn.silu(c)
    for i in range(DEPTH):
        kind = i % N_MIXERS
        j = i // N_MIXERS
        mod = c_act @ w_ada[i] + b_ada[i]
        sh_m, sc_m, g_m, sh_f, sc_f, g_f = [m[:, None, :] for m in jnp.split(mod, 6, axis=-1)]
        h = rms_norm(x, norm_mix[i]) * (1 + sc_m) + sh_m
        if kind == 0:
            y = fox_mixer(h, fox_w_in[j], fox_b_f[j], fox_q_norm[j], fox_k_norm[j], fox_w_out[j])
        elif kind == 1:
            y = gmlp_mixer(h, sg_w_in[j], sg_ln_g[j], sg_ln_b[j], sg_w_s[j], sg_b_s[j], sg_w_out[j])
        else:
            y = conv_mixer(h, cv_w_pw1[j], cv_b_pw1[j], cv_w_dw[j], cv_b_dw[j],
                           cv_ln_g[j], cv_ln_b[j], cv_w_pw2[j], cv_b_pw2[j])
        x = x + g_m * y
        h = rms_norm(x, norm_mlp[i]) * (1 + sc_f) + sh_f
        x = x + g_f * (jnp.square(jax.nn.relu(h @ w_mlp_in[i])) @ w_mlp_out[i])
    return x


D_MIX = D_MODEL
D_POOL = D_MIX // 4
POOL_WINDOWS = (2, 4, 8, 16)
N_POOL_GROUPS = len(POOL_WINDOWS)
POOL_GROUP = D_POOL // N_POOL_GROUPS
D_RWKV = D_MIX - D_POOL
HEAD_SIZE = 64
N_RWKV_HEADS = D_RWKV // HEAD_SIZE
D_DECAY_LORA = 64
D_AAA_LORA = 64
D_GATE_LORA = 128
D_RWKV_IN = 3 * D_RWKV + D_DECAY_LORA + D_AAA_LORA + D_GATE_LORA
D_IN = D_POOL + D_RWKV_IN

N_GROUPS = 4
EXPERTS_PER_GROUP = 8
N_EXPERTS = N_GROUPS * EXPERTS_PER_GROUP
TOP_K = 2
D_EXPERT = D_MODEL // 4
ROW_BLOCK = 128

LN_EPS = 1e-5
LNX_EPS = 64e-5
DEEPNORM_ALPHA = (2.0 * DEPTH) ** 0.25
DEEPNORM_BETA = (8.0 * DEPTH) ** -0.25


def layer_norm_2(x, g, b):
    xf = x.astype(jnp.float32)
    mu = jnp.mean(xf, axis=-1, keepdims=True)
    var = jnp.mean(jnp.square(xf - mu), axis=-1, keepdims=True)
    return ((xf - mu) * lax.rsqrt(var + LN_EPS) * g.astype(jnp.float32) + b.astype(jnp.float32)).astype(x.dtype)

def multiscale_pool(p, pool_w, pool_scale):
    b, s, _ = p.shape
    pf = p.astype(jnp.float32)
    csum = jnp.cumsum(pf, axis=1)
    count = jnp.arange(1, s + 1, dtype=jnp.float32)[None, :, None]
    outs = []
    for gi, win in enumerate(POOL_WINDOWS):
        c = csum[..., gi * POOL_GROUP:(gi + 1) * POOL_GROUP]
        c_lag = jnp.pad(c, ((0, 0), (win, 0), (0, 0)))[:, :s]
        mean = (c - c_lag) / jnp.minimum(count, float(win))
        outs.append(mean - pf[..., gi * POOL_GROUP:(gi + 1) * POOL_GROUP])
    diff = jnp.stack(outs, axis=2)
    mixed = jnp.einsum('bsgc,gcd->bsgd', diff, pool_w.astype(jnp.float32)).reshape(b, s, D_POOL)
    return (mixed * pool_scale.astype(jnp.float32)).astype(p.dtype)

def rwkv7_step(state, inp):
    r, decay, k, v, kk, a = inp
    sa = jnp.einsum('bhij,bhj->bhi', state, -kk)
    state = (state * decay[:, :, None, :]
             + sa[..., None] * (kk * a)[:, :, None, :]
             + v[..., None] * k[:, :, None, :])
    out = jnp.einsum('bhij,bhj->bhi', state, r)
    return state, out

def rwkv7_mix(z, mu_shift, w0, w_up, a0, a_up, g_up, k_k, k_a, r_k, lnx_g, lnx_b):
    b, s, _ = z.shape
    f32 = jnp.float32
    zf = z.astype(f32)
    prev = jnp.pad(zf, ((0, 0), (1, 0), (0, 0)))[:, :s]
    zm = zf + (prev - zf) * mu_shift.astype(f32)
    o = 0
    r = zm[..., o:o + D_RWKV]; o += D_RWKV
    k = zm[..., o:o + D_RWKV]; o += D_RWKV
    v = zm[..., o:o + D_RWKV]; o += D_RWKV
    wd = zm[..., o:o + D_DECAY_LORA]; o += D_DECAY_LORA
    ad = zm[..., o:o + D_AAA_LORA]; o += D_AAA_LORA
    gd = zm[..., o:o + D_GATE_LORA]
    w_log = -jax.nn.softplus(-(w0.astype(f32) + jnp.tanh(wd) @ w_up.astype(f32))) - 0.5
    decay = jnp.exp(-jnp.exp(w_log))
    a = jax.nn.sigmoid(a0.astype(f32) + ad @ a_up.astype(f32))
    g = jax.nn.sigmoid(gd) @ g_up.astype(f32)
    kk = k * k_k.astype(f32)
    k = k * (1.0 + (a - 1.0) * k_a.astype(f32))
    hs = lambda t: t.reshape(b, s, N_RWKV_HEADS, HEAD_SIZE)
    r, k, v, kk, a, decay = hs(r), hs(k), hs(v), hs(kk), hs(a), hs(decay)
    kk = kk / jnp.maximum(jnp.sqrt(jnp.sum(kk * kk, axis=-1, keepdims=True)), 1e-12)
    tmaj = lambda t: jnp.moveaxis(t, 1, 0)
    state0 = jnp.zeros((b, N_RWKV_HEADS, HEAD_SIZE, HEAD_SIZE), f32)
    _, y = lax.scan(rwkv7_step, state0, (tmaj(r), tmaj(decay), tmaj(k), tmaj(v), tmaj(kk), tmaj(a)))
    y = jnp.moveaxis(y, 0, 1)
    mu = jnp.mean(y, axis=-1, keepdims=True)
    var = jnp.mean(jnp.square(y - mu), axis=-1, keepdims=True)
    y = ((y - mu) * lax.rsqrt(var + LNX_EPS)).reshape(b, s, D_RWKV) * lnx_g.astype(f32) + lnx_b.astype(f32)
    bonus = jnp.sum(r * k * r_k.astype(f32), axis=-1, keepdims=True) * v
    y = (y + bonus.reshape(b, s, D_RWKV)) * g
    return y.astype(z.dtype)

def hierarchical_moe(h, router_group, router_group_b, router_expert, router_expert_b,
                     exp_gate, exp_up, exp_down):
    n, d = h.shape
    hf = h.astype(jnp.float32)
    g_prob = jax.nn.softmax(hf @ router_group.astype(jnp.float32) + router_group_b.astype(jnp.float32), axis=-1)
    g_top_p, g_idx = lax.top_k(g_prob, 1)
    e_logits = (hf @ router_expert.astype(jnp.float32) + router_expert_b.astype(jnp.float32)
                ).reshape(n, N_GROUPS, EXPERTS_PER_GROUP)
    e_sel = jnp.take_along_axis(e_logits, g_idx[:, :, None], axis=1)[:, 0]
    e_top_logit, e_idx = lax.top_k(e_sel, TOP_K)
    weights = g_top_p * jax.nn.softmax(e_top_logit, axis=-1)
    expert_id = g_idx * EXPERTS_PER_GROUP + e_idx

    m = n * TOP_K
    flat_e = expert_id.reshape(m).astype(jnp.int32)
    flat_tok = jnp.repeat(jnp.arange(n, dtype=jnp.int32), TOP_K)
    flat_w = weights.reshape(m)
    order = jnp.argsort(flat_e)
    e_sorted, tok_sorted, w_sorted = flat_e[order], flat_tok[order], flat_w[order]
    counts = jnp.bincount(flat_e, length=N_EXPERTS)
    padded = (counts + ROW_BLOCK - 1) // ROW_BLOCK * ROW_BLOCK
    start = jnp.cumsum(counts) - counts
    pend = jnp.cumsum(padded)
    pstart = pend - padded
    dest = pstart[e_sorted] + (jnp.arange(m, dtype=jnp.int32) - start[e_sorted])
    m_pad = (m + ROW_BLOCK - 1) // ROW_BLOCK * ROW_BLOCK + N_EXPERTS * ROW_BLOCK
    n_blocks = m_pad // ROW_BLOCK
    row_tok = jnp.zeros((m_pad,), jnp.int32).at[dest].set(tok_sorted)
    row_w = jnp.zeros((m_pad,), h.dtype).at[dest].set(w_sorted.astype(h.dtype))
    block_start = jnp.arange(n_blocks, dtype=jnp.int32) * ROW_BLOCK
    block_expert = jnp.minimum(jnp.searchsorted(pend, block_start, side='right'), N_EXPERTS - 1)

    def expert_block(args):
        tok, wgt, e = args
        xb = h[tok]
        hid = jax.nn.silu(xb @ exp_gate[e]) * (xb @ exp_up[e])
        return (hid @ exp_down[e]) * wgt[:, None]

    ys = lax.map(expert_block, (row_tok.reshape(n_blocks, ROW_BLOCK),
                                row_w.reshape(n_blocks, ROW_BLOCK), block_expert))
    return jnp.zeros((n, d), h.dtype).at[row_tok].add(ys.reshape(m_pad, d))

def hybrid_layer(x, w_in, pool_w, pool_scale, mu_shift, w0, w_up, a0, a_up, g_up, k_k, k_a, r_k,
                 lnx_g, lnx_b, w_out, ln1_g, ln1_b, router_group, router_group_b, router_expert,
                 router_expert_b, exp_gate, exp_up, exp_down, ln2_g, ln2_b):
    b, s, d = x.shape
    proj = x @ w_in
    pool_out = multiscale_pool(proj[..., :D_POOL], pool_w, pool_scale)
    rwkv_out = rwkv7_mix(proj[..., D_POOL:], mu_shift, w0, w_up, a0, a_up, g_up,
                         k_k, k_a, r_k, lnx_g, lnx_b)
    mixed = jnp.concatenate([pool_out, rwkv_out], axis=-1) @ w_out
    h = layer_norm_2(DEEPNORM_ALPHA * x + mixed, ln1_g, ln1_b)
    ffn = hierarchical_moe(h.reshape(b * s, d), router_group, router_group_b, router_expert,
                           router_expert_b, exp_gate, exp_up, exp_down).reshape(b, s, d)
    return layer_norm_2(DEEPNORM_ALPHA * h + ffn, ln2_g, ln2_b)

def second_inputs(seed: int = 0) -> dict:
    key = jax.random.key(seed)
    ks = jax.random.split(key, 28)
    nrm = lambda k, shape, scale: jax.random.normal(k, shape, jnp.float32) * scale
    L = DEPTH
    return {
        "x": nrm(ks[0], (BATCH, SEQ, D_MODEL), 1.0),
        "w_in": nrm(ks[1], (L, D_MODEL, D_IN), D_MODEL ** -0.5),
        "pool_w": nrm(ks[2], (L, N_POOL_GROUPS, POOL_GROUP, POOL_GROUP), POOL_GROUP ** -0.5),
        "pool_scale": 1.0 + nrm(ks[3], (L, D_POOL), 0.1),
        "mu_shift": jax.random.uniform(ks[4], (L, D_RWKV_IN), jnp.float32),
        "w0": jnp.linspace(-6.0, -1.0, D_RWKV, dtype=jnp.float32)[None, :] + nrm(ks[5], (L, D_RWKV), 0.1),
        "w_up": nrm(ks[6], (L, D_DECAY_LORA, D_RWKV), 0.1),
        "a0": nrm(ks[7], (L, D_RWKV), 0.1),
        "a_up": nrm(ks[8], (L, D_AAA_LORA, D_RWKV), 0.1),
        "g_up": nrm(ks[9], (L, D_GATE_LORA, D_RWKV), D_GATE_LORA ** -0.5),
        "k_k": 0.85 + nrm(ks[10], (L, D_RWKV), 0.05),
        "k_a": 1.0 + nrm(ks[11], (L, D_RWKV), 0.05),
        "r_k": nrm(ks[12], (L, N_RWKV_HEADS, HEAD_SIZE), 0.1),
        "lnx_g": 1.0 + nrm(ks[13], (L, D_RWKV), 0.1),
        "lnx_b": nrm(ks[14], (L, D_RWKV), 0.01),
        "w_out": nrm(ks[15], (L, D_MIX, D_MODEL), D_MIX ** -0.5 * DEEPNORM_BETA),
        "ln1_g": 1.0 + nrm(ks[16], (L, D_MODEL), 0.05),
        "ln1_b": nrm(ks[17], (L, D_MODEL), 0.01),
        "router_group": nrm(ks[18], (L, D_MODEL, N_GROUPS), D_MODEL ** -0.5),
        "router_group_b": nrm(ks[19], (L, N_GROUPS), 0.01),
        "router_expert": nrm(ks[20], (L, D_MODEL, N_EXPERTS), D_MODEL ** -0.5),
        "router_expert_b": nrm(ks[21], (L, N_EXPERTS), 0.01),
        "exp_gate": nrm(ks[22], (L, N_EXPERTS, D_MODEL, D_EXPERT), D_MODEL ** -0.5),
        "exp_up": nrm(ks[23], (L, N_EXPERTS, D_MODEL, D_EXPERT), D_MODEL ** -0.5),
        "exp_down": nrm(ks[24], (L, N_EXPERTS, D_EXPERT, D_MODEL), D_EXPERT ** -0.5 * DEEPNORM_BETA),
        "ln2_g": 1.0 + nrm(ks[25], (L, D_MODEL), 0.05),
        "ln2_b": nrm(ks[26], (L, D_MODEL), 0.01),
    }

def second_block(x, w_in, pool_w, pool_scale, mu_shift, w0, w_up, a0, a_up, g_up, k_k, k_a, r_k,
              lnx_g, lnx_b, w_out, ln1_g, ln1_b, router_group, router_group_b, router_expert,
              router_expert_b, exp_gate, exp_up, exp_down, ln2_g, ln2_b):
    for l in range(DEPTH):
        x = hybrid_layer(x, w_in[l], pool_w[l], pool_scale[l], mu_shift[l], w0[l], w_up[l], a0[l],
                         a_up[l], g_up[l], k_k[l], k_a[l], r_k[l], lnx_g[l], lnx_b[l], w_out[l],
                         ln1_g[l], ln1_b[l], router_group[l], router_group_b[l], router_expert[l],
                         router_expert_b[l], exp_gate[l], exp_up[l], exp_down[l], ln2_g[l], ln2_b[l])
    return x


def setup_inputs(seed=0):
    out = dict(first_inputs(seed))
    for name, value in second_inputs(seed + 1).items():
        if name != "x":
            out[name + "_2"] = value
    return out


def reference(
    x, c, norm_mix, norm_mlp, w_ada, b_ada, w_mlp_in, w_mlp_out, fox_w_in, fox_b_f, fox_q_norm,
    fox_k_norm, fox_w_out, sg_w_in, sg_ln_g, sg_ln_b, sg_w_s, sg_b_s, sg_w_out, cv_w_pw1,
    cv_b_pw1, cv_w_dw, cv_b_dw, cv_ln_g, cv_ln_b, cv_w_pw2, cv_b_pw2, w_in_2, pool_w_2,
    pool_scale_2, mu_shift_2, w0_2, w_up_2, a0_2, a_up_2, g_up_2, k_k_2, k_a_2, r_k_2, lnx_g_2,
    lnx_b_2, w_out_2, ln1_g_2, ln1_b_2, router_group_2, router_group_b_2, router_expert_2,
    router_expert_b_2, exp_gate_2, exp_up_2, exp_down_2, ln2_g_2, ln2_b_2,
):
    x = first_block(
        x, c, norm_mix, norm_mlp, w_ada, b_ada, w_mlp_in, w_mlp_out, fox_w_in, fox_b_f,
        fox_q_norm, fox_k_norm, fox_w_out, sg_w_in, sg_ln_g, sg_ln_b, sg_w_s, sg_b_s, sg_w_out,
        cv_w_pw1, cv_b_pw1, cv_w_dw, cv_b_dw, cv_ln_g, cv_ln_b, cv_w_pw2, cv_b_pw2,
    )
    return second_block(
        x, w_in_2, pool_w_2, pool_scale_2, mu_shift_2, w0_2, w_up_2, a0_2, a_up_2, g_up_2,
        k_k_2, k_a_2, r_k_2, lnx_g_2, lnx_b_2, w_out_2, ln1_g_2, ln1_b_2, router_group_2,
        router_group_b_2, router_expert_2, router_expert_b_2, exp_gate_2, exp_up_2, exp_down_2,
        ln2_g_2, ln2_b_2,
    )


_drawn_inputs = setup_inputs


def setup_inputs(seed=0):
    import zlib

    import numpy as np

    out = dict(_drawn_inputs(seed))
    spreads = {}
    factors = {'norm_mix': 4.219,
     'fox_q_norm': 5.695,
     'fox_k_norm': 6.257,
     'a0_2': 4.622,
     'k_k_2': 23.644,
     'k_a_2': 3.193,
     'lnx_b_2': 28.92,
     'ln1_b_2': 3.768,
     'router_group_b_2': 4.998,
     'router_expert_b_2': 7.635,
     'ln2_b_2': 5.52,
     'w_up_2': 4.148,
     'lnx_g_2': 3.401}
    for name, (base, spread) in spreads.items():
        noise = np.random.default_rng([zlib.crc32(name.encode()), seed]).standard_normal(out[name].shape)
        drawn = base * np.exp(spread * noise) if base else spread * noise
        out[name] = __import__('jax').numpy.asarray(drawn.astype(out[name].dtype))
    for name, factor in factors.items():
        out[name] = (out[name] * factor).astype(out[name].dtype)
    return out
```

```python
from contextlib import ExitStack

import concourse.bass as bass
from concourse import mybir

F32 = mybir.dt.float32
BF16 = mybir.dt.bfloat16
I32 = mybir.dt.int32
U32 = mybir.dt.uint32
ALU = mybir.AluOpType
ACT = mybir.ActivationFunctionType
AX = mybir.AxisListType

P = 128
S = 1024
D = 1024
TT = S // P
KT = D // P
NB = 512
HEADS = 16
HD = D // HEADS
QKV = 3 * D
QN = 384
D_FF = 4 * D
FT = D_FF // P
EPS = 1e-6


class Scope:

    def __init__(self, nc, tag):
        self.nc, self.tag, self.stack = nc, tag, ExitStack()

    def __enter__(self):
        self.stack.__enter__()
        return self

    def __exit__(self, *a):
        return self.stack.__exit__(*a)

    def sb(self, name, shape, dt=F32):
        return self.stack.enter_context(self.nc.sbuf_tensor(f"{self.tag}_{name}", shape, dt))

    def ps(self, name, shape, dt=F32):
        return self.stack.enter_context(self.nc.psum_tensor(f"{self.tag}_{name}", shape, dt))

    def sem(self, name):
        handle = self.stack.enter_context(self.nc.semaphore(f"{self.tag}_{name}"))
        USED.append(handle)
        return handle


USED = []


def clear_semaphores(nc):
    numbers = sorted({handle.num for handle in USED})
    USED.clear()
    with nc.Block() as block:
        @block.gpsimd
        def _(pool):
            at = 0
            while at < len(numbers):
                end = at
                while end + 1 < len(numbers) and numbers[end + 1] == numbers[end] + 1:
                    end += 1
                pool.sem_clear(range(numbers[at], numbers[end] + 1))
                at = end + 1


def constants(nc, scope):
    ident = scope.sb("ident", [P, P])
    ones = scope.sb("ones", [P, P])
    cumul = scope.sb("cumul", [P, P])
    ident16 = scope.sb("ident16", [P, P], BF16)
    future16 = scope.sb("future16", [P, P], BF16)
    with Scope(nc, "cst") as c, nc.Block() as block:
        cleared = c.sem("cleared")
        built = c.sem("built")

        @block.gpsimd
        def _(pool):
            nc.gpsimd.memset(ident[:], 0.0).then_inc(cleared, 1)
            nc.gpsimd.memset(ones[:], 1.0).then_inc(cleared, 1)
            nc.gpsimd.memset(cumul[:], 1.0).then_inc(cleared, 1)
            nc.gpsimd.memset(ident16[:], 0.0).then_inc(cleared, 1)
            nc.gpsimd.memset(future16[:], 0.0).then_inc(cleared, 1)
            pool.wait_ge(cleared, 5)
            for m in (ident, ident16):
                nc.gpsimd.affine_select(out=m[:], in_=m[:], compare_op=ALU.not_equal, fill=1.0, base=0,
                                        pattern=[[-1, P]], channel_multiplier=1).then_inc(built, 1)
            nc.gpsimd.affine_select(out=cumul[:], in_=cumul[:], compare_op=ALU.is_ge, fill=0.0, base=0,
                                    pattern=[[1, P]], channel_multiplier=-1).then_inc(built, 1)
            nc.gpsimd.affine_select(out=future16[:], in_=future16[:], compare_op=ALU.is_ge, fill=-1e30, base=0,
                                    pattern=[[-1, P]], channel_multiplier=1).then_inc(built, 1)
            pool.wait_ge(built, 4)
    return ident, ones, cumul, ident16, future16


def stage_modulation(nc, x, cols1, w_ada, b_ada, xres, modc, gates, ones):
    CB, CN1, CN2 = KT, KT + 6 * KT, 2 * KT + 6 * KT
    with Scope(nc, "mod") as s:
        cols = s.sb("cols", [P, 9 * KT])
        silu = s.sb("silu", [P, 3, KT])
        wa = s.sb("wa", [P, 2, 6 * D])
        acc = s.sb("acc", [P, 6 * D])
        brow = s.sb("brow", [P, 2, D])
        mod = s.sb("mod", [P, 6 * KT])
        pmod = s.ps("pmod", [P, 6 * KT])
        pgate = s.ps("pgate", [P, 4, NB])
        cols_in, x_in, brow_in = s.sem("cols_in"), s.sem("x_in"), s.sem("brow_in")
        w_in = [s.sem("w_in0"), s.sem("w_in1")]
        w_used, silu_st, acc_done = s.sem("w_used"), s.sem("silu_st"), s.sem("acc_done")
        silu_exp, mm_mod, mm_gate, mod_done = s.sem("silu_exp"), s.sem("mm_mod"), s.sem("mm_gate"), s.sem("mod_done")
        finished = s.sem("finished")
        with nc.Block() as block:
            @block.sync
            def _(sp):
                sp.dma_start(cols[:], cols1).then_inc(cols_in, 16)
                for k in range(KT):
                    if k >= 2:
                        sp.wait_ge(w_used, k - 1)
                    sp.dma_start(wa[:, k % 2, :], w_ada[k * P:(k + 1) * P, :]).then_inc(w_in[k % 2], 16)

            @block.scalar
            def _(act):
                act.dma_start(xres[:], x.rearrange("(t p) d -> p t d", p=P)).then_inc(x_in, 16)
                for g, off in enumerate((2 * D, 5 * D)):
                    act.dma_start(brow[:, g, :], b_ada[off:off + D].partition_broadcast(P)).then_inc(brow_in, 16)
                act.wait_ge(cols_in, 16)
                nc.scalar.activation(silu[:, 0, :], cols[:, 0:KT], ACT.Exp, scale=-1.0).then_inc(silu_exp, 1)
                act.wait_ge(x_in, 16)

            @block.vector
            def _(dve):
                dve.wait_ge(silu_exp, 1)
                nc.vector.tensor_scalar_add(silu[:, 1, :], silu[:, 0, :], 1.0).then_inc(silu_st, 1)
                dve.wait_ge(silu_st, 1)
                nc.vector.reciprocal(silu[:, 2, :], silu[:, 1, :]).then_inc(silu_st, 1)
                dve.wait_ge(silu_st, 2)
                nc.vector.tensor_tensor(silu[:, 0, :], silu[:, 2, :], cols[:, 0:KT], ALU.mult).then_inc(silu_st, 1)
                dve.wait_ge(silu_st, 3)
                for k in range(KT):
                    dve.wait_ge(w_in[k % 2], 16 * (k // 2 + 1))
                    if k == 0:
                        nc.vector.tensor_scalar(acc[:], wa[:, 0, :], silu[:, 0, 0:1], None,
                                                ALU.mult).then_inc(w_used, 1)
                    else:
                        dve.wait_ge(w_used, k)
                        nc.vector.scalar_tensor_tensor(out=acc[:], in0=wa[:, k % 2, :], scalar=silu[:, 0, k:k + 1],
                                                       in1=acc[:], op0=ALU.mult, op1=ALU.add).then_inc(w_used, 1)
                dve.wait_ge(mm_mod, 1)
                nc.vector.tensor_tensor(mod[:], pmod[:], cols[:, CB:CB + 6 * KT], ALU.add).then_inc(mod_done, 1)
                dve.wait_ge(mod_done, 1)
                for n, (norm, shift, scale) in enumerate(((CN1, 0, KT), (CN2, 3 * KT, 4 * KT))):
                    nc.vector.scalar_tensor_tensor(out=modc[:, n, 0, :], in0=mod[:, scale:scale + KT], scalar=1.0,
                                                   in1=cols[:, norm:norm + KT], op0=ALU.add,
                                                   op1=ALU.mult).then_inc(finished, 1)
                    nc.vector.tensor_copy(modc[:, n, 1, :], mod[:, shift:shift + KT]).then_inc(finished, 1)
                dve.wait_ge(mm_gate, 1)
                dve.wait_ge(brow_in, 32)
                for g in range(2):
                    nc.vector.tensor_tensor(gates[:, g, :], pgate[:, 2 * g:2 * g + 2, :].rearrange("p a b -> p (a b)"),
                                            brow[:, g, :], ALU.add).then_inc(finished, 1)
                dve.wait_ge(finished, 6)

            @block.tensor
            def _(pe):
                pe.wait_ge(w_used, KT)
                for m in range(6 * KT):
                    last = nc.tensor.matmul(pmod[:, m:m + 1], lhsT=acc[:, m * P:(m + 1) * P], rhs=ones[:, 0:1],
                                            start=True, stop=True)
                last.then_inc(mm_mod, 1)
                for g, off in enumerate((2 * D, 5 * D)):
                    for h in range(2):
                        last = nc.tensor.matmul(pgate[:, 2 * g + h, :], lhsT=ones[:],
                                                rhs=acc[:, off + h * NB:off + (h + 1) * NB], start=True, stop=True)
                last.then_inc(mm_gate, 1)


def stage_norm(nc, tag, xres, hT, modc, ident):
    with Scope(nc, tag) as s:
        xn = s.sb("xn", [P, TT, D])
        ss = s.sb("ss", [P, TT])
        st = s.sb("st", [P, 3, TT])
        pt = s.ps("pt", [P, 4, NB])
        sq_done, var_ok, root, rstd_ok = s.sem("sq_done"), s.sem("var_ok"), s.sem("root"), s.sem("rstd_ok")
        xn_done, turned, taken_a, taken_v = s.sem("xn_done"), s.sem("turned"), s.sem("taken_a"), s.sem("taken_v")
        with nc.Block() as block:
            @block.scalar
            def _(act):
                for t in range(TT):
                    nc.scalar.activation(xn[:, t, :], xres[:, t, :], ACT.Square,
                                         accum_out=ss[:, t:t + 1]).then_inc(sq_done, 1)
                act.wait_ge(var_ok, 1)
                nc.scalar.activation(st[:, 1, :], st[:, 0, :], ACT.Sqrt).then_inc(root, 1)
                for r in range(1, 2 * KT, 2):
                    act.wait_ge(turned, r + 1)
                    c, half = r // 2, r % 2
                    nc.scalar.activation(hT[:, c, half * NB:(half + 1) * NB], pt[:, r % 4, :], ACT.Identity,
                                         scale=modc[:, 0, c:c + 1], bias=modc[:, 1, c:c + 1]).then_inc(taken_a, 1)
                act.wait_ge(taken_a, KT)

            @block.vector
            def _(dve):
                dve.wait_ge(sq_done, TT)
                nc.vector.tensor_scalar(st[:, 0, :], ss[:], 1.0 / D, EPS, ALU.mult, ALU.add).then_inc(var_ok, 1)
                dve.wait_ge(root, 1)
                nc.vector.reciprocal(st[:, 2, :], st[:, 1, :]).then_inc(rstd_ok, 1)
                dve.wait_ge(rstd_ok, 1)
                for t in range(TT):
                    nc.vector.tensor_scalar(xn[:, t, :], xres[:, t, :], st[:, 2, t:t + 1], None,
                                            ALU.mult).then_inc(xn_done, 1)
                for r in range(0, 2 * KT, 2):
                    dve.wait_ge(turned, r + 1)
                    c = r // 2
                    nc.vector.tensor_scalar(hT[:, c, 0:NB], pt[:, r % 4, :], modc[:, 0, c:c + 1],
                                            modc[:, 1, c:c + 1], ALU.mult, ALU.add).then_inc(taken_v, 1)
                dve.wait_ge(taken_v, KT)

            @block.tensor
            def _(pe):
                for r in range(2 * KT):
                    c, half = r // 2, r % 2
                    if r < 2:
                        pe.wait_ge(xn_done, 4 * (r + 1))
                    if r >= 4:
                        pe.wait_ge(taken_a if r % 2 else taken_v, r // 2 - 1)
                    for j in range(4):
                        last = nc.tensor.transpose(pt[:, r % 4, j * P:(j + 1) * P],
                                                   xn[:, 4 * half + j, c * P:(c + 1) * P], ident[:])
                    last.then_inc(turned, 1)


def stage_qkv(nc, hT, w_qkv, w_f, bf_row, qkv, ss, neg_f, cumul, ones):
    CH = QKV // QN
    HPC = QN // HD
    with Scope(nc, "qkv") as s:
        wq = s.sb("wq", [P, 2, KT, QN])
        wf = s.sb("wf", [P, KT, HEADS])
        fb = s.sb("fb", [P, HEADS])
        lf = s.sb("lf", [P, 4, TT, HEADS])
        sq = s.sb("sq", [P, 2, QN])
        pq = s.ps("pq", [P, 4, NB])
        pf = s.ps("pf", [P, TT, HEADS])
        pc = s.ps("pc", [P, TT, HEADS])
        w_in = [s.sem("w_in0"), s.sem("w_in1")]
        wf_in, mm, copied, squared, summed = s.sem("wf_in"), s.sem("mm"), s.sem("copied"), s.sem("squared"), s.sem("summed")
        mm_f, f_st, f_act, f_lin, mm_c, ends = s.sem("mm_f"), s.sem("f_st"), s.sem("f_act"), s.sem("f_lin"), s.sem("mm_c"), s.sem("ends")
        with nc.Block() as block:
            @block.sync
            def _(sp):
                sp.dma_start(wf[:], w_f).then_inc(wf_in, 16)
                sp.dma_start(fb[:], bf_row.partition_broadcast(P)).then_inc(wf_in, 16)
                for n in range(2):
                    sp.dma_start(wq[:, n, :, :], w_qkv[n]).then_inc(w_in[n], 16)
                with sp.Fori(1, CH // 2) as i:
                    for n in range(2):
                        sp.wait_ge(mm, (2 * i + n - 1) * TT)
                        sp.dma_start(wq[:, n, :, :], w_qkv[2 * i + n]).then_inc(w_in[n], 16)

            @block.tensor
            def _(pe):
                pe.wait_ge(wf_in, 32)
                for t in range(TT):
                    for k in range(KT):
                        last = nc.tensor.matmul(pf[:, t, :], lhsT=hT[:, k, t * P:(t + 1) * P], rhs=wf[:, k, :],
                                                start=(k == 0), stop=(k == KT - 1))
                last.then_inc(mm_f, 1)
                with pe.Fori(0, CH // 2) as i:
                    for n in range(2):
                        pe.wait_ge(w_in[n], 16 * i + 16)
                        for t in range(TT):
                            b = t % 4
                            pe.wait_ge(copied, (2 * i + n) * TT + t + 1)
                            for k in range(KT):
                                last = nc.tensor.matmul(pq[:, b, 0:QN], lhsT=hT[:, k, t * P:(t + 1) * P],
                                                        rhs=wq[:, n, k, :], start=(k == 0), stop=(k == KT - 1))
                            last.then_inc(mm, 1)
                pe.wait_ge(f_st, 1)
                for t in range(TT):
                    for j in range(t + 1):
                        last = nc.tensor.matmul(pc[:, t, :], lhsT=(cumul if j == t else ones)[:], rhs=lf[:, 3, j, :],
                                                start=(j == 0), stop=(j == t))
                last.then_inc(mm_c, 1)

            @block.scalar
            def _(act):
                act.wait_ge(f_lin, 3)
                nc.scalar.activation(lf[:, 2, :, :], lf[:, 1, :, :], ACT.Exp).then_inc(f_act, 1)
                act.wait_ge(f_act, 1)
                nc.scalar.activation(lf[:, 1, :, :], lf[:, 2, :, :], ACT.Ln, bias=1.0).then_inc(f_act, 1)
                with act.Fori(0, CH // 2) as i:
                    for n in range(2):
                        for t in range(TT):
                            m = (2 * i + n) * TT + t
                            act.wait_ge(copied, m + 5)
                            act.wait_ge(summed, m + 1)
                            nc.scalar.activation(sq[:, t % 2, :], qkv[:, t, bass.ds((2 * i + n) * QN, QN)],
                                                 ACT.Square).then_inc(squared, 1)

            @block.vector
            def _(dve):
                dve.sem_inc(copied, 4)
                dve.sem_inc(summed, 2)
                dve.wait_ge(mm_f, 1)
                nc.vector.tensor_tensor(lf[:, 0, :, :], pf[:], fb[:].unsqueeze(1).to_broadcast([P, TT, HEADS]),
                                        ALU.add).then_inc(f_lin, 1)
                dve.wait_ge(f_lin, 1)
                nc.vector.tensor_scalar(lf[:, 2, :, :], lf[:, 0, :, :], -1.0, None, ALU.mult).then_inc(f_lin, 1)
                dve.wait_ge(f_lin, 2)
                nc.vector.tensor_tensor(lf[:, 1, :, :], lf[:, 0, :, :], lf[:, 2, :, :], ALU.min).then_inc(f_lin, 1)
                dve.wait_ge(f_act, 2)
                nc.vector.scalar_tensor_tensor(out=lf[:, 3, :, :], in0=lf[:, 0, :, :], scalar=0.0,
                                               in1=lf[:, 1, :, :], op0=ALU.min, op1=ALU.subtract).then_inc(f_st, 1)
                with dve.Fori(0, CH // 2) as i:
                    for n in range(2):
                        for t in range(TT):
                            m = (2 * i + n) * TT + t
                            dve.wait_ge(mm, m + 1)
                            nc.vector.tensor_copy(qkv[:, t, bass.ds((2 * i + n) * QN, QN)],
                                                  pq[:, t % 4, 0:QN]).then_inc(copied, 1)
                            dve.wait_ge(squared, m + 1)
                            nc.vector.tensor_reduce(ss[:, t, bass.ds((2 * i + n) * HPC, HPC)],
                                                    sq[:, t % 2, :].rearrange("p (h d) -> p h d", d=HD),
                                                    AX.X, ALU.add).then_inc(summed, 1)
                dve.wait_ge(copied, CH * TT + 4)
                dve.wait_ge(summed, CH * TT + 2)
                dve.wait_ge(mm_c, 1)
                nc.vector.tensor_scalar(neg_f[:], pc[:], -1.0, None, ALU.mult).then_inc(ends, 1)
                dve.wait_ge(ends, 1)


def stage_attention(nc, qkv, ss, neg_f, qk_gain, o_all, ident, ident16, future16):
    HA = HD + 1
    with Scope(nc, "att") as s:
        norm = s.sb("norm", [P, 3, TT, 2 * HEADS])
        qk = s.sb("qk", [P, 2, TT, HA])
        qkT = s.sb("qkT", [HA, 2, S])
        gain = s.sb("gain", [HA, 2])
        gq = s.sb("gq", [HA, 3])
        prob = s.sb("prob", [P, 2, S])
        pT = s.sb("pT", [P, 4, NB])
        nmax = s.sb("nmax", [P, 2, TT])
        rsum = s.sb("rsum", [P, 2, TT])
        rinv = s.sb("rinv", [P, TT])
        logit = s.ps("logit", [P, 4, NB])
        turn = s.ps("turn", [P, 2, NB])
        po = s.ps("po", [P, TT * HD])
        gain_in, prep, root, set_up = s.sem("gain_in"), s.sem("prep"), s.sem("root"), s.sem("set_up")
        staged, turned, left, scored = s.sem("staged"), s.sem("turned"), s.sem("left"), s.sem("scored")
        qk_left, maxed, exped, ov, o_left, inv = s.sem("qk_left"), s.sem("maxed"), s.sem("exped"), s.sem("ov"), s.sem("o_left"), s.sem("inv")
        ROUNDS = 4 + sum((i + 4) // 4 for i in range(TT))

        def first_round(i):
            return 4 + sum((j + 4) // 4 for j in range(i))

        with nc.Block() as block:
            @block.sync
            def _(sp):
                sp.dma_start(gq[0:HD, 0:2], qk_gain).then_inc(gain_in, 16)

            @block.vector
            def _(dve):
                nc.vector.memset(gq[:, 2:3], HD ** -0.5).then_inc(prep, 1)
                nc.vector.memset(gain[:], 1.0).then_inc(prep, 1)
                nc.vector.tensor_scalar(norm[:, 0, :, :], ss[:, :, 0:2 * HEADS], 1.0 / HD, EPS, ALU.mult,
                                        ALU.add).then_inc(prep, 1)
                dve.wait_ge(gain_in, 16)
                dve.wait_ge(prep, 3)
                nc.vector.scalar_tensor_tensor(out=gain[0:HD, 0:1], in0=gq[0:HD, 0:1], scalar=gq[0:HD, 1:2],
                                               in1=gq[0:HD, 2:3], op0=ALU.mult, op1=ALU.mult).then_inc(set_up, 1)
                dve.wait_ge(root, 1)
                nc.vector.reciprocal(norm[:, 2, :, :], norm[:, 1, :, :]).then_inc(set_up, 1)
                dve.sem_inc(o_left, 1)
                dve.sem_inc(left, 2)
                with dve.Fori(0, HEADS) as h:
                    for r in range(2):
                        dve.wait_ge(turned, h * ROUNDS + r + 2)
                        nc.vector.tensor_copy(qkT[:, 0, r * NB:(r + 1) * NB], turn[0:HA, r % 2, :]).then_inc(left, 1)
                    for r in range(2, 4):
                        dve.wait_ge(turned, h * ROUNDS + r + 2)
                        nc.vector.tensor_scalar(qkT[:, 1, (r - 2) * NB:(r - 1) * NB], turn[0:HA, r % 2, :],
                                                gain[:, 0:1], None, ALU.mult).then_inc(left, 1)

                    def row_max(i):
                        dve.wait_ge(scored, h * TT + i + 1)
                        nc.vector.tensor_reduce(nmax[:, h % 2, i:i + 1],
                                                logit[:, 2 * (i % 2):2 * (i % 2) + 2, :].rearrange("p a b -> p (a b)")[:, 0:(i + 1) * P],
                                                AX.X, ALU.max, negate=True).then_inc(maxed, 1)

                    row_max(0)
                    for i in range(TT):
                        if i + 1 < TT:
                            row_max(i + 1)
                        for r in range((i + 4) // 4):
                            n = first_round(i) + r
                            w = min(4, i + 1 - 4 * r) * P
                            dve.wait_ge(turned, h * ROUNDS + n + 2)
                            nc.vector.tensor_copy(pT[:, n % 4, 0:w], turn[:, n % 2, 0:w]).then_inc(left, 1)
                    dve.wait_ge(exped, (h + 1) * TT + 1)
                    nc.vector.reciprocal(rinv[:], rsum[:, h % 2, :]).then_inc(inv, 1)
                    dve.wait_ge(inv, h + 1)
                    dve.wait_ge(ov, (h + 1) * TT)
                    nc.vector.tensor_tensor(o_all[:, :, bass.ds(h * HD, HD)], po[:].rearrange("p (t d) -> p t d", d=HD),
                                            rinv[:].unsqueeze(2).to_broadcast([P, TT, HD]), ALU.mult).then_inc(o_left, 1)
                dve.wait_ge(o_left, HEADS + 1)

            @block.scalar
            def _(act):
                act.sem_inc(exped, 1)
                act.wait_ge(prep, 3)
                nc.scalar.activation(norm[:, 1, :, :], norm[:, 0, :, :], ACT.Sqrt).then_inc(root, 1)
                with act.Fori(0, HEADS) as h:
                    for i in range(TT):
                        act.wait_ge(maxed, h * TT + i + 1)
                        n = first_round(i - 2) + (i + 2) // 4 if i >= 2 else 0
                        act.wait_ge(turned, h * ROUNDS + n + 1)
                        nc.scalar.activation(prob[:, i % 2, 0:(i + 1) * P],
                                             logit[:, 2 * (i % 2):2 * (i % 2) + 2, :].rearrange("p a b -> p (a b)")[:, 0:(i + 1) * P],
                                             ACT.Exp, bias=nmax[:, h % 2, i:i + 1],
                                             accum_out=rsum[:, h % 2, i:i + 1]).then_inc(exped, 1)

            @block.gpsimd
            def _(pool):
                nc.gpsimd.memset(qk[:], 1.0).then_inc(staged, 1)
                pool.wait_ge(staged, 1)
                pool.wait_ge(set_up, 2)
                pool.sem_inc(qk_left, 1)
                with pool.Fori(0, HEADS) as h:
                    pool.wait_ge(turned, h * ROUNDS + 1)
                    for w in range(2):
                        nc.gpsimd.tensor_tensor(qk[:, w, :, 0:HD], qkv[:, :, bass.ds(w * D + h * HD, HD)],
                                                norm[:, 2, :, bass.ds(w * HEADS + h, 1)].to_broadcast([P, TT, HD]),
                                                ALU.mult).then_inc(staged, 1)
                    nc.gpsimd.tensor_copy(qk[:, 1, :, HD:HA], neg_f[:, :, bass.ds(h, 1)]).then_inc(staged, 1)

            @block.tensor
            def _(pe):
                pe.sem_inc(turned, 1)
                with pe.Fori(0, HEADS) as h:
                    pe.wait_ge(staged, 3 * h + 4)
                    for r in range(4):
                        pe.wait_ge(left, h * ROUNDS + r + 1)
                        for j in range(4):
                            last = nc.tensor.transpose(turn[0:HA, r % 2, j * P:(j + 1) * P],
                                                       qk[:, r // 2, (r % 2) * 4 + j, :], ident[:])
                        last.then_inc(turned, 1)

                    def scores(i):
                        if i == 0:
                            pe.wait_ge(left, h * ROUNDS + 6)
                        if i < 2:
                            pe.wait_ge(exped, h * TT + 1)
                        else:
                            pe.wait_ge(exped, h * TT + i)
                        b = 2 * (i % 2)
                        for c in range((i + 4) // 4):
                            w = min(NB, (i + 1) * P - c * NB)
                            mine = c == i // 4
                            last = nc.tensor.matmul(logit[:, b + c, 0:w], lhsT=qkT[:, 0, i * P:(i + 1) * P],
                                                    rhs=qkT[:, 1, c * NB:c * NB + w], start=True, stop=not mine)
                        at = (i % 4) * P
                        last = nc.tensor.matmul(logit[:, b + i // 4, at:at + P], lhsT=ident16[:], rhs=future16[:],
                                                start=False, stop=True)
                        last.then_inc(scored, 1)

                    scores(0)
                    for i in range(TT):
                        if i + 1 < TT:
                            scores(i + 1)
                        pe.wait_ge(exped, h * TT + i + 2)
                        for r in range((i + 4) // 4):
                            n = first_round(i) + r
                            pe.wait_ge(left, h * ROUNDS + n + 1)
                            for j in range(4 * r, min(4 * r + 4, i + 1)):
                                last = nc.tensor.transpose(turn[:, n % 2, (j % 4) * P:(j % 4 + 1) * P],
                                                           prob[:, i % 2, j * P:(j + 1) * P], ident[:])
                            last.then_inc(turned, 1)
                        if i == 0:
                            pe.wait_ge(o_left, h + 1)
                        for j in range(i + 1):
                            n = first_round(i) + j // 4
                            if j % 4 == 0:
                                pe.wait_ge(left, h * ROUNDS + n + 3)
                            last = nc.tensor.matmul(po[:, i * HD:(i + 1) * HD], lhsT=pT[:, n % 4, (j % 4) * P:(j % 4 + 1) * P],
                                                    rhs=qkv[:, j, bass.ds(2 * D + h * HD, HD)],
                                                    start=(j == 0), stop=(j == i))
                        last.then_inc(ov, 1)


def stage_out(nc, tag, src, w, xres, gate, ident, room):
    with Scope(nc, tag) as s:
        sT = room[:, 0:KT * S].rearrange("p (k t) -> p k t", k=KT)
        ws = room[:, KT * S:2 * KT * S].rearrange("p (n k c) -> p n k c", n=2, k=KT)
        tmp = s.sb("tmp", [P, 2, NB])
        pt = s.ps("pt", [P, 4, NB])
        py = s.ps("py", [P, 4, NB])
        w_in = [s.sem("w_in0"), s.sem("w_in1")]
        turned, taken, mm, gated, added = s.sem("turned"), s.sem("taken"), s.sem("mm"), s.sem("gated"), s.sem("added")
        with nc.Block() as block:
            @block.sync
            def _(sp):
                for n in range(2):
                    sp.dma_start(ws[:, n, :, :], w[n]).then_inc(w_in[n], 16)

            @block.scalar
            def _(act):
                for r in range(2 * KT):
                    act.wait_ge(turned, r + 1)
                    nc.scalar.copy(sT[:, r // 2, (r % 2) * NB:(r % 2 + 1) * NB], pt[:, r % 4, :]).then_inc(taken, 1)

            @block.tensor
            def _(pe):
                for r in range(2 * KT):
                    if r >= 4:
                        pe.wait_ge(taken, r - 3)
                    for j in range(4):
                        last = nc.tensor.transpose(pt[:, r % 4, j * P:(j + 1) * P],
                                                   src[:, 4 * (r % 2) + j, (r // 2) * P:(r // 2 + 1) * P], ident[:])
                    last.then_inc(turned, 1)
                pe.wait_ge(taken, 2 * KT)
                for n in range(2):
                    pe.wait_ge(w_in[n], 16)
                    for t in range(TT):
                        m = n * TT + t
                        if m >= 4:
                            pe.wait_ge(gated, m - 3)
                        for k in range(KT):
                            last = nc.tensor.matmul(py[:, m % 4, :], lhsT=sT[:, k, t * P:(t + 1) * P],
                                                    rhs=ws[:, n, k, :], start=(k == 0), stop=(k == KT - 1))
                        last.then_inc(mm, 1)

            @block.vector
            def _(dve):
                for n in range(2):
                    for t in range(TT):
                        m = n * TT + t
                        dve.wait_ge(mm, m + 1)
                        if m >= 2:
                            dve.wait_ge(added, m - 1)
                        cs = slice(n * NB, (n + 1) * NB)
                        nc.vector.tensor_tensor(tmp[:, m % 2, :], py[:, m % 4, :], gate[:, cs], ALU.mult).then_inc(gated, 1)
                        dve.wait_ge(gated, m + 1)
                        nc.vector.tensor_tensor(xres[:, t, cs], xres[:, t, cs], tmp[:, m % 2, :], ALU.add).then_inc(added, 1)
                dve.wait_ge(added, 2 * TT)


def stage_mlp(nc, hT, w1, w2, xres, gate, ident):
    with Scope(nc, "mlp") as s:
        hid = s.sb("hid", [P, FT, NB])
        w1s = s.sb("w1s", [P, 4, KT, P])
        w2s = s.sb("w2s", [P, 4, D])
        rel = s.sb("rel", [P, 2, NB])
        yT = s.sb("yT", [P, KT, NB])
        tmp = s.sb("tmp", [P, 2, NB])
        ps = s.ps("ps", [P, 8, NB])
        w1_in = [s.sem(f"w1_in{n}") for n in range(4)]
        w2_in = [s.sem(f"w2_in{n}") for n in range(4)]
        up, down, relu, squared, y_left = s.sem("up"), s.sem("down"), s.sem("relu"), s.sem("squared"), s.sem("y_left")
        turned, gated, added = s.sem("turned"), s.sem("gated"), s.sem("added")
        with nc.Block() as block:
            @block.sync
            def _(sp):
                sp.sem_inc(up, 4)
                sp.sem_inc(down, 4)
                for half in range(2):
                    with sp.Fori(0, FT // 4) as g:
                        for n in range(4):
                            sp.wait_ge(up, half * FT + 4 * g + n + 1)
                            sp.dma_start(w1s[:, n, :, :], w1[4 * g + n]).then_inc(w1_in[n], 16)
                    with sp.Fori(0, FT // 4) as g:
                        for n in range(4):
                            sp.wait_ge(down, half * FT + 4 * g + n + 1)
                            sp.dma_start(w2s[:, n, :], w2[4 * g + n]).then_inc(w2_in[n], 16)

            @block.tensor
            def _(pe):
                for half in range(2):
                    if half:
                        pe.wait_ge(gated, 8)
                    with pe.Fori(0, FT // 4) as g:
                        for n in range(4):
                            m = half * FT + 4 * g + n
                            pe.wait_ge(w1_in[n], 16 * (half * (FT // 4) + g + 1))
                            pe.wait_ge(relu, m + 1)
                            for k in range(KT):
                                last = nc.tensor.matmul(ps[:, n, :], lhsT=w1s[:, n, k, :],
                                                        rhs=hT[:, k, half * NB:(half + 1) * NB],
                                                        start=(k == 0), stop=(k == KT - 1))
                            last.then_inc(up, 1)
                    pe.wait_ge(relu, (half + 1) * FT + 4)

                    def down_group(g, first, end):
                        for n in range(4):
                            pe.wait_ge(squared, half * FT + 4 * g + n + 3)
                            pe.wait_ge(w2_in[n], 16 * (half * (FT // 4) + g + 1))
                            for c in range(KT):
                                last = nc.tensor.matmul(ps[:, c, :], lhsT=w2s[:, n, c * P:(c + 1) * P],
                                                        rhs=hid[:, 4 * g + n, :], start=first and n == 0,
                                                        stop=end and n == 3)
                            last.then_inc(down, 1)

                    down_group(0, True, False)
                    with pe.Fori(1, FT // 4 - 1) as g:
                        down_group(g, False, False)
                    down_group(FT // 4 - 1, False, True)
                    pe.wait_ge(y_left, 8 * (half + 1))
                    for r in range(8):
                        t, c0 = r // 2, 4 * (r % 2)
                        for j in range(4):
                            last = nc.tensor.transpose(ps[:, r, j * P:(j + 1) * P], yT[:, c0 + j, t * P:(t + 1) * P],
                                                       ident[:])
                        last.then_inc(turned, 1)

            @block.scalar
            def _(act):
                act.sem_inc(relu, 4)
                for half in range(2):
                    with act.Fori(0, FT // 4) as g:
                        for n in range(4):
                            m = half * FT + 4 * g + n
                            act.wait_ge(up, m + 5)
                            act.wait_ge(squared, m + 1)
                            nc.scalar.activation(rel[:, n % 2, :], ps[:, n, :], ACT.Relu).then_inc(relu, 1)
                    act.wait_ge(down, (half + 1) * FT + 4)
                    if half:
                        act.wait_ge(turned, 8)
                    for c in range(KT):
                        nc.scalar.copy(yT[:, c, :], ps[:, c, :]).then_inc(y_left, 1)

            @block.vector
            def _(dve):
                dve.sem_inc(squared, 2)
                for half in range(2):
                    if half:
                        dve.wait_ge(down, FT + 4)
                    with dve.Fori(0, FT // 4) as g:
                        for n in range(4):
                            m = half * FT + 4 * g + n
                            dve.wait_ge(relu, m + 5)
                            nc.vector.tensor_tensor(hid[:, bass.ds(4 * g + n, 1), :], rel[:, n % 2:n % 2 + 1, :],
                                                    rel[:, n % 2:n % 2 + 1, :], ALU.mult).then_inc(squared, 1)
                    for r in range(8):
                        m = half * 8 + r
                        t, cs = half * 4 + r // 2, slice((r % 2) * NB, (r % 2 + 1) * NB)
                        dve.wait_ge(turned, m + 1)
                        if m >= 2:
                            dve.wait_ge(added, m - 1)
                        nc.vector.tensor_tensor(tmp[:, m % 2, :], ps[:, r, :], gate[:, cs], ALU.mult).then_inc(gated, 1)
                        dve.wait_ge(gated, m + 1)
                        nc.vector.tensor_tensor(xres[:, t, cs], xres[:, t, cs], tmp[:, m % 2, :],
                                                ALU.add).then_inc(added, 1)
                dve.wait_ge(added, 16)


PAIRS = 6
HS = 64
NPAR = 10
MU_R, MU_K, MU_V, W0, A0, K_K, K_A, R_K, LNX_G, LNX_B = range(NPAR)
WIN = 128
WPAIRS = S // WIN // 2
LEVELS = 7
LN_EPS = 1e-5
LNX_EPS = 64e-5
ALPHA = 2.0 ** 0.25
DECAY = -0.6065306597126334


class Steps:

    def __init__(self, sem, names):
        self.sem, self.names = sem, names.split()

    def at(self, i, name):
        return i * len(self.names) + self.names.index(name) + 1


def stage_turn(nc, tag, src, dst, ident):
    with Scope(nc, tag) as s:
        pt = s.ps("pt", [P, 8, NB])
        turned, taken = s.sem("turned"), s.sem("taken")
        with nc.Block() as block:
            @block.tensor
            def _(pe):
                for r in range(2 * KT):
                    if r >= 8:
                        pe.wait_ge(taken, r - 7)
                    for j in range(4):
                        last = nc.tensor.transpose(pt[:, r % 8, j * P:(j + 1) * P],
                                                   src[:, 4 * (r % 2) + j, (r // 2) * P:(r // 2 + 1) * P], ident[:])
                    last.then_inc(turned, 1)

            @block.vector
            def _(dve):
                for r in range(2 * KT):
                    dve.wait_ge(turned, r + 1)
                    nc.vector.tensor_copy(dst[:, r // 2, (r % 2) * NB:(r % 2 + 1) * NB],
                                          pt[:, r % 8, :]).then_inc(taken, 1)
                dve.wait_ge(taken, 2 * KT)


def stage_pool(nc, xT, w_head, head_cols, pool_w, inv_count, mixT, lora_in):
    PAD = 16
    with Scope(nc, "pool") as s:
        ws = s.sb("ws", [P, 4, KT, P])
        hc = s.sb("hc", [P, 6])
        pw = s.sb("pw", [P, 2, P])
        ic = s.sb("ic", [P, 2, PAD])
        z = s.sb("z", [P, 4, PAD + S])
        acc = s.sb("acc", [P, 2, PAD + S])
        dif = s.sb("dif", [P, 2, S])
        ps = s.ps("ps", [P, 8, NB])
        w_in, c_in, mm, copied, cleared = s.sem("w_in"), s.sem("c_in"), s.sem("mm"), s.sem("copied"), s.sem("cleared")
        v, mapped, ends = s.sem("vector_step"), s.sem("mapped"), s.sem("ends")
        with nc.Block() as block:
            @block.sync
            def _(sp):
                sp.dma_start(ws[:], w_head).then_inc(w_in, 16)
                sp.dma_start(hc[:], head_cols).then_inc(c_in, 16)
                sp.dma_start(pw[:], pool_w).then_inc(c_in, 16)
                sp.dma_start(ic[:], inv_count).then_inc(c_in, 16)

            @block.tensor
            def _(pe):
                pe.wait_ge(w_in, 16)
                for n in range(4):
                    for half in range(2):
                        for k in range(KT):
                            last = nc.tensor.matmul(ps[:, 2 * n + half, :], lhsT=ws[:, n, k, :],
                                                    rhs=xT[:, k, half * NB:(half + 1) * NB],
                                                    start=(k == 0), stop=(k == KT - 1))
                    last.then_inc(mm, 1)
                pe.wait_ge(copied, 4)
                pe.wait_ge(c_in, 48)
                for n in range(2):
                    pe.wait_ge(mapped, n + 1)
                    for half in range(2):
                        last = nc.tensor.matmul(ps[:, 2 * n + half, :], lhsT=pw[:, n, :],
                                                rhs=dif[:, n, half * NB:(half + 1) * NB], start=True, stop=True)
                    last.then_inc(mm, 1)

            @block.scalar
            def _(act):
                for n in range(4):
                    act.wait_ge(mm, n + 1)
                    nc.scalar.copy(z[:, n, PAD:], ps[:, 2 * n:2 * n + 2, :].rearrange("p a b -> p (a b)")).then_inc(copied, 1)
                act.wait_ge(v, 4)
                nc.scalar.activation(lora_in[0:HS, 0, :], lora_in[0:HS, 0, :], ACT.Tanh).then_inc(ends, 1)
                nc.scalar.activation(lora_in[:, 1, :], lora_in[:, 1, :], ACT.Sigmoid).then_inc(ends, 1)
                act.wait_ge(ends, 2)

            @block.vector
            def _(dve):
                step = [0]

                def done(ins):
                    step[0] += 1
                    ins.then_inc(v, 1)
                    dve.wait_ge(v, step[0])

                nc.vector.memset(z[:, :, 0:PAD], 0.0).then_inc(cleared, 1)
                nc.vector.memset(acc[:, :, 0:PAD], 0.0).then_inc(cleared, 1)
                dve.wait_ge(cleared, 2)
                dve.wait_ge(c_in, 48)
                dve.wait_ge(copied, 4)
                for n in range(2):
                    cur = z[:, 2 + n, PAD:]
                    done(nc.vector.tensor_tensor(dif[:, 0, :], z[:, 2 + n, PAD - 1:PAD - 1 + S], cur, ALU.subtract))
                    done(nc.vector.scalar_tensor_tensor(out=lora_in[:, n, :], in0=dif[:, 0, :], scalar=hc[:, n:n + 1],
                                                        in1=cur, op0=ALU.mult, op1=ALU.add))
                for n in range(2):
                    src, dst, lag = z[:, n, :], acc[:, 0, :], 1
                    for level in range(1 + 2 * n):
                        done(nc.vector.tensor_tensor(dst[:, PAD:], src[:, PAD:], src[:, PAD - lag:PAD - lag + S], ALU.add))
                        src, dst, lag = dst, acc[:, (level + 1) % 2, :], 2 * lag
                    done(nc.vector.tensor_tensor(dst[HS:P, PAD:], src[HS:P, PAD:], src[HS:P, PAD - lag:PAD - lag + S], ALU.add))
                    done(nc.vector.tensor_copy(dst[0:HS, PAD:], src[0:HS, PAD:]))
                    done(nc.vector.tensor_tensor(src[:, PAD:2 * PAD], dst[:, PAD:2 * PAD], ic[:, n, :], ALU.mult))
                    done(nc.vector.tensor_tensor(dif[:, n, 0:PAD], src[:, PAD:2 * PAD], z[:, n, PAD:2 * PAD], ALU.subtract))
                    nc.vector.scalar_tensor_tensor(out=dif[:, n, PAD:], in0=dst[:, 2 * PAD:], scalar=hc[:, 4 + n:5 + n],
                                                   in1=z[:, n, 2 * PAD:], op0=ALU.mult, op1=ALU.subtract).then_inc(mapped, 1)
                    dve.wait_ge(mapped, n + 1)
                for n in range(2):
                    dve.wait_ge(mm, 5 + n)
                    done(nc.vector.tensor_scalar(mixT[:, n, :], ps[:, 2 * n:2 * n + 2, :].rearrange("p a b -> p (a b)"),
                                                 hc[:, 2 + n:3 + n], None, ALU.mult))


def stage_rwkv(nc, xT, w_rkv, lora_up, pair_cols, consts, scan_keep, lora_in, mixT, ident):
    with Scope(nc, "rwkv") as s:
        ws = s.sb("ws", [P, 3, KT, P])
        up = s.sb("up", [P, 2, P])
        par_all = s.sb("par_all", [P, PAIRS * NPAR])
        par = s.sb("par", [P, NPAR + 1])
        cst = s.sb("cst", [P, 4 + LEVELS + 2, P])
        causal = cst[:, 0:4, :].rearrange("p a b -> p (a b)")
        level = [cst[:, 4 + n, :] for n in range(LEVELS)]
        head_sum, head_mean = cst[:, 4 + LEVELS, :], cst[:, 5 + LEVELS, :]
        keep = s.sb("keep", [P, S])
        Z = s.sb("Z", [P, 3, S + 1])
        rkv = s.sb("rkv", [P, 3, S])
        R, K, V = rkv[:, 0, :], rkv[:, 1, :], rkv[:, 2, :]
        T0, LW, L, LM, SA, AG, BON, GG = (s.sb(n, [P, S]) for n in "T0 LW L LM SA AG BON GG".split())
        EP, EN, KK = Z[:, 0, 1:], Z[:, 1, 1:], Z[:, 2, 1:]
        EX = T0
        Y = LW
        fac = s.sb("fac", [P, 2, 8])
        AR = s.sb("AR", [P, 2, 2, WIN])
        KB = s.sb("KB", [P, 2, 2, WIN])
        VS = s.sb("VS", [P, 2, WIN])
        tm = s.sb("tm", [P, 2, 4, P])
        GM = s.sb("GM", [P, 4, 4, WIN])
        ML = s.sb("ML", [P, 3, 4, WIN])
        TI = s.sb("TI", [P, 4, WIN])
        TX = s.sb("TX", [P, 4, WIN])
        XS = s.sb("XS", [P, 4, WIN])
        AW = s.sb("AW", [P, 4, 2, HS])
        GH = s.sb("GH", [P, 4, 2, HS])
        QT = s.sb("QT", [P, 2, WIN])
        ZT = s.sb("ZT", [P, 2, HS])
        ST = s.sb("ST", [P, HS])
        SU = s.sb("SU", [P, HS])
        ps = s.ps("ps", [P, 8, NB])

        def wide(b):
            return ps[:, b:b + 2, :].rearrange("p a b -> p (a b)")

        w_in, up_in, c_in, cleared = s.sem("w_in"), s.sem("up_in"), s.sem("c_in"), s.sem("cleared")
        pe_p = Steps(s.sem("pe_pair"), "r k w v a g kk_sum bonus mean var")
        act_p = Steps(s.sem("act_pair"), "r k v w a g kk_sq root ep en ex fac y_sq y_root")
        dve_p = Steps(s.sem("dve_pair"), "par one_ka r_d r k_d k v_d v lw scan lm lref lx kk sq_max inv kkn ag k2 b rk rk2 bonus state "
                      "y_c y_eps y_inv y_n y_gb y_b y_out")
        pe_w = Steps(s.sem("pe_win"), "turn0 turn1 gram0 gram1 gram2 gram3 ak_v ti0 " +
                     " ".join(f"x{l} t{l}" for l in range(1, LEVELS)) + " gh q z e0 y0 e1 y1")
        act_w = Steps(s.sem("act_win"), "tm0 tm1 a_tm w_tm ti0 " + " ".join(f"x{l}" for l in range(1, LEVELS)) + " gh z y0 y1")
        dve_w = Steps(s.sem("dve_win"), "A R K B gm0 gm1 gm2 gm3 ab0 tx0 " +
                      " ".join(f"ti{l} tx{l}" for l in range(1, LEVELS - 1)) + f" tx{LEVELS - 1} q su0 st0 su1 st1")
        pool_w = Steps(s.sem("pool_win"), "VS " + " ".join(f"m{l}" for l in range(1, LEVELS)))

        def units():
            return [(2 * w + h, w, h) for w in range(2) for h in range(2)]

        with nc.Block() as block:
            @block.sync
            def _(sp):
                sp.dma_start(par_all[:], pair_cols).then_inc(c_in, 16)
                sp.dma_start(cst[:], consts).then_inc(c_in, 16)
                sp.dma_start(keep[:], scan_keep).then_inc(c_in, 16)
                sp.dma_start(up[:], lora_up[0]).then_inc(up_in, 16)
                sp.dma_start(ws[:], w_rkv[0]).then_inc(w_in, 16)
                with sp.Fori(1, PAIRS) as p:
                    sp.wait_ge(pe_p.sem, pe_p.at(p - 1, "g"))
                    sp.dma_start(up[:], lora_up[p]).then_inc(up_in, 16)
                    sp.dma_start(ws[:], w_rkv[p]).then_inc(w_in, 16)

            @block.tensor
            def _(pe):
                def project(n, bank):
                    for half in range(2):
                        for k in range(KT):
                            last = nc.tensor.matmul(ps[:, bank + half, :], lhsT=ws[:, n, k, :],
                                                    rhs=xT[:, k, half * NB:(half + 1) * NB],
                                                    start=(k == 0), stop=(k == KT - 1))
                    last.then_inc(pe_p.sem, 1)

                def wide_product(lhsT, rhs, bank):
                    for half in range(2):
                        last = nc.tensor.matmul(ps[:, bank + half, :], lhsT=lhsT, rhs=rhs[:, half * NB:(half + 1) * NB],
                                                start=True, stop=True)
                    last.then_inc(pe_p.sem, 1)

                pe.sem_inc(pe_w.sem, len(pe_w.names))
                pe.wait_ge(c_in, 48)
                with pe.Fori(0, PAIRS) as p:
                    pe.wait_ge(w_in, 16 * p + 16)
                    pe.wait_ge(up_in, 16 * p + 16)
                    pe.wait_ge(act_p.sem, act_p.at(p, "y_root"))
                    pe.wait_ge(dve_p.sem, dve_p.at(p, "y_out"))
                    project(0, 0)
                    project(1, 2)
                    wide_product(up[0:HS, 0, :], lora_in[0:HS, 0, :], 4)
                    pe.wait_ge(act_p.sem, act_p.at(p + 1, "r"))
                    project(2, 0)
                    pe.wait_ge(act_p.sem, act_p.at(p + 1, "k"))
                    wide_product(up[HS:P, 0, :], lora_in[HS:P, 0, :], 2)
                    wide_product(up[:, 1, :], lora_in[:, 1, :], 6)
                    pe.wait_ge(act_p.sem, act_p.at(p + 1, "kk_sq"))
                    wide_product(head_sum, L, 4)
                    pe.wait_ge(dve_p.sem, dve_p.at(p + 1, "rk2"))
                    wide_product(head_sum, AG, 0)
                    with pe.Fori(0, WPAIRS) as wp:
                        q = p * WPAIRS + wp
                        pe.wait_ge(dve_p.sem, dve_p.at(p + 1, "state"))
                        pe.wait_ge(dve_w.sem, dve_w.at(q, "B"))
                        pe.wait_ge(pool_w.sem, pool_w.at(q, "VS"))
                        for w in range(2):
                            for n, src in enumerate((AR[:, w, 0, :], KB[:, w, 1, :], KB[:, w, 0, :], VS[:, w, :])):
                                last = nc.tensor.transpose(ps[:, w, n * P:(n + 1) * P], src, ident[:])
                            last.then_inc(pe_w.sem, 1)
                        for u, w, h in units():
                            hp = slice(h * HS, (h + 1) * HS)
                            both = AR[hp, w, :, :].rearrange("p a b -> p (a b)")
                            nc.tensor.matmul(ps[:, 2 + u, 0:2 * WIN], lhsT=KB[hp, w, 1, :], rhs=both, start=True, stop=True)
                            nc.tensor.matmul(ps[:, 2 + u, 2 * WIN:4 * WIN], lhsT=KB[hp, w, 0, :], rhs=both,
                                             start=True, stop=True).then_inc(pe_w.sem, 1)
                        pe.wait_ge(act_w.sem, act_w.at(q, "a_tm"))
                        pe.wait_ge(dve_w.sem, dve_w.at(q, "gm3"))
                        for u, w, h in units():
                            last = nc.tensor.matmul(ps[:, 0, u * HS:(u + 1) * HS], lhsT=GM[:, u, 2, :],
                                                    rhs=tm[:, w, 3, h * HS:(h + 1) * HS], start=True, stop=True)
                        last.then_inc(pe_w.sem, 1)
                        pe.wait_ge(dve_w.sem, dve_w.at(q, "tx0"))
                        for u in range(4):
                            last = nc.tensor.transpose(ps[:, 1, u * P:(u + 1) * P], TX[:, u, :], ident[:])
                        last.then_inc(pe_w.sem, 1)
                        for l in range(1, LEVELS):
                            pe.wait_ge(pool_w.sem, pool_w.at(q, f"m{l}"))
                            if l == 1:
                                pe.wait_ge(act_w.sem, act_w.at(q, "ti0"))
                            else:
                                pe.wait_ge(dve_w.sem, dve_w.at(q, f"tx{l - 1}"))
                            for u in range(4):
                                last = nc.tensor.matmul(ps[:, 2, u * P:(u + 1) * P], lhsT=ML[:, l % 3, u, :], rhs=TI[:, u, :],
                                                        start=True, stop=True)
                            last.then_inc(pe_w.sem, 1)
                            pe.wait_ge(act_w.sem, act_w.at(q, f"x{l}"))
                            if l < LEVELS - 1:
                                for u in range(4):
                                    nc.tensor.matmul(ps[:, 3, u * P:(u + 1) * P], lhsT=TX[:, u, :], rhs=XS[:, u, :],
                                                     start=True, stop=True)
                            for u in range(4):
                                last = nc.tensor.matmul(ps[:, 4, u * P:(u + 1) * P], lhsT=XS[:, u, :], rhs=TX[:, u, :],
                                                        start=True, stop=True)
                            last.then_inc(pe_w.sem, 1)
                        pe.wait_ge(dve_w.sem, dve_w.at(q, f"tx{LEVELS - 1}"))
                        pe.wait_ge(act_w.sem, act_w.at(q, "w_tm"))
                        for u in range(4):
                            last = nc.tensor.matmul(ps[:, 5, u * P:(u + 1) * P], lhsT=TX[:, u, :],
                                                    rhs=AW[:, u, :, :].rearrange("p a b -> p (a b)"), start=True, stop=True)
                        last.then_inc(pe_w.sem, 1)
                        pe.wait_ge(act_w.sem, act_w.at(q, "gh"))
                        for u, w, h in units():
                            last = nc.tensor.matmul(ps[h * HS:(h + 1) * HS, 2, w * WIN:(w + 1) * WIN], lhsT=GH[:, u, 0, :],
                                                    rhs=GM[:, u, 1, :], start=True, stop=True)
                        last.then_inc(pe_w.sem, 1)
                        for u, w, h in units():
                            last = nc.tensor.matmul(ps[h * HS:(h + 1) * HS, 3, w * HS:(w + 1) * HS], lhsT=GH[:, u, 0, :],
                                                    rhs=tm[:, w, 1, h * HS:(h + 1) * HS], start=True, stop=True)
                        last.then_inc(pe_w.sem, 1)
                        pe.wait_ge(act_w.sem, act_w.at(q, "z"))
                        for w in range(2):
                            for h in range(2):
                                u, hp = 2 * w + h, slice(h * HS, (h + 1) * HS)
                                out = ps[hp, 6, 0:HS]
                                if w:
                                    pe.wait_ge(dve_w.sem, dve_w.at(q, "st0"))
                                nc.tensor.matmul(out, lhsT=tm[:, w, 1, hp], rhs=GH[:, u, 1, :], start=True, stop=False)
                                nc.tensor.matmul(out, lhsT=tm[:, w, 2, hp], rhs=tm[:, w, 3, hp], start=False, stop=False)
                                last = nc.tensor.matmul(out, lhsT=ZT[hp, w, :], rhs=ST[hp, :], start=False, stop=True)
                            last.then_inc(pe_w.sem, 1)
                            if w == 0:
                                pe.wait_ge(dve_w.sem, dve_w.at(q, "q"))
                            else:
                                pe.wait_ge(act_w.sem, act_w.at(q, "y0"))
                            for h in range(2):
                                u, hp = 2 * w + h, slice(h * HS, (h + 1) * HS)
                                out = ps[hp, 7, 0:WIN]
                                nc.tensor.matmul(out, lhsT=GH[:, u, 1, :], rhs=GM[:, u, 1, :], start=True, stop=False)
                                nc.tensor.matmul(out, lhsT=tm[:, w, 3, hp], rhs=GM[:, u, 3, :], start=False, stop=False)
                                last = nc.tensor.matmul(out, lhsT=ST[hp, :], rhs=QT[hp, w, :], start=False, stop=True)
                            last.then_inc(pe_w.sem, 1)
                    pe.wait_ge(act_w.sem, act_w.at(p * WPAIRS + WPAIRS - 1, "y1"))
                    pe.wait_ge(dve_w.sem, dve_w.at(p * WPAIRS + WPAIRS - 1, "st1"))
                    wide_product(head_mean, Y, 0)
                    pe.wait_ge(act_p.sem, act_p.at(p + 1, "y_sq"))
                    wide_product(head_mean, L, 2)

            @block.scalar
            def _(act):
                def step(*args, **kw):
                    nc.scalar.activation(*args, **kw).then_inc(act_p.sem, 1)

                act.sem_inc(act_p.sem, len(act_p.names))
                with act.Fori(0, PAIRS) as p:
                    for n, name in enumerate("rk"):
                        act.wait_ge(pe_p.sem, pe_p.at(p, name))
                        act.wait_ge(dve_p.sem, dve_p.at(p, "y_out"))
                        nc.scalar.copy(Z[:, n, 1:], wide(2 * n)).then_inc(act_p.sem, 1)
                    act.wait_ge(pe_p.sem, pe_p.at(p, "v"))
                    nc.scalar.copy(Z[:, 2, 1:], wide(0)).then_inc(act_p.sem, 1)
                    act.wait_ge(dve_p.sem, dve_p.at(p + 1, "par"))
                    step(LW[:], wide(4), ACT.Sigmoid, bias=par[:, W0:W0 + 1])
                    act.wait_ge(pe_p.sem, pe_p.at(p, "a"))
                    step(SA[:], wide(2), ACT.Sigmoid, bias=par[:, A0:A0 + 1])
                    act.wait_ge(pe_p.sem, pe_p.at(p, "g"))
                    nc.scalar.copy(GG[:], wide(6)).then_inc(act_p.sem, 1)
                    act.wait_ge(dve_p.sem, dve_p.at(p + 1, "kk"))
                    step(L[:], KK, ACT.Square)
                    act.wait_ge(dve_p.sem, dve_p.at(p + 1, "sq_max"))
                    step(L[:], L[:], ACT.Sqrt)
                    act.wait_ge(dve_p.sem, dve_p.at(p + 1, "v"))
                    step(EP, LM[:], ACT.Exp)
                    step(EN, LM[:], ACT.Exp, scale=-1.0)
                    step(EX[:], EX[:], ACT.Exp)
                    step(fac[:, 1, 0:7], fac[:, 0, 0:7], ACT.Exp)
                    with act.Fori(0, WPAIRS) as wp:
                        q = p * WPAIRS + wp
                        for w in range(2):
                            act.wait_ge(pe_w.sem, pe_w.at(q + 1, f"turn{w}"))
                            nc.scalar.copy(tm[:, w, :, :], ps[:, w, :].rearrange("p (a b) -> p a b", a=4)).then_inc(act_w.sem, 1)
                        act.wait_ge(act_w.sem, act_w.at(q, "tm1"))
                        nc.scalar.copy(AW[:, :, 0, :].rearrange("p (w h) d -> p w h d", w=2),
                                       tm[:, :, 0, :].rearrange("p w (h d) -> p w h d", h=2)).then_inc(act_w.sem, 1)
                        act.wait_ge(pe_w.sem, pe_w.at(q + 1, "ak_v"))
                        nc.scalar.copy(AW[:, :, 1, :], ps[:, 0, 0:4 * HS].rearrange("p (u d) -> p u d", u=4)).then_inc(act_w.sem, 1)
                        act.wait_ge(pe_w.sem, pe_w.at(q + 1, "ti0"))
                        nc.scalar.copy(TI[:].rearrange("p u t -> p (u t)"), ps[:, 1, :]).then_inc(act_w.sem, 1)
                        for l in range(1, LEVELS):
                            act.wait_ge(pe_w.sem, pe_w.at(q + 1, f"x{l}"))
                            nc.scalar.copy(XS[:].rearrange("p u t -> p (u t)"), ps[:, 2, :]).then_inc(act_w.sem, 1)
                        act.wait_ge(pe_w.sem, pe_w.at(q + 1, "gh"))
                        nc.scalar.copy(GH[:].rearrange("p u a d -> p (u a d)"), ps[:, 5, :]).then_inc(act_w.sem, 1)
                        act.wait_ge(pe_w.sem, pe_w.at(q + 1, "z"))
                        nc.scalar.copy(ZT[:].rearrange("p w d -> p (w d)"), ps[:, 3, 0:2 * HS]).then_inc(act_w.sem, 1)
                        for w in range(2):
                            act.wait_ge(pe_w.sem, pe_w.at(q + 1, f"y{w}"))
                            nc.scalar.copy(Y[:, bass.ds(wp * 2 * WIN + w * WIN, WIN)], ps[:, 7, 0:WIN]).then_inc(act_w.sem, 1)
                    act.wait_ge(dve_p.sem, dve_p.at(p + 1, "y_c"))
                    step(L[:], T0[:], ACT.Square)
                    act.wait_ge(dve_p.sem, dve_p.at(p + 1, "y_eps"))
                    step(L[:], L[:], ACT.Sqrt)

            @block.gpsimd
            def _(pool):
                pool.wait_ge(c_in, 48)
                with pool.Fori(0, PAIRS) as p:
                    with pool.Fori(0, WPAIRS) as wp:
                        q = p * WPAIRS + wp
                        pool.wait_ge(dve_w.sem, dve_w.at(q, "A"))
                        nc.gpsimd.tensor_copy(VS[:].rearrange("p w t -> p (w t)"),
                                              V[:, bass.ds(wp * 2 * WIN, 2 * WIN)]).then_inc(pool_w.sem, 1)
                        for l in range(1, LEVELS):
                            if l == 1:
                                pool.wait_ge(dve_w.sem, dve_w.at(q, "gm3"))
                            if l > 3:
                                pool.wait_ge(pe_w.sem, pe_w.at(q + 1, f"x{l - 3}"))
                            nc.gpsimd.tensor_tensor(ML[:, l % 3, :, :], GM[:, :, 0, :],
                                                    level[l].unsqueeze(1).to_broadcast([P, 4, WIN]),
                                                    ALU.mult).then_inc(pool_w.sem, 1)

            @block.vector
            def _(dve):
                sem_p, sem_w = dve_p.sem, dve_w.sem

                dve.sem_inc(sem_p, len(dve_p.names))
                nc.vector.memset(Z[:, :, 0:1], 0.0).then_inc(cleared, 1)
                nc.vector.memset(fac[:], 0.0).then_inc(cleared, 1)
                dve.wait_ge(cleared, 2)
                dve.wait_ge(c_in, 48)
                with dve.Fori(0, PAIRS) as p:
                    def at(name):
                        return dve_p.at(p + 1, name)

                    def step(need, ins_of):
                        dve.wait_ge(sem_p, at(need))
                        ins_of().then_inc(sem_p, 1)

                    tt, ts, stt = nc.vector.tensor_tensor, nc.vector.tensor_scalar, nc.vector.scalar_tensor_tensor

                    def col(n):
                        return par[:, n:n + 1]

                    dve.wait_ge(sem_p, dve_p.at(p, "y_out"))
                    nc.vector.tensor_copy(par[:, 0:NPAR], par_all[:, bass.ds(p * NPAR, NPAR)]).then_inc(sem_p, 1)
                    step("par", lambda: ts(par[:, NPAR:NPAR + 1], col(K_A), -1.0, 1.0, ALU.mult, ALU.add))
                    for n, name in enumerate("rkv"):
                        dve.wait_ge(act_p.sem, act_p.at(p + 1, name))
                        step(("one_ka", "r", "k")[n], lambda: tt(T0[:], Z[:, n, 0:S], Z[:, n, 1:], ALU.subtract))
                        step(name + "_d", lambda: stt(out=rkv[:, n, :], in0=T0[:], scalar=col(n), in1=Z[:, n, 1:],
                                                      op0=ALU.mult, op1=ALU.add))
                    dve.wait_ge(act_p.sem, act_p.at(p + 1, "w"))
                    step("v", lambda: ts(LW[:], LW[:], DECAY, None, ALU.mult))
                    step("lw", lambda: nc.vector.tensor_tensor_scan(L[:], keep[:], LW[:], 0.0, ALU.mult, ALU.add))
                    L3, LM3 = (a[:].rearrange("p (w t) -> p w t", t=WIN) for a in (L, LM))
                    step("scan", lambda: tt(LM3, L3, L3[:, :, HS - 1:HS].to_broadcast([P, 8, WIN]), ALU.subtract))
                    step("lm", lambda: tt(fac[:, 0, 0:7], LM3[:, 0:7, WIN - 1], L3[:, 1:8, HS - 1], ALU.add))
                    step("lref", lambda: tt(EX[:], LM[:], LW[:], ALU.subtract))
                    step("v", lambda: ts(KK, K, col(K_K), None, ALU.mult))
                    dve.wait_ge(pe_p.sem, pe_p.at(p, "kk_sum"))
                    step("kk", lambda: ts(L[:], wide(4), 1e-24, None, ALU.max))
                    dve.wait_ge(act_p.sem, act_p.at(p + 1, "root"))
                    step("sq_max", lambda: nc.vector.reciprocal(L[:], L[:]))
                    step("inv", lambda: tt(KK, KK, L[:], ALU.mult))
                    dve.wait_ge(act_p.sem, act_p.at(p + 1, "a"))
                    step("kk", lambda: ts(AG[:], SA[:], col(K_A), col(NPAR), ALU.mult, ALU.add))
                    step("ag", lambda: tt(K, K, AG[:], ALU.mult))
                    step("k2", lambda: tt(SA[:], SA[:], KK, ALU.mult))
                    step("k2", lambda: tt(AG[:], R, K, ALU.mult))
                    step("rk", lambda: ts(AG[:], AG[:], col(R_K), None, ALU.mult))
                    dve.wait_ge(pe_p.sem, pe_p.at(p, "bonus"))
                    step("rk2", lambda: tt(BON[:], wide(0), V, ALU.mult))
                    step("bonus", lambda: nc.vector.memset(ST[:], 0.0))
                    with dve.Fori(0, WPAIRS) as wp:
                        q = p * WPAIRS + wp
                        dve.wait_ge(act_p.sem, act_p.at(p + 1, "fac"))
                        dve.wait_ge(sem_p, at("state"))

                        def wstep(need, ins_of):
                            if need:
                                dve.wait_ge(sem_w, dve_w.at(q, need))
                            ins_of().then_inc(sem_w, 1)

                        def win(a):
                            return a[:, bass.ds(wp * 2 * WIN, 2 * WIN)].rearrange("p (w t) -> p w t", w=2)

                        dve.wait_ge(pe_w.sem, pe_w.at(q, "y1"))
                        wstep(None, lambda: stt(out=AR[:, :, 0, :], in0=win(KK), scalar=-1.0, in1=win(EX), op0=ALU.mult,
                                                op1=ALU.mult))
                        wstep(None, lambda: tt(AR[:, :, 1, :], win(R), win(EP), ALU.mult))
                        wstep(None, lambda: tt(KB[:, :, 0, :], win(K), win(EN), ALU.mult))
                        wstep(None, lambda: tt(KB[:, :, 1, :], win(SA), win(EN), ALU.mult))
                        for u in range(4):
                            dve.wait_ge(pe_w.sem, pe_w.at(q + 1, f"gram{u}"))
                            wstep(None, lambda: tt(GM[:, u, :, :].rearrange("p a b -> p (a b)"), ps[:, 2 + u, :], causal,
                                                   ALU.mult))
                        wstep("gm3", lambda: tt(TX[:], GM[:, :, 0, :], level[0].unsqueeze(1).to_broadcast([P, 4, WIN]),
                                                ALU.mult))
                        wstep("ab0", lambda: tt(TX[:], TX[:], ident[:].unsqueeze(1).to_broadcast([P, 4, WIN]), ALU.add))
                        for l in range(1, LEVELS):
                            dve.wait_ge(pe_w.sem, pe_w.at(q + 1, f"t{l}"))
                            if l < LEVELS - 1:
                                wstep(None, lambda: tt(TI[:], ps[:, 3, :].rearrange("p (u t) -> p u t", u=4), TI[:], ALU.add))
                            wstep(f"tx{l - 1}", lambda: tt(TX[:], ps[:, 4, :].rearrange("p (u t) -> p u t", u=4), TX[:], ALU.add))
                        dve.wait_ge(pe_w.sem, pe_w.at(q + 1, "q"))
                        wstep(None, lambda: tt(QT[:], ps[:, 2, 0:2 * WIN].rearrange("p (w t) -> p w t", w=2), AR[:, :, 1, :],
                                               ALU.add))
                        for w in range(2):
                            dve.wait_ge(pe_w.sem, pe_w.at(q + 1, f"e{w}"))
                            wstep(None if w == 0 else "st0", lambda: tt(SU[:], ps[:, 6, 0:HS], ST[:], ALU.add))
                            dve.wait_ge(pe_w.sem, pe_w.at(q + 1, f"y{w}"))
                            at_w = wp * 2 + w
                            wstep(f"su{w}", lambda: ts(ST[:], SU[:], fac[:, 1, bass.ds(at_w, 1)], None, ALU.mult))
                    dve.wait_ge(pe_p.sem, pe_p.at(p, "mean"))
                    step("state", lambda: tt(T0[:], Y[:], wide(0), ALU.subtract))
                    dve.wait_ge(pe_p.sem, pe_p.at(p, "var"))
                    step("y_c", lambda: ts(L[:], wide(2), LNX_EPS, None, ALU.add))
                    dve.wait_ge(act_p.sem, act_p.at(p + 1, "y_root"))
                    step("y_eps", lambda: nc.vector.reciprocal(L[:], L[:]))
                    step("y_inv", lambda: tt(T0[:], T0[:], L[:], ALU.mult))
                    step("y_n", lambda: ts(T0[:], T0[:], col(LNX_G), col(LNX_B), ALU.mult, ALU.add))
                    step("y_gb", lambda: tt(T0[:], T0[:], BON[:], ALU.add))
                    step("y_b", lambda: tt(mixT[:, bass.ds(2 + p, 1), :].rearrange("p a t -> p (a t)"), T0[:], GG[:], ALU.mult))
                dve.wait_ge(sem_p, dve_p.at(PAIRS, "y_out"))


def layer_norm_steps(nc, dve, src, stats, mv, g_row, b_row, n, done, root_ready, rooted):
    for c in range(2):
        done(nc.vector.bn_stats(stats[:, c, :], src[:, c * NB:(c + 1) * NB]))
    done(nc.vector.bn_aggr(mv[:, 0:2], stats[:].rearrange("p a b -> p (a b)")))
    nc.vector.tensor_scalar(mv[:, 2:3], mv[:, 1:2], LN_EPS, None, ALU.add).then_inc(root_ready, 1)
    dve.wait_ge(rooted, n + 1)
    done(nc.vector.reciprocal(mv[:, 2:3], mv[:, 2:3]))
    done(nc.vector.tensor_scalar(src, src, mv[:, 0:1], mv[:, 2:3], ALU.subtract, ALU.mult))
    done(nc.vector.tensor_tensor(src, src, g_row, ALU.mult))
    done(nc.vector.tensor_tensor(src, src, b_row, ALU.add))


def stage_mix_out(nc, mixT, w_out, x_dram, ln_rows, hres, h_dram):
    with Scope(nc, "mixo") as s:
        ws = s.sb("ws", [P, 2, KT, NB])
        rows = s.sb("rows", [P, 2, D])
        stats = s.sb("stats", [P, 2, 6])
        mv = s.sb("mv", [P, 3])
        ps = s.ps("ps", [P, 8, NB])
        w_in, r_in, x_in = s.sem("w_in"), s.sem("r_in"), s.sem("x_in")
        mm, v, root_ready, rooted, h_ready, h_out = (s.sem(n) for n in "mm vector_step root_ready rooted h_ready h_out".split())
        with nc.Block() as block:
            @block.sync
            def _(sp):
                for n in range(2):
                    sp.dma_start(ws[:, n, :, :], w_out[n]).then_inc(w_in, 16)
                sp.dma_start(hres[:], x_dram.rearrange("(t p) d -> p t d", p=P)).then_inc(x_in, 16)
                for n in range(2):
                    sp.dma_start(rows[:, n, :], ln_rows[n].partition_broadcast(P)).then_inc(r_in, 16)
                for t in range(TT):
                    sp.wait_ge(h_ready, t + 1)
                    sp.dma_start(h_dram[t * P:(t + 1) * P, :], hres[:, t, :]).then_inc(h_out, 16)
                sp.wait_ge(h_out, 16 * TT)

            @block.tensor
            def _(pe):
                pe.wait_ge(w_in, 32)
                for t in range(TT):
                    b = 2 * (t % 4)
                    if t >= 4:
                        pe.wait_ge(h_ready, t - 3)
                    for n in range(2):
                        for k in range(KT):
                            last = nc.tensor.matmul(ps[:, b + n, :], lhsT=mixT[:, k, t * P:(t + 1) * P], rhs=ws[:, n, k, :],
                                                    start=(k == 0), stop=(k == KT - 1))
                    last.then_inc(mm, 1)

            @block.scalar
            def _(act):
                for t in range(TT):
                    act.wait_ge(root_ready, t + 1)
                    nc.scalar.activation(mv[:, 2:3], mv[:, 2:3], ACT.Sqrt).then_inc(rooted, 1)

            @block.vector
            def _(dve):
                step = [0]

                def done(ins):
                    step[0] += 1
                    ins.then_inc(v, 1)
                    dve.wait_ge(v, step[0])

                dve.wait_ge(x_in, 16)
                dve.wait_ge(r_in, 32)
                for t in range(TT):
                    dve.wait_ge(mm, t + 1)
                    b = 2 * (t % 4)
                    h = hres[:, t, :]
                    done(nc.vector.scalar_tensor_tensor(out=h, in0=h, scalar=ALPHA, in1=ps[:, b:b + 2, :].rearrange("p a b -> p (a b)"),
                                                        op0=ALU.mult, op1=ALU.add))
                    layer_norm_steps(nc, dve, h, stats, mv, rows[:, 0, :], rows[:, 1, :], t, done, root_ready, rooted)
                    dve.sem_inc(h_ready, 1)


GROUPS = 4
PER_GROUP = 8
EXPERTS = GROUPS * PER_GROUP
D_EXP = D // 4
LOGITS = GROUPS + EXPERTS
MAX_MORE = S // P - 1
OVERFLOW = 2 * S // P - 1
BLOCKS = EXPERTS + OVERFLOW
ROWS = BLOCKS * P
FAR = 1e30


def stage_router(nc, hT, w_router, b_router, counts_in, dest, wgt, over, row_tok, tok_of_row, y_dram, ones, cumul,
                 ident):
    IG, IE, IB, IJ = 0, GROUPS, GROUPS + EXPERTS, GROUPS + EXPERTS + OVERFLOW
    with Scope(nc, "rt") as s:
        wr = s.sb("wr", [P, KT, LOGITS])
        br = s.sb("br", [P, LOGITS])
        cnt = s.sb("cnt", [P, GROUPS + EXPERTS + OVERFLOW + MAX_MORE])
        lg = s.sb("lg", [P, TT, LOGITS])
        a1 = s.sb("a1", [P, TT, 12])
        g4 = s.sb("g4", [P, 3, TT, GROUPS])
        em = s.sb("em", [P, TT, EXPERTS])
        e32 = s.sb("e32", [P, TT, EXPERTS])
        oh = s.sb("oh", [P, 2, TT, EXPERTS])
        both = s.sb("both", [P, TT, EXPERTS])
        cum = s.sb("cum", [P, TT, EXPERTS])
        row = s.sb("row", [P, 6, EXPERTS])
        more = s.sb("more", [P, EXPERTS, MAX_MORE])
        ble = s.sb("ble", [P, OVERFLOW, EXPERTS])
        blk = s.sb("blk", [P, OVERFLOW + 1])
        dst = s.sb("dst", [P, 2, TT])
        tok = s.sb("tok", [P, TT], I32)
        zero = s.sb("zero", [BLOCKS, P], I32)
        back = s.sb("back", [BLOCKS, P], I32)
        backf = s.sb("backf", [BLOCKS, P])
        blank = s.sb("blank", [P, D])
        pl = s.ps("pl", [P, TT, 64])
        pc = s.ps("pc", [P, TT, EXPERTS])
        pn = s.ps("pn", [P, EXPERTS])
        pt = s.ps("pt", [P, BLOCKS])
        cleared = s.sem("cleared")
        w_in, mm, v, exp_in, exps = s.sem("w_in"), s.sem("mm"), s.sem("vector_step"), s.sem("exp_in"), s.sem("exps")
        both_ready, placed, tok_ready, zero_ready = s.sem("both_ready"), s.sem("placed"), s.sem("tok_ready"), s.sem("zero_ready")
        zeroed, scattered, back_in, backf_ready, turned, ready = (s.sem(n) for n in "zeroed scattered back_in backf_ready turned ready".split())
        with nc.Block() as block:
            @block.sync
            def _(sp):
                sp.dma_start(wr[:], w_router).then_inc(w_in, 16)
                sp.dma_start(br[:], b_router.partition_broadcast(P)).then_inc(w_in, 16)
                sp.dma_start(cnt[:], counts_in.partition_broadcast(P)).then_inc(w_in, 16)
                sp.wait_ge(zero_ready, 2)
                sp.dma_start(row_tok.rearrange("(b p) a -> b (p a)", p=P), zero[:]).then_inc(zeroed, 16)
                sp.wait_ge(scattered, 16 * 2 * TT)
                sp.dma_start(back[:], row_tok.rearrange("(b p) a -> b (p a)", p=P)).then_inc(back_in, 16)

            @block.tensor
            def _(pe):
                pe.wait_ge(w_in, 48)
                for t in range(TT):
                    for k in range(KT):
                        last = nc.tensor.matmul(pl[:, t, 0:LOGITS], lhsT=hT[:, k, t * P:(t + 1) * P], rhs=wr[:, k, :],
                                                start=(k == 0), stop=(k == KT - 1))
                last.then_inc(mm, 1)
                pe.wait_ge(both_ready, 1)
                for t in range(TT):
                    for j in range(t + 1):
                        last = nc.tensor.matmul(pc[:, t, :], lhsT=(cumul if j == t else ones)[:], rhs=both[:, j, :],
                                                start=(j == 0), stop=(j == t))
                for j in range(TT):
                    last = nc.tensor.matmul(pn[:], lhsT=ones[:], rhs=both[:, j, :], start=(j == 0), stop=(j == TT - 1))
                last.then_inc(mm, 1)
                pe.wait_ge(backf_ready, 1)
                nc.tensor.transpose(pt[:], backf[:], ident[0:BLOCKS, 0:BLOCKS]).then_inc(turned, 1)

            @block.scalar
            def _(act):
                act.wait_ge(zero_ready, 2)
                for n in range(EXPERTS, BLOCKS):
                    act.dma_start(y_dram[n * P:(n + 1) * P, :], blank[:]).then_inc(cleared, 16)
                act.wait_ge(exp_in, 1)
                nc.scalar.activation(g4[:, 1, :, :], g4[:, 1, :, :], ACT.Exp).then_inc(exps, 1)
                act.wait_ge(exp_in, 2)
                nc.scalar.activation(a1[:, :, 5], a1[:, :, 5], ACT.Exp).then_inc(exps, 1)
                act.wait_ge(cleared, 16 * OVERFLOW)

            @block.gpsimd
            def _(pool):
                nc.gpsimd.iota(tok[:], pattern=[[P, TT]], base=0, channel_multiplier=1).then_inc(tok_ready, 1)
                nc.gpsimd.memset(zero[:], 0).then_inc(zero_ready, 1)
                nc.gpsimd.memset(blank[:], 0.0).then_inc(zero_ready, 1)
                pool.wait_ge(tok_ready, 1)
                pool.wait_ge(zeroed, 16)
                pool.wait_ge(placed, 1)
                for c in range(2):
                    for t in range(TT):
                        nc.gpsimd.indirect_dma_start(out=row_tok, out_offset=bass.IndirectOffsetOnAxis(ap=dest[:, c, t:t + 1], axis=0),
                                                     in_=tok[:, t:t + 1], in_offset=None).then_inc(scattered, 16)

            @block.vector
            def _(dve):
                step = [0]
                tt, ts, stt, red = (nc.vector.tensor_tensor, nc.vector.tensor_scalar, nc.vector.scalar_tensor_tensor,
                                    nc.vector.tensor_reduce)

                def done(ins):
                    step[0] += 1
                    ins.then_inc(v, 1)
                    dve.wait_ge(v, step[0])

                def over_tokens(a, n):
                    return a.unsqueeze(1).to_broadcast([P, TT, n])

                def over_last(a, n):
                    return a.unsqueeze(2).to_broadcast([P, TT, n])

                def first_max(vals, n, iota, scratch, top, index, onehot):
                    done(red(top, vals, AX.X, ALU.max))
                    done(tt(scratch, vals, over_last(top, n), ALU.is_lt))
                    done(stt(out=scratch, in0=scratch, scalar=1000.0, in1=over_tokens(iota, n), op0=ALU.mult, op1=ALU.add))
                    done(red(index, scratch, AX.X, ALU.min))
                    done(tt(onehot, over_tokens(iota, n), over_last(index, n), ALU.is_equal))

                dve.wait_ge(w_in, 48)
                dve.wait_ge(mm, 1)
                done(tt(lg[:], pl[:, :, 0:LOGITS], over_tokens(br[:], LOGITS), ALU.add))
                iota_g, iota_e = cnt[:, IG:IG + GROUPS], cnt[:, IE:IE + EXPERTS]
                gl, el = lg[:, :, 0:GROUPS], lg[:, :, GROUPS:]
                first_max(gl, GROUPS, iota_g, g4[:, 0], a1[:, :, 0], a1[:, :, 1], g4[:, 2])
                tt(g4[:, 1], gl, over_last(a1[:, :, 0], GROUPS), ALU.subtract).then_inc(exp_in, 1)
                grp = g4[:, 2].unsqueeze(3).to_broadcast([P, TT, GROUPS, PER_GROUP])
                done(tt(em[:].rearrange("p t (g e) -> p t g e", g=GROUPS), el.rearrange("p t (g e) -> p t g e", g=GROUPS), grp,
                        ALU.mult))
                done(ts(g4[:, 0], g4[:, 2], -1.0, FAR, ALU.add, ALU.mult))
                done(tt(em[:].rearrange("p t (g e) -> p t g e", g=GROUPS), em[:].rearrange("p t (g e) -> p t g e", g=GROUPS),
                        g4[:, 0].unsqueeze(3).to_broadcast([P, TT, GROUPS, PER_GROUP]), ALU.add))
                first_max(em[:], EXPERTS, iota_e, e32[:], a1[:, :, 2], a1[:, :, 3], oh[:, 0])
                done(stt(out=em[:], in0=oh[:, 0], scalar=-3.0 * FAR, in1=em[:], op0=ALU.mult, op1=ALU.add))
                first_max(em[:], EXPERTS, iota_e, e32[:], a1[:, :, 4], a1[:, :, 6], oh[:, 1])
                tt(a1[:, :, 5], a1[:, :, 4], a1[:, :, 2], ALU.subtract).then_inc(exp_in, 1)
                tt(both[:], oh[:, 0], oh[:, 1], ALU.add).then_inc(both_ready, 1)
                dve.wait_ge(exps, 1)
                done(red(a1[:, :, 7], g4[:, 1], AX.X, ALU.add))
                dve.wait_ge(exps, 2)
                done(ts(a1[:, :, 8], a1[:, :, 5], 1.0, None, ALU.add))
                done(tt(a1[:, :, 7], a1[:, :, 7], a1[:, :, 8], ALU.mult))
                done(nc.vector.reciprocal(wgt[:, 0, :], a1[:, :, 7]))
                done(tt(wgt[:, 1, :], wgt[:, 0, :], a1[:, :, 5], ALU.mult))
                dve.wait_ge(mm, 2)
                done(nc.vector.tensor_copy(row[:, 0, :], pn[:]))
                done(tt(more[:], row[:, 0, :].unsqueeze(2).to_broadcast([P, EXPERTS, MAX_MORE]),
                        cnt[:, IJ:IJ + MAX_MORE].unsqueeze(1).to_broadcast([P, EXPERTS, MAX_MORE]), ALU.is_gt))
                done(red(row[:, 1, :], more[:], AX.X, ALU.add))
                done(nc.vector.memset(row[:, 2, :], 1.0))
                done(nc.vector.tensor_tensor_scan(row[:, 3, :], row[:, 2, :], row[:, 1, :], 0.0, ALU.mult, ALU.add))
                done(tt(row[:, 4, :], row[:, 3, :], row[:, 1, :], ALU.subtract))
                done(ts(row[:, 5, :], row[:, 4, :], float(P), float((EXPERTS - 1) * P), ALU.mult, ALU.add))
                done(tt(ble[:], row[:, 3, :].unsqueeze(1).to_broadcast([P, OVERFLOW, EXPERTS]),
                        cnt[:, IB:IB + OVERFLOW].unsqueeze(2).to_broadcast([P, OVERFLOW, EXPERTS]), ALU.is_le))
                done(red(blk[:, 0:OVERFLOW], ble[:], AX.X, ALU.add))
                done(ts(blk[:, 0:OVERFLOW], blk[:, 0:OVERFLOW], float(EXPERTS - 1), None, ALU.min))
                done(nc.vector.tensor_copy(blk[:, OVERFLOW:], row[:, 3, EXPERTS - 1:]))
                done(nc.vector.tensor_copy(over[:], blk[0:1, :]))
                done(nc.vector.tensor_copy(cum[:], pc[:]))
                for c in range(2):
                    e = a1[:, :, 3] if c == 0 else a1[:, :, 6]
                    done(tt(e32[:], oh[:, c], cum[:], ALU.mult))
                    done(red(a1[:, :, 9], e32[:], AX.X, ALU.add))
                    done(ts(a1[:, :, 9], a1[:, :, 9], -1.0, None, ALU.add))
                    done(tt(e32[:], oh[:, c], over_tokens(row[:, 5, :], EXPERTS), ALU.mult))
                    done(red(a1[:, :, 10], e32[:], AX.X, ALU.add))
                    done(stt(out=a1[:, :, 10], in0=e, scalar=-float(P), in1=a1[:, :, 10], op0=ALU.mult, op1=ALU.add))
                    done(ts(a1[:, :, 11], a1[:, :, 9], float(P), None, ALU.is_ge))
                    done(tt(a1[:, :, 10], a1[:, :, 10], a1[:, :, 11], ALU.mult))
                    done(stt(out=a1[:, :, 9], in0=e, scalar=float(P), in1=a1[:, :, 9], op0=ALU.mult, op1=ALU.add))
                    done(tt(dst[:, c, :], a1[:, :, 9], a1[:, :, 10], ALU.add))
                nc.vector.tensor_copy(dest[:], dst[:]).then_inc(placed, 1)
                dve.wait_ge(back_in, 16)
                nc.vector.tensor_copy(backf[:], back[:]).then_inc(backf_ready, 1)
                dve.wait_ge(turned, 1)
                nc.vector.tensor_copy(tok_of_row[:], pt[:]).then_inc(ready, 1)
                dve.wait_ge(ready, 1)


def stage_experts(nc, h_dram, w_gu, w_d, over, tok_of_row, y_dram, ident):
    NW = 4
    with Scope(nc, "ex") as s:
        gu = s.sb("gu", [P, NW, KT, 2 * D_EXP])
        dn = s.sb("dn", [P, NW, 2, D])
        idx = s.sb("idx", [P, NW], I32)
        xg = s.sb("xg", [P, NW, D])
        xT = s.sb("xT", [P, 2, KT, P])
        sil = s.sb("sil", [P, 2, D_EXP])
        hid = s.sb("hid", [P, 2, D_EXP])
        hT = s.sb("hT", [P, 2, 2, P])
        y = s.sb("y", [P, 2, D])
        px = s.ps("px", [P, 2, NB])
        pg = s.ps("pg", [P, 2, NB])
        ph = s.ps("ph", [P, 2, NB])
        py = s.ps("py", [P, 2, NB])
        names = "x_turned x_taken gated silu hidden h_turned h_taken downed y_taken_a y_taken_v"

        class Ring:
            pass

        pipe, more = Ring(), Ring()
        for ring, tag in ((pipe, "p"), (more, "o")):
            (ring.x_turned, ring.x_taken, ring.gated, ring.silu, ring.hidden, ring.h_turned, ring.h_taken, ring.downed,
             ring.y_taken_a, ring.y_taken_v) = (s.sem(f"{tag}_{n}") for n in names.split())
        w_in = [s.sem(f"w_in{n}") for n in range(NW)]
        x_in = [s.sem(f"x_in{n}") for n in range(NW)]
        y_out = [s.sem("y_out0"), s.sem("y_out1")]
        idx_ready, gate = s.sem("idx_ready"), s.sem("pool_gate")
        o_w_in, o_x_in, o_y_out, o_idx, o_stored = (s.sem(n) for n in "o_w_in o_x_in o_y_out o_idx o_stored".split())
        y_rows = y_dram.rearrange("(b p) d -> b p d", p=P)

        def number_of_overflow(eng):
            return eng.value_load(over[0:1, OVERFLOW:OVERFLOW + 1], min_val=0, max_val=OVERFLOW)

        with nc.Block() as block:
            @block.sync
            def _(sp):
                def load(b, n):
                    sp.dma_start(gu[:, n, :, :], w_gu[b]).then_inc(w_in[n], 16)
                    sp.dma_start(dn[:, n, :, :], w_d[b]).then_inc(w_in[n], 16)

                def store(b, n):
                    sp.wait_ge(pipe.y_taken_a, b + 2)
                    sp.wait_ge(pipe.y_taken_v, b + 2)
                    sp.dma_start(y_rows[b], y[:, n % 2, :]).then_inc(y_out[n % 2], 16)

                for n in range(NW):
                    load(n, n)
                with sp.Fori(0, EXPERTS // NW - 1) as j:
                    for n in range(NW):
                        store(NW * j + n, n)
                        sp.wait_ge(pipe.downed, NW * j + n + 3)
                        load(NW * j + n + NW, n)
                for b in range(EXPERTS - NW, EXPERTS):
                    store(b, b % NW)
                sp.wait_ge(pipe.downed, EXPERTS + 2)
                n_over = number_of_overflow(sp)
                with sp.Fori(0, OVERFLOW) as b:
                    with sp.If(b < n_over):
                        e = sp.value_load(over[0:1, bass.ds(b, 1)], min_val=0, max_val=EXPERTS - 1)
                        sp.wait_ge(more.downed, b + 1)
                        sp.dma_start(gu[:, 0, :, :], w_gu[e]).then_inc(o_w_in, 16)
                        sp.dma_start(dn[:, 0, :, :], w_d[e]).then_inc(o_w_in, 16)
                        sp.wait_ge(more.y_taken_a, b + 1)
                        sp.wait_ge(more.y_taken_v, b + 1)
                        sp.dma_start(y_rows[EXPERTS + b], y[:, 0, :]).then_inc(o_y_out, 16)
                        sp.wait_ge(o_y_out, 16 * b + 16)
                        sp.sem_inc(o_stored, 1)
                for n in range(2):
                    sp.wait_ge(y_out[n], 16 * (EXPERTS // 2 + 1))

            @block.gpsimd
            def _(pool):
                def gather(b, n, index):
                    nc.gpsimd.tensor_copy(idx[:, n:n + 1], tok_of_row[:, index]).then_inc(idx_ready, 1)
                    pool.wait_ge(idx_ready, b + 1)
                    pool.sem_inc(gate, 1)
                    nc.gpsimd.indirect_dma_start(out=xg[:, n, :], out_offset=None, in_=h_dram,
                                                 in_offset=bass.IndirectOffsetOnAxis(ap=idx[:, n:n + 1], axis=0)
                                                 ).then_inc(x_in[n], 16)

                for n in range(NW):
                    gather(n, n, slice(n, n + 1))
                with pool.Fori(1, EXPERTS // NW) as j:
                    for n in range(NW):
                        pool.wait_ge(pipe.x_turned, NW * j + n - NW + 1)
                        pool.sem_inc(gate, 1)
                        gather(NW * j + n, n, bass.ds(NW * j + n, 1))
                pool.wait_ge(pipe.x_turned, EXPERTS)
                n_over = number_of_overflow(pool)
                with pool.Fori(0, OVERFLOW) as b:
                    with pool.If(b < n_over):
                        pool.wait_ge(more.x_turned, b + 1)
                        pool.sem_inc(gate, 1)
                        nc.gpsimd.tensor_copy(idx[:, 0:1], tok_of_row[:, bass.ds(b + EXPERTS, 1)]).then_inc(o_idx, 1)
                        pool.wait_ge(o_idx, b + 1)
                        pool.sem_inc(gate, 1)
                        nc.gpsimd.indirect_dma_start(out=xg[:, 0, :], out_offset=None, in_=h_dram,
                                                     in_offset=bass.IndirectOffsetOnAxis(ap=idx[:, 0:1], axis=0)
                                                     ).then_inc(o_x_in, 16)

            @block.tensor
            def _(pe):
                def turn_x(ring, b, n):
                    for k in range(KT):
                        last = nc.tensor.transpose(px[:, k // 4, (k % 4) * P:(k % 4 + 1) * P], xg[:, n, k * P:(k + 1) * P],
                                                   ident[:])
                    last.then_inc(ring.x_turned, 1)

                def up(ring, b, n):
                    for k in range(KT):
                        last = nc.tensor.matmul(pg[:, n % 2, :], lhsT=xT[:, n % 2, k, :], rhs=gu[:, n, k, :], start=(k == 0),
                                                stop=(k == KT - 1))
                    last.then_inc(ring.gated, 1)

                def turn_h(ring, b, n):
                    for j in range(2):
                        last = nc.tensor.transpose(ph[:, n % 2, j * P:(j + 1) * P], hid[:, n % 2, j * P:(j + 1) * P], ident[:])
                    last.then_inc(ring.h_turned, 1)

                def down(ring, b, n):
                    for half in range(2):
                        for j in range(2):
                            last = nc.tensor.matmul(py[:, half, :], lhsT=hT[:, n % 2, j, :],
                                                    rhs=dn[:, n, j, half * NB:(half + 1) * NB], start=(j == 0), stop=(j == 1))
                    last.then_inc(ring.downed, 1)

                def p_turn_x(b, n, turn):
                    pe.wait_ge(x_in[n], 16 * turn)
                    pe.wait_ge(pipe.x_taken, b + 1)
                    turn_x(pipe, b, n)

                def p_up(b, n, turn):
                    pe.wait_ge(w_in[n], 32 * turn)
                    pe.wait_ge(pipe.x_taken, b + 2)
                    pe.wait_ge(pipe.hidden, b + 1)
                    up(pipe, b, n)

                def p_turn_h(b, n):
                    pe.wait_ge(pipe.hidden, b + 3)
                    pe.wait_ge(pipe.h_taken, b + 1)
                    turn_h(pipe, b, n)

                def p_down(b, n):
                    pe.wait_ge(pipe.h_taken, b + 3)
                    pe.wait_ge(pipe.y_taken_a, b + 1)
                    pe.wait_ge(pipe.y_taken_v, b + 1)
                    down(pipe, b, n)

                pe.sem_inc(pipe.gated, 2)
                pe.sem_inc(pipe.h_turned, 2)
                pe.sem_inc(pipe.downed, 2)
                pe.sem_inc(more.downed, 1)
                pe.sem_inc(more.x_turned, 1)
                p_turn_x(0, 0, 1)
                p_turn_x(1, 1, 1)
                p_up(0, 0, 1)
                with pe.Fori(0, EXPERTS // NW - 1) as j:
                    for n in range(NW):
                        b = NW * j + n
                        p_up(b + 1, (n + 1) % NW, j + 1 + (n + 1) // NW)
                        p_turn_h(b, n)
                        p_turn_x(b + 2, (n + 2) % NW, j + 1 + (n + 2) // NW)
                        p_down(b, n)
                for b in range(EXPERTS - NW, EXPERTS):
                    if b + 1 < EXPERTS:
                        p_up(b + 1, (b + 1) % NW, EXPERTS // NW)
                    p_turn_h(b, b % NW)
                    if b + 2 < EXPERTS:
                        p_turn_x(b + 2, (b + 2) % NW, EXPERTS // NW)
                    p_down(b, b % NW)
                pe.wait_ge(pipe.y_taken_a, EXPERTS + 1)
                pe.wait_ge(pipe.y_taken_v, EXPERTS + 1)
                n_over = number_of_overflow(pe)
                with pe.Fori(0, OVERFLOW) as b:
                    with pe.If(b < n_over):
                        pe.wait_ge(o_x_in, 16 * b + 16)
                        turn_x(more, b, 0)
                        pe.wait_ge(o_w_in, 32 * b + 32)
                        pe.wait_ge(more.x_taken, b + 1)
                        up(more, b, 0)
                        pe.wait_ge(more.hidden, b + 1)
                        turn_h(more, b, 0)
                        pe.wait_ge(more.h_taken, b + 1)
                        down(more, b, 0)

            @block.scalar
            def _(act):
                def take_x(ring, b, n):
                    nc.scalar.copy(xT[:, n % 2, :, :].rearrange("p a b -> p (a b)"),
                                   px[:].rearrange("p a b -> p (a b)")).then_inc(ring.x_taken, 1)

                def silu(ring, b, n):
                    nc.scalar.activation(sil[:, n % 2, :], pg[:, n % 2, 0:D_EXP], ACT.Silu).then_inc(ring.silu, 1)

                def take_y(ring, b, n):
                    nc.scalar.copy(y[:, n % 2, NB:], py[:, 1, :]).then_inc(ring.y_taken_a, 1)

                def p_take_x(b, n):
                    act.wait_ge(pipe.x_turned, b + 1)
                    act.wait_ge(pipe.gated, b + 1)
                    take_x(pipe, b, n)

                def p_silu(b, n):
                    act.wait_ge(pipe.gated, b + 3)
                    act.wait_ge(pipe.hidden, b + 1)
                    silu(pipe, b, n)

                def p_take_y(b, n, turn):
                    act.wait_ge(pipe.downed, b + 3)
                    act.wait_ge(y_out[n % 2], 16 * turn)
                    take_y(pipe, b, n)

                act.sem_inc(pipe.x_taken, 1)
                act.sem_inc(pipe.y_taken_a, 1)
                p_take_x(0, 0)
                p_take_x(1, 1)
                p_silu(0, 0)
                with act.Fori(0, EXPERTS // NW - 1) as j:
                    for n in range(NW):
                        b = NW * j + n
                        p_silu(b + 1, n + 1)
                        p_take_x(b + 2, n)
                        p_take_y(b, n, 2 * j + n // 2 + 1)
                for b in range(EXPERTS - NW, EXPERTS):
                    if b + 1 < EXPERTS:
                        p_silu(b + 1, b + 1)
                    if b + 2 < EXPERTS:
                        p_take_x(b + 2, b)
                    p_take_y(b, b, b // 2 + 1)
                act.wait_ge(y_out[0], 16 * (EXPERTS // 2 + 1))
                n_over = number_of_overflow(act)
                with act.Fori(0, OVERFLOW) as b:
                    with act.If(b < n_over):
                        act.wait_ge(more.x_turned, b + 2)
                        take_x(more, b, 0)
                        act.wait_ge(more.gated, b + 1)
                        silu(more, b, 0)
                        act.wait_ge(more.downed, b + 2)
                        act.wait_ge(o_stored, b + 1)
                        take_y(more, b, 0)

            @block.vector
            def _(dve):
                def hidden(ring, b, n):
                    nc.vector.tensor_tensor(hid[:, n % 2, :], pg[:, n % 2, D_EXP:], sil[:, n % 2, :], ALU.mult
                                            ).then_inc(ring.hidden, 1)

                def take_h(ring, b, n):
                    nc.vector.tensor_copy(hT[:, n % 2, :, :].rearrange("p a b -> p (a b)"), ph[:, n % 2, 0:2 * P]
                                          ).then_inc(ring.h_taken, 1)

                def take_y(ring, b, n):
                    nc.vector.tensor_copy(y[:, n % 2, 0:NB], py[:, 0, :]).then_inc(ring.y_taken_v, 1)

                def p_hidden(b, n):
                    dve.wait_ge(pipe.silu, b + 1)
                    dve.wait_ge(pipe.h_turned, b + 1)
                    hidden(pipe, b, n)

                def p_take_h(b, n):
                    dve.wait_ge(pipe.h_turned, b + 3)
                    dve.wait_ge(pipe.downed, b + 1)
                    take_h(pipe, b, n)

                def p_take_y(b, n, turn):
                    dve.wait_ge(pipe.downed, b + 3)
                    dve.wait_ge(y_out[n % 2], 16 * turn)
                    take_y(pipe, b, n)

                dve.sem_inc(pipe.hidden, 2)
                dve.sem_inc(pipe.h_taken, 2)
                dve.sem_inc(pipe.y_taken_v, 1)
                dve.sem_inc(y_out[0], 16)
                dve.sem_inc(y_out[1], 16)
                dve.sem_inc(o_stored, 1)
                p_hidden(0, 0)
                with dve.Fori(0, EXPERTS // NW - 1) as j:
                    for n in range(NW):
                        b = NW * j + n
                        p_hidden(b + 1, n + 1)
                        p_take_h(b, n)
                        p_take_y(b, n, 2 * j + n // 2 + 1)
                for b in range(EXPERTS - NW, EXPERTS):
                    if b + 1 < EXPERTS:
                        p_hidden(b + 1, b + 1)
                    p_take_h(b, b)
                    p_take_y(b, b, b // 2 + 1)
                dve.wait_ge(y_out[0], 16 * (EXPERTS // 2 + 1))
                n_over = number_of_overflow(dve)
                with dve.Fori(0, OVERFLOW) as b:
                    with dve.If(b < n_over):
                        dve.wait_ge(more.silu, b + 1)
                        hidden(more, b, 0)
                        dve.wait_ge(more.h_turned, b + 1)
                        take_h(more, b, 0)
                        dve.wait_ge(more.downed, b + 2)
                        dve.wait_ge(o_stored, b + 1)
                        take_y(more, b, 0)


def stage_combine(nc, hres, y_dram, dest, wgt, ln_rows, out_rows):
    with Scope(nc, "cmb") as s:
        rows = s.sb("rows", [P, 2, D])
        yg = s.sb("yg", [P, 4, 2, D])
        stats = s.sb("stats", [P, 2, 6])
        mv = s.sb("mv", [P, 3])
        r_in, g_in = s.sem("r_in"), [s.sem(f"g_in{n}") for n in range(4)]
        v, root_ready, rooted, ready, stored = (s.sem(n) for n in "vector_step root_ready rooted ready stored".split())
        with nc.Block() as block:
            @block.sync
            def _(sp):
                for n in range(2):
                    sp.dma_start(rows[:, n, :], ln_rows[n].partition_broadcast(P)).then_inc(r_in, 16)
                for t in range(TT):
                    sp.wait_ge(ready, t + 1)
                    sp.dma_start(out_rows[t * P:(t + 1) * P, :], hres[:, t, :]).then_inc(stored, 16)
                sp.wait_ge(stored, 16 * TT)

            @block.gpsimd
            def _(pool):
                for t in range(TT):
                    if t >= 4:
                        pool.wait_ge(ready, t - 3)
                    for c in range(2):
                        nc.gpsimd.indirect_dma_start(out=yg[:, t % 4, c, :], out_offset=None, in_=y_dram,
                                                     in_offset=bass.IndirectOffsetOnAxis(ap=dest[:, c, t:t + 1], axis=0)
                                                     ).then_inc(g_in[t % 4], 16)

            @block.scalar
            def _(act):
                for t in range(TT):
                    act.wait_ge(root_ready, t + 1)
                    nc.scalar.activation(mv[:, 2:3], mv[:, 2:3], ACT.Sqrt).then_inc(rooted, 1)

            @block.vector
            def _(dve):
                step = [0]

                def done(ins):
                    step[0] += 1
                    ins.then_inc(v, 1)
                    dve.wait_ge(v, step[0])

                dve.wait_ge(r_in, 32)
                for t in range(TT):
                    h = hres[:, t, :]
                    done(nc.vector.tensor_scalar(h, h, ALPHA, None, ALU.mult))
                    dve.wait_ge(g_in[t % 4], 32 * (t // 4 + 1))
                    for c in range(2):
                        done(nc.vector.scalar_tensor_tensor(out=h, in0=yg[:, t % 4, c, :], scalar=wgt[:, c, t:t + 1], in1=h,
                                                            op0=ALU.mult, op1=ALU.add))
                    layer_norm_steps(nc, dve, h, stats, mv, rows[:, 0, :], rows[:, 1, :], t, done, root_ready, rooted)
                    dve.sem_inc(ready, 1)


def first_program(nc, A, x_dram, consts):
    ident, ones, cumul, ident16, future16 = consts
    with Scope(nc, "first") as g:
        xres = g.sb("xres", [P, TT, D])
        with Scope(nc, "b1") as b:
            gates = b.sb("gates", [P, 2, D])
            modc = b.sb("modc", [P, 2, 2, KT])
            stage_modulation(nc, A["x"], A["cols1"], A["w_ada"], A["b_ada"], xres, modc, gates, ones)
            with Scope(nc, "att_data") as a:
                qkv = a.sb("qkv", [P, TT, QKV])
                ss = a.sb("ss", [P, TT, 3 * HEADS])
                neg_f = a.sb("neg_f", [P, TT, HEADS])
                with Scope(nc, "h1") as h:
                    hT = h.sb("hT", [P, KT, S])
                    stage_norm(nc, "norm1", xres, hT, modc[:, 0], ident)
                    stage_qkv(nc, hT, A["w_qkv"], A["w_f"], A["b_f"], qkv, ss, neg_f, cumul, ones)
                with Scope(nc, "o") as o:
                    o_all = o.sb("o_all", [P, TT, D])
                    stage_attention(nc, qkv, ss, neg_f, A["qk_gain"], o_all, ident, ident16, future16)
                    stage_out(nc, "out1", o_all, A["w_o"], xres, gates[:, 0, :], ident,
                              qkv[:].rearrange("p t c -> p (t c)"))
            with Scope(nc, "h2") as h:
                hT = h.sb("hT", [P, KT, S])
                stage_norm(nc, "norm2", xres, hT, modc[:, 1], ident)
                stage_mlp(nc, hT, A["w1"], A["w2"], xres, gates[:, 1, :], ident)
        with Scope(nc, "end") as e, nc.Block() as block:
            done = e.sem("done")

            @block.sync
            def _(sp):
                sp.dma_start(x_dram.rearrange("(t p) d -> p t d", p=P), xres[:]).then_inc(done, 16)
                sp.wait_ge(done, 16)


def third_program(nc, A, hres, h_dram, row_tok, y_dram, out_rows, ident, ones, cumul):
    with Scope(nc, "b3") as b:
        dest = b.sb("dest", [P, 2, TT], I32)
        wgt = b.sb("wgt", [P, 2, TT])
        over = b.sb("over", [1, OVERFLOW + 1], I32)
        tok_of_row = b.sb("tok_of_row", [P, BLOCKS], I32)
        with Scope(nc, "rh") as r:
            hT = r.sb("hT", [P, KT, S])
            stage_turn(nc, "turn3", hres, hT, ident)
            stage_router(nc, hT, A["w_router"], A["b_router"], A["counts"], dest, wgt, over, row_tok, tok_of_row, y_dram, ones,
                         cumul, ident)
        stage_experts(nc, h_dram, A["w_gu"], A["w_d"], over, tok_of_row, y_dram, ident)
        stage_combine(nc, hres, y_dram, dest, wgt, A["ln2"], out_rows)


def second_program(nc, A, x_dram, h_dram, row_tok, y_dram, out_rows, consts):
    ident, ones, cumul = consts[:3]
    with Scope(nc, "b2") as b:
        with Scope(nc, "mx") as m:
            mixT = m.sb("mixT", [P, KT, S])
            with Scope(nc, "x2") as x2:
                xT = x2.sb("xT", [P, KT, S])
                lora_in = x2.sb("lora_in", [P, 2, S])
                with Scope(nc, "xr") as xr:
                    xres = xr.sb("xres", [P, TT, D])
                    load_rows(nc, "ld", x_dram, xres)
                    stage_turn(nc, "turn2", xres, xT, ident)
                stage_pool(nc, xT, A["w_head"], A["head_cols"], A["pool_w"], A["inv_count"], mixT, lora_in)
                stage_rwkv(nc, xT, A["w_rkv"], A["lora_up"], A["pair_cols"], A["window_consts"], A["scan_keep"], lora_in,
                           mixT, ident)
            hres = m.sb("hres", [P, TT, D])
            stage_mix_out(nc, mixT, A["w_mix"], x_dram, A["ln1"], hres, h_dram)
            third_program(nc, A, hres, h_dram, row_tok, y_dram, out_rows, ident, ones, cumul)


def load_rows(nc, tag, dram, tile):
    with Scope(nc, tag) as s, nc.Block() as block:
        rows_in = s.sem("rows_in")

        @block.sync
        def _(sp):
            sp.dma_start(tile[:], dram.rearrange("(t p) d -> p t d", p=P)).then_inc(rows_in, 16)
            sp.wait_ge(rows_in, 16)


def col(v):
    return v.reshape(-1, P).T


def chunks(w, n):
    k, m = w.shape
    return w.reshape(k // P, P, m // n, n).transpose(2, 1, 0, 3)


def layouts_second(np, I):
    wi = I["w_in_2"][0]
    pool, rw = wi[:, :256], wi[:, 256:]
    dr = PAIRS * P
    r, k, v = (rw[:, n * dr:(n + 1) * dr] for n in range(3))
    head = np.concatenate([pool, rw[:, 3 * dr:]], axis=1)
    mu = I["mu_shift_2"][0]
    windows = (2, 4, 8, 16)
    t = np.arange(S)
    w_of = np.repeat(np.array(windows), 64).reshape(2, P)
    inv_count = (1.0 / np.minimum(t[None, None, :16] + 1, w_of[:, :, None])).astype(np.float32).transpose(1, 0, 2)
    head_cols = np.concatenate([col(mu[3 * dr:]), col(I["pool_scale_2"][0]), (1.0 / w_of).astype(np.float32).T], axis=1)
    pool_w = np.zeros((P, 2, P), np.float32)
    for g in range(4):
        h = slice(64 * (g % 2), 64 * (g % 2) + 64)
        pool_w[h, g // 2, h] = I["pool_w_2"][0, g]
    rkv = np.stack([np.stack([chunks(w, P)[p] for w in (r, k, v)], axis=1) for p in range(PAIRS)])
    up = np.zeros((PAIRS, P, 2, P), np.float32)
    for p in range(PAIRS):
        c = slice(p * P, (p + 1) * P)
        up[p, :64, 0], up[p, 64:, 0], up[p, :, 1] = I["w_up_2"][0][:, c], I["a_up_2"][0][:, c], I["g_up_2"][0][:, c]
    per = [mu[0:dr], mu[dr:2 * dr], mu[2 * dr:3 * dr], I["w0_2"][0], I["a0_2"][0], I["k_k_2"][0], I["k_a_2"][0],
           I["r_k_2"][0].reshape(-1), I["lnx_g_2"][0], I["lnx_b_2"][0]]
    pair_cols = np.stack([col(a) for a in per], axis=2).reshape(P, PAIRS * NPAR)
    a = np.arange(P)
    src, dst = a[:, None], a[None, :]
    masks = [src < dst, src <= dst, src < dst, src <= dst]
    for l in range(LEVELS):
        n = 1 << l
        masks.append((src // (2 * n) == dst // (2 * n)) & (src // n < dst // n))
    same = src // 64 == dst // 64
    cst = np.stack([m.astype(np.float32) for m in masks + [same]] + [same.astype(np.float32) / 64], axis=1)
    keep = np.broadcast_to((t % WIN != 0).astype(np.float32), (P, S))
    return {
        "w_head": chunks(head, P).transpose(1, 0, 2, 3), "head_cols": head_cols, "pool_w": pool_w, "inv_count": inv_count,
        "w_rkv": rkv, "lora_up": up, "pair_cols": pair_cols, "window_consts": cst, "scan_keep": keep,
        "w_mix": chunks(I["w_out_2"][0], NB), "ln1": np.stack([I["ln1_g_2"][0], I["ln1_b_2"][0]]),
    }


def layouts_third(np, I):
    gu = np.concatenate([I["exp_gate_2"][0], I["exp_up_2"][0]], axis=2)
    counts = np.concatenate([np.arange(GROUPS), np.arange(EXPERTS), np.arange(OVERFLOW), P * np.arange(1, MAX_MORE + 1)])
    return {
        "w_router": np.concatenate([I["router_group_2"][0], I["router_expert_2"][0]], axis=1).reshape(KT, P, LOGITS)
        .transpose(1, 0, 2),
        "b_router": np.concatenate([I["router_group_b_2"][0], I["router_expert_b_2"][0]]),
        "counts": counts.astype(np.float32),
        "w_gu": gu.reshape(EXPERTS, KT, P, 2 * D_EXP).transpose(0, 2, 1, 3),
        "w_d": I["exp_down_2"][0].reshape(EXPERTS, 2, P, D).transpose(0, 2, 1, 3),
        "ln2": np.stack([I["ln2_g_2"][0], I["ln2_b_2"][0]]),
    }


def layouts_first(np, I):
    wi = I["fox_w_in"][0]
    return {
        "x": I["x"][0],
        "cols1": np.concatenate([col(I["c"][0]), col(I["b_ada"][0]), col(I["norm_mix"][0]), col(I["norm_mlp"][0])], axis=1),
        "w_ada": I["w_ada"][0],
        "b_ada": I["b_ada"][0],
        "w_qkv": chunks(wi[:, :QKV], QN),
        "w_f": wi[:, QKV:].reshape(KT, P, HEADS).transpose(1, 0, 2),
        "b_f": I["fox_b_f"][0],
        "qk_gain": np.stack([I["fox_q_norm"][0], I["fox_k_norm"][0]], axis=1),
        "w_o": chunks(I["fox_w_out"][0], NB),
        "w1": chunks(I["w_mlp_in"][0], P),
        "w2": I["w_mlp_out"][0].reshape(FT, P, D),
    }


def kernel(**inputs):
    import numpy as np
    import concourse.bacc as _bacc
    from concourse.bass_utils import run_bass_kernel_spmd as _run

    I = {k: np.asarray(v) for k, v in inputs.items()}
    L = {**layouts_first(np, I), **layouts_second(np, I), **layouts_third(np, I)}
    nc = _bacc.Bacc("TRN2", target_bir_lowering=False, num_devices=1)
    arrays, A = {}, {}
    for name, a in L.items():
        a = np.ascontiguousarray(a)
        arrays[f"in_{name}"] = a
        A[name] = nc.dram_tensor(f"in_{name}", a.shape, mybir.dt.from_np(a.dtype), kind="ExternalInput").ap()
    out = nc.dram_tensor("out_0", (1, S, D), F32, kind="ExternalOutput").ap()
    x_mid = nc.dram_tensor("x_mid", (S, D), F32, kind="Internal").ap()
    h_rows = nc.dram_tensor("h_rows", (S, D), F32, kind="Internal").ap()
    row_tok = nc.dram_tensor("row_tok", (ROWS, 1), I32, kind="Internal").ap()
    y_rows = nc.dram_tensor("y_rows", (ROWS, D), F32, kind="Internal").ap()
    USED.clear()
    with Scope(nc, "all") as g:
        consts = constants(nc, g)
        first_program(nc, A, x_mid, consts)
        clear_semaphores(nc)
        second_program(nc, A, x_mid, h_rows, row_tok, y_rows, out.rearrange("b s d -> (b s) d"), consts)
    r = _run(nc, [arrays], core_ids=[0])
    return r.results[0]["out_0"]
```

```python
from contextlib import ExitStack

import concourse.bass as bass
from concourse import mybir

F32 = mybir.dt.float32
BF16 = mybir.dt.bfloat16
I32 = mybir.dt.int32
U32 = mybir.dt.uint32
ALU = mybir.AluOpType
ACT = mybir.ActivationFunctionType
AX = mybir.AxisListType

P = 128
S = 1024
D = 1024
TT = S // P
KT = D // P
NB = 512
HEADS = 16
HD = D // HEADS
QKV = 3 * D
QN = 384
D_FF = 4 * D
FT = D_FF // P
EPS = 1e-6


class Scope:

    def __init__(self, nc, tag):
        self.nc, self.tag, self.stack = nc, tag, ExitStack()

    def __enter__(self):
        self.stack.__enter__()
        return self

    def __exit__(self, *a):
        return self.stack.__exit__(*a)

    def sb(self, name, shape, dt=F32):
        return self.stack.enter_context(self.nc.sbuf_tensor(f"{self.tag}_{name}", shape, dt))

    def ps(self, name, shape, dt=F32):
        return self.stack.enter_context(self.nc.psum_tensor(f"{self.tag}_{name}", shape, dt))

    def sem(self, name):
        handle = self.stack.enter_context(self.nc.semaphore(f"{self.tag}_{name}"))
        USED.append(handle)
        return handle


USED = []


def clear_semaphores(nc):
    numbers = sorted({handle.num for handle in USED})
    USED.clear()
    with nc.Block() as block:
        @block.gpsimd
        def _(pool):
            at = 0
            while at < len(numbers):
                end = at
                while end + 1 < len(numbers) and numbers[end + 1] == numbers[end] + 1:
                    end += 1
                pool.sem_clear(range(numbers[at], numbers[end] + 1))
                at = end + 1


def constants(nc, scope):
    ident = scope.sb("ident", [P, P])
    ones = scope.sb("ones", [P, P])
    cumul = scope.sb("cumul", [P, P])
    ident16 = scope.sb("ident16", [P, P], BF16)
    future16 = scope.sb("future16", [P, P], BF16)
    with Scope(nc, "cst") as c, nc.Block() as block:
        cleared = c.sem("cleared")
        built = c.sem("built")

        @block.gpsimd
        def _(pool):
            nc.gpsimd.memset(ident[:], 0.0).then_inc(cleared, 1)
            nc.gpsimd.memset(ones[:], 1.0).then_inc(cleared, 1)
            nc.gpsimd.memset(cumul[:], 1.0).then_inc(cleared, 1)
            nc.gpsimd.memset(ident16[:], 0.0).then_inc(cleared, 1)
            nc.gpsimd.memset(future16[:], 0.0).then_inc(cleared, 1)
            pool.wait_ge(cleared, 5)
            for m in (ident, ident16):
                nc.gpsimd.affine_select(out=m[:], in_=m[:], compare_op=ALU.not_equal, fill=1.0, base=0,
                                        pattern=[[-1, P]], channel_multiplier=1).then_inc(built, 1)
            nc.gpsimd.affine_select(out=cumul[:], in_=cumul[:], compare_op=ALU.is_ge, fill=0.0, base=0,
                                    pattern=[[1, P]], channel_multiplier=-1).then_inc(built, 1)
            nc.gpsimd.affine_select(out=future16[:], in_=future16[:], compare_op=ALU.is_ge, fill=-1e30, base=0,
                                    pattern=[[-1, P]], channel_multiplier=1).then_inc(built, 1)
            pool.wait_ge(built, 4)
    return ident, ones, cumul, ident16, future16


def stage_modulation(nc, x, cols1, w_ada, b_ada, xres, modc, gates, ones):
    CB, CN1, CN2 = KT, KT + 6 * KT, 2 * KT + 6 * KT
    with Scope(nc, "mod") as s:
        cols = s.sb("cols", [P, 9 * KT])
        silu = s.sb("silu", [P, 3, KT])
        wa = s.sb("wa", [P, 2, 6 * D])
        acc = s.sb("acc", [P, 6 * D])
        brow = s.sb("brow", [P, 2, D])
        mod = s.sb("mod", [P, 6 * KT])
        pmod = s.ps("pmod", [P, 6 * KT])
        pgate = s.ps("pgate", [P, 4, NB])
        cols_in, x_in, brow_in = s.sem("cols_in"), s.sem("x_in"), s.sem("brow_in")
        w_in = [s.sem("w_in0"), s.sem("w_in1")]
        w_used, silu_st, acc_done = s.sem("w_used"), s.sem("silu_st"), s.sem("acc_done")
        silu_exp, mm_mod, mm_gate, mod_done = s.sem("silu_exp"), s.sem("mm_mod"), s.sem("mm_gate"), s.sem("mod_done")
        finished = s.sem("finished")
        with nc.Block() as block:
            @block.sync
            def _(sp):
                sp.dma_start(cols[:], cols1).then_inc(cols_in, 16)
                for k in range(KT):
                    if k >= 2:
                        sp.wait_ge(w_used, k - 1)
                    sp.dma_start(wa[:, k % 2, :], w_ada[k * P:(k + 1) * P, :]).then_inc(w_in[k % 2], 16)

            @block.scalar
            def _(act):
                act.dma_start(xres[:], x.rearrange("(t p) d -> p t d", p=P)).then_inc(x_in, 16)
                for g, off in enumerate((2 * D, 5 * D)):
                    act.dma_start(brow[:, g, :], b_ada[off:off + D].partition_broadcast(P)).then_inc(brow_in, 16)
                act.wait_ge(cols_in, 16)
                nc.scalar.activation(silu[:, 0, :], cols[:, 0:KT], ACT.Exp, scale=-1.0).then_inc(silu_exp, 1)
                act.wait_ge(x_in, 16)

            @block.vector
            def _(dve):
                dve.wait_ge(silu_exp, 1)
                nc.vector.tensor_scalar_add(silu[:, 1, :], silu[:, 0, :], 1.0).then_inc(silu_st, 1)
                dve.wait_ge(silu_st, 1)
                nc.vector.reciprocal(silu[:, 2, :], silu[:, 1, :]).then_inc(silu_st, 1)
                dve.wait_ge(silu_st, 2)
                nc.vector.tensor_tensor(silu[:, 0, :], silu[:, 2, :], cols[:, 0:KT], ALU.mult).then_inc(silu_st, 1)
                dve.wait_ge(silu_st, 3)
                for k in range(KT):
                    dve.wait_ge(w_in[k % 2], 16 * (k // 2 + 1))
                    if k == 0:
                        nc.vector.tensor_scalar(acc[:], wa[:, 0, :], silu[:, 0, 0:1], None,
                                                ALU.mult).then_inc(w_used, 1)
                    else:
                        dve.wait_ge(w_used, k)
                        nc.vector.scalar_tensor_tensor(out=acc[:], in0=wa[:, k % 2, :], scalar=silu[:, 0, k:k + 1],
                                                       in1=acc[:], op0=ALU.mult, op1=ALU.add).then_inc(w_used, 1)
                dve.wait_ge(mm_mod, 1)
                nc.vector.tensor_tensor(mod[:], pmod[:], cols[:, CB:CB + 6 * KT], ALU.add).then_inc(mod_done, 1)
                dve.wait_ge(mod_done, 1)
                for n, (norm, shift, scale) in enumerate(((CN1, 0, KT), (CN2, 3 * KT, 4 * KT))):
                    nc.vector.scalar_tensor_tensor(out=modc[:, n, 0, :], in0=mod[:, scale:scale + KT], scalar=1.0,
                                                   in1=cols[:, norm:norm + KT], op0=ALU.add,
                                                   op1=ALU.mult).then_inc(finished, 1)
                    nc.vector.tensor_copy(modc[:, n, 1, :], mod[:, shift:shift + KT]).then_inc(finished, 1)
                dve.wait_ge(mm_gate, 1)
                dve.wait_ge(brow_in, 32)
                for g in range(2):
                    nc.vector.tensor_tensor(gates[:, g, :], pgate[:, 2 * g:2 * g + 2, :].rearrange("p a b -> p (a b)"),
                                            brow[:, g, :], ALU.add).then_inc(finished, 1)
                dve.wait_ge(finished, 6)

            @block.tensor
            def _(pe):
                pe.wait_ge(w_used, KT)
                for m in range(6 * KT):
                    last = nc.tensor.matmul(pmod[:, m:m + 1], lhsT=acc[:, m * P:(m + 1) * P], rhs=ones[:, 0:1],
                                            start=True, stop=True)
                last.then_inc(mm_mod, 1)
                for g, off in enumerate((2 * D, 5 * D)):
                    for h in range(2):
                        last = nc.tensor.matmul(pgate[:, 2 * g + h, :], lhsT=ones[:],
                                                rhs=acc[:, off + h * NB:off + (h + 1) * NB], start=True, stop=True)
                last.then_inc(mm_gate, 1)


def stage_norm(nc, tag, xres, hT, modc, ident):
    with Scope(nc, tag) as s:
        xn = s.sb("xn", [P, TT, D])
        ss = s.sb("ss", [P, TT])
        st = s.sb("st", [P, 3, TT])
        pt = s.ps("pt", [P, 4, NB])
        sq_done, var_ok, root, rstd_ok = s.sem("sq_done"), s.sem("var_ok"), s.sem("root"), s.sem("rstd_ok")
        xn_done, turned, taken_a, taken_v = s.sem("xn_done"), s.sem("turned"), s.sem("taken_a"), s.sem("taken_v")
        with nc.Block() as block:
            @block.scalar
            def _(act):
                for t in range(TT):
                    nc.scalar.activation(xn[:, t, :], xres[:, t, :], ACT.Square,
                                         accum_out=ss[:, t:t + 1]).then_inc(sq_done, 1)
                act.wait_ge(var_ok, 1)
                nc.scalar.activation(st[:, 1, :], st[:, 0, :], ACT.Sqrt).then_inc(root, 1)
                for r in range(1, 2 * KT, 2):
                    act.wait_ge(turned, r + 1)
                    c, half = r // 2, r % 2
                    nc.scalar.activation(hT[:, c, half * NB:(half + 1) * NB], pt[:, r % 4, :], ACT.Identity,
                                         scale=modc[:, 0, c:c + 1], bias=modc[:, 1, c:c + 1]).then_inc(taken_a, 1)
                act.wait_ge(taken_a, KT)

            @block.vector
            def _(dve):
                dve.wait_ge(sq_done, TT)
                nc.vector.tensor_scalar(st[:, 0, :], ss[:], 1.0 / D, EPS, ALU.mult, ALU.add).then_inc(var_ok, 1)
                dve.wait_ge(root, 1)
                nc.vector.reciprocal(st[:, 2, :], st[:, 1, :]).then_inc(rstd_ok, 1)
                dve.wait_ge(rstd_ok, 1)
                for t in range(TT):
                    nc.vector.tensor_scalar(xn[:, t, :], xres[:, t, :], st[:, 2, t:t + 1], None,
                                            ALU.mult).then_inc(xn_done, 1)
                for r in range(0, 2 * KT, 2):
                    dve.wait_ge(turned, r + 1)
                    c = r // 2
                    nc.vector.tensor_scalar(hT[:, c, 0:NB], pt[:, r % 4, :], modc[:, 0, c:c + 1],
                                            modc[:, 1, c:c + 1], ALU.mult, ALU.add).then_inc(taken_v, 1)
                dve.wait_ge(taken_v, KT)

            @block.tensor
            def _(pe):
                for r in range(2 * KT):
                    c, half = r // 2, r % 2
                    if r < 2:
                        pe.wait_ge(xn_done, 4 * (r + 1))
                    if r >= 4:
                        pe.wait_ge(taken_a if r % 2 else taken_v, r // 2 - 1)
                    for j in range(4):
                        last = nc.tensor.transpose(pt[:, r % 4, j * P:(j + 1) * P],
                                                   xn[:, 4 * half + j, c * P:(c + 1) * P], ident[:])
                    last.then_inc(turned, 1)


def stage_qkv(nc, hT, w_qkv, w_f, bf_row, qkv, ss, neg_f, cumul, ones):
    CH = QKV // QN
    HPC = QN // HD
    with Scope(nc, "qkv") as s:
        wq = s.sb("wq", [P, 2, KT, QN])
        wf = s.sb("wf", [P, KT, HEADS])
        fb = s.sb("fb", [P, HEADS])
        lf = s.sb("lf", [P, 4, TT, HEADS])
        sq = s.sb("sq", [P, 2, QN])
        pq = s.ps("pq", [P, 4, NB])
        pf = s.ps("pf", [P, TT, HEADS])
        pc = s.ps("pc", [P, TT, HEADS])
        w_in = [s.sem("w_in0"), s.sem("w_in1")]
        wf_in, mm, copied, squared, summed = s.sem("wf_in"), s.sem("mm"), s.sem("copied"), s.sem("squared"), s.sem("summed")
        mm_f, f_st, f_act, f_lin, mm_c, ends = s.sem("mm_f"), s.sem("f_st"), s.sem("f_act"), s.sem("f_lin"), s.sem("mm_c"), s.sem("ends")
        with nc.Block() as block:
            @block.sync
            def _(sp):
                sp.dma_start(wf[:], w_f).then_inc(wf_in, 16)
                sp.dma_start(fb[:], bf_row.partition_broadcast(P)).then_inc(wf_in, 16)
                for n in range(2):
                    sp.dma_start(wq[:, n, :, :], w_qkv[n]).then_inc(w_in[n], 16)
                with sp.Fori(1, CH // 2) as i:
                    for n in range(2):
                        sp.wait_ge(mm, (2 * i + n - 1) * TT)
                        sp.dma_start(wq[:, n, :, :], w_qkv[2 * i + n]).then_inc(w_in[n], 16)

            @block.tensor
            def _(pe):
                pe.wait_ge(wf_in, 32)
                for t in range(TT):
                    for k in range(KT):
                        last = nc.tensor.matmul(pf[:, t, :], lhsT=hT[:, k, t * P:(t + 1) * P], rhs=wf[:, k, :],
                                                start=(k == 0), stop=(k == KT - 1))
                last.then_inc(mm_f, 1)
                with pe.Fori(0, CH // 2) as i:
                    for n in range(2):
                        pe.wait_ge(w_in[n], 16 * i + 16)
                        for t in range(TT):
                            b = t % 4
                            pe.wait_ge(copied, (2 * i + n) * TT + t + 1)
                            for k in range(KT):
                                last = nc.tensor.matmul(pq[:, b, 0:QN], lhsT=hT[:, k, t * P:(t + 1) * P],
                                                        rhs=wq[:, n, k, :], start=(k == 0), stop=(k == KT - 1))
                            last.then_inc(mm, 1)
                pe.wait_ge(f_st, 1)
                for t in range(TT):
                    for j in range(t + 1):
                        last = nc.tensor.matmul(pc[:, t, :], lhsT=(cumul if j == t else ones)[:], rhs=lf[:, 3, j, :],
                                                start=(j == 0), stop=(j == t))
                last.then_inc(mm_c, 1)

            @block.scalar
            def _(act):
                act.wait_ge(f_lin, 3)
                nc.scalar.activation(lf[:, 2, :, :], lf[:, 1, :, :], ACT.Exp).then_inc(f_act, 1)
                act.wait_ge(f_act, 1)
                nc.scalar.activation(lf[:, 1, :, :], lf[:, 2, :, :], ACT.Ln, bias=1.0).then_inc(f_act, 1)
                with act.Fori(0, CH // 2) as i:
                    for n in range(2):
                        for t in range(TT):
                            m = (2 * i + n) * TT + t
                            act.wait_ge(copied, m + 5)
                            act.wait_ge(summed, m + 1)
                            nc.scalar.activation(sq[:, t % 2, :], qkv[:, t, bass.ds((2 * i + n) * QN, QN)],
                                                 ACT.Square).then_inc(squared, 1)

            @block.vector
            def _(dve):
                dve.sem_inc(copied, 4)
                dve.sem_inc(summed, 2)
                dve.wait_ge(mm_f, 1)
                nc.vector.tensor_tensor(lf[:, 0, :, :], pf[:], fb[:].unsqueeze(1).to_broadcast([P, TT, HEADS]),
                                        ALU.add).then_inc(f_lin, 1)
                dve.wait_ge(f_lin, 1)
                nc.vector.tensor_scalar(lf[:, 2, :, :], lf[:, 0, :, :], -1.0, None, ALU.mult).then_inc(f_lin, 1)
                dve.wait_ge(f_lin, 2)
                nc.vector.tensor_tensor(lf[:, 1, :, :], lf[:, 0, :, :], lf[:, 2, :, :], ALU.min).then_inc(f_lin, 1)
                dve.wait_ge(f_act, 2)
                nc.vector.scalar_tensor_tensor(out=lf[:, 3, :, :], in0=lf[:, 0, :, :], scalar=0.0,
                                               in1=lf[:, 1, :, :], op0=ALU.min, op1=ALU.subtract).then_inc(f_st, 1)
                with dve.Fori(0, CH // 2) as i:
                    for n in range(2):
                        for t in range(TT):
                            m = (2 * i + n) * TT + t
                            dve.wait_ge(mm, m + 1)
                            nc.vector.tensor_copy(qkv[:, t, bass.ds((2 * i + n) * QN, QN)],
                                                  pq[:, t % 4, 0:QN]).then_inc(copied, 1)
                            dve.wait_ge(squared, m + 1)
                            nc.vector.tensor_reduce(ss[:, t, bass.ds((2 * i + n) * HPC, HPC)],
                                                    sq[:, t % 2, :].rearrange("p (h d) -> p h d", d=HD),
                                                    AX.X, ALU.add).then_inc(summed, 1)
                dve.wait_ge(copied, CH * TT + 4)
                dve.wait_ge(summed, CH * TT + 2)
                dve.wait_ge(mm_c, 1)
                nc.vector.tensor_scalar(neg_f[:], pc[:], -1.0, None, ALU.mult).then_inc(ends, 1)
                dve.wait_ge(ends, 1)


def stage_attention(nc, qkv, ss, neg_f, qk_gain, o_all, ident, ident16, future16):
    HA = HD + 1
    with Scope(nc, "att") as s:
        norm = s.sb("norm", [P, 3, TT, 2 * HEADS])
        qk = s.sb("qk", [P, 2, TT, HA])
        qkT = s.sb("qkT", [HA, 2, S])
        gain = s.sb("gain", [HA, 2])
        gq = s.sb("gq", [HA, 3])
        prob = s.sb("prob", [P, 2, S])
        pT = s.sb("pT", [P, 4, NB])
        nmax = s.sb("nmax", [P, 2, TT])
        rsum = s.sb("rsum", [P, 2, TT])
        rinv = s.sb("rinv", [P, TT])
        logit = s.ps("logit", [P, 4, NB])
        turn = s.ps("turn", [P, 2, NB])
        po = s.ps("po", [P, TT * HD])
        gain_in, prep, root, set_up = s.sem("gain_in"), s.sem("prep"), s.sem("root"), s.sem("set_up")
        staged, turned, left, scored = s.sem("staged"), s.sem("turned"), s.sem("left"), s.sem("scored")
        qk_left, maxed, exped, ov, o_left, inv = s.sem("qk_left"), s.sem("maxed"), s.sem("exped"), s.sem("ov"), s.sem("o_left"), s.sem("inv")
        ROUNDS = 4 + sum((i + 4) // 4 for i in range(TT))

        def first_round(i):
            return 4 + sum((j + 4) // 4 for j in range(i))

        with nc.Block() as block:
            @block.sync
            def _(sp):
                sp.dma_start(gq[0:HD, 0:2], qk_gain).then_inc(gain_in, 16)

            @block.vector
            def _(dve):
                nc.vector.memset(gq[:, 2:3], HD ** -0.5).then_inc(prep, 1)
                nc.vector.memset(gain[:], 1.0).then_inc(prep, 1)
                nc.vector.tensor_scalar(norm[:, 0, :, :], ss[:, :, 0:2 * HEADS], 1.0 / HD, EPS, ALU.mult,
                                        ALU.add).then_inc(prep, 1)
                dve.wait_ge(gain_in, 16)
                dve.wait_ge(prep, 3)
                nc.vector.scalar_tensor_tensor(out=gain[0:HD, 0:1], in0=gq[0:HD, 0:1], scalar=gq[0:HD, 1:2],
                                               in1=gq[0:HD, 2:3], op0=ALU.mult, op1=ALU.mult).then_inc(set_up, 1)
                dve.wait_ge(root, 1)
                nc.vector.reciprocal(norm[:, 2, :, :], norm[:, 1, :, :]).then_inc(set_up, 1)
                dve.sem_inc(o_left, 1)
                dve.sem_inc(left, 2)
                with dve.Fori(0, HEADS) as h:
                    for r in range(2):
                        dve.wait_ge(turned, h * ROUNDS + r + 2)
                        nc.vector.tensor_copy(qkT[:, 0, r * NB:(r + 1) * NB], turn[0:HA, r % 2, :]).then_inc(left, 1)
                    for r in range(2, 4):
                        dve.wait_ge(turned, h * ROUNDS + r + 2)
                        nc.vector.tensor_scalar(qkT[:, 1, (r - 2) * NB:(r - 1) * NB], turn[0:HA, r % 2, :],
                                                gain[:, 0:1], None, ALU.mult).then_inc(left, 1)

                    def row_max(i):
                        dve.wait_ge(scored, h * TT + i + 1)
                        nc.vector.tensor_reduce(nmax[:, h % 2, i:i + 1],
                                                logit[:, 2 * (i % 2):2 * (i % 2) + 2, :].rearrange("p a b -> p (a b)")[:, 0:(i + 1) * P],
                                                AX.X, ALU.max, negate=True).then_inc(maxed, 1)

                    row_max(0)
                    for i in range(TT):
                        if i + 1 < TT:
                            row_max(i + 1)
                        for r in range((i + 4) // 4):
                            n = first_round(i) + r
                            w = min(4, i + 1 - 4 * r) * P
                            dve.wait_ge(turned, h * ROUNDS + n + 2)
                            nc.vector.tensor_copy(pT[:, n % 4, 0:w], turn[:, n % 2, 0:w]).then_inc(left, 1)
                    dve.wait_ge(exped, (h + 1) * TT + 1)
                    nc.vector.reciprocal(rinv[:], rsum[:, h % 2, :]).then_inc(inv, 1)
                    dve.wait_ge(inv, h + 1)
                    dve.wait_ge(ov, (h + 1) * TT)
                    nc.vector.tensor_tensor(o_all[:, :, bass.ds(h * HD, HD)], po[:].rearrange("p (t d) -> p t d", d=HD),
                                            rinv[:].unsqueeze(2).to_broadcast([P, TT, HD]), ALU.mult).then_inc(o_left, 1)
                dve.wait_ge(o_left, HEADS + 1)

            @block.scalar
            def _(act):
                act.sem_inc(exped, 1)
                act.wait_ge(prep, 3)
                nc.scalar.activation(norm[:, 1, :, :], norm[:, 0, :, :], ACT.Sqrt).then_inc(root, 1)
                with act.Fori(0, HEADS) as h:
                    for i in range(TT):
                        act.wait_ge(maxed, h * TT + i + 1)
                        n = first_round(i - 2) + (i + 2) // 4 if i >= 2 else 0
                        act.wait_ge(turned, h * ROUNDS + n + 1)
                        nc.scalar.activation(prob[:, i % 2, 0:(i + 1) * P],
                                             logit[:, 2 * (i % 2):2 * (i % 2) + 2, :].rearrange("p a b -> p (a b)")[:, 0:(i + 1) * P],
                                             ACT.Exp, bias=nmax[:, h % 2, i:i + 1],
                                             accum_out=rsum[:, h % 2, i:i + 1]).then_inc(exped, 1)

            @block.gpsimd
            def _(pool):
                nc.gpsimd.memset(qk[:], 1.0).then_inc(staged, 1)
                pool.wait_ge(staged, 1)
                pool.wait_ge(set_up, 2)
                pool.sem_inc(qk_left, 1)
                with pool.Fori(0, HEADS) as h:
                    pool.wait_ge(turned, h * ROUNDS + 1)
                    for w in range(2):
                        nc.gpsimd.tensor_tensor(qk[:, w, :, 0:HD], qkv[:, :, bass.ds(w * D + h * HD, HD)],
                                                norm[:, 2, :, bass.ds(w * HEADS + h, 1)].to_broadcast([P, TT, HD]),
                                                ALU.mult).then_inc(staged, 1)
                    nc.gpsimd.tensor_copy(qk[:, 1, :, HD:HA], neg_f[:, :, bass.ds(h, 1)]).then_inc(staged, 1)

            @block.tensor
            def _(pe):
                pe.sem_inc(turned, 1)
                with pe.Fori(0, HEADS) as h:
                    pe.wait_ge(staged, 3 * h + 4)
                    for r in range(4):
                        pe.wait_ge(left, h * ROUNDS + r + 1)
                        for j in range(4):
                            last = nc.tensor.transpose(turn[0:HA, r % 2, j * P:(j + 1) * P],
                                                       qk[:, r // 2, (r % 2) * 4 + j, :], ident[:])
                        last.then_inc(turned, 1)

                    def scores(i):
                        if i == 0:
                            pe.wait_ge(left, h * ROUNDS + 6)
                        if i < 2:
                            pe.wait_ge(exped, h * TT + 1)
                        else:
                            pe.wait_ge(exped, h * TT + i)
                        b = 2 * (i % 2)
                        for c in range((i + 4) // 4):
                            w = min(NB, (i + 1) * P - c * NB)
                            mine = c == i // 4
                            last = nc.tensor.matmul(logit[:, b + c, 0:w], lhsT=qkT[:, 0, i * P:(i + 1) * P],
                                                    rhs=qkT[:, 1, c * NB:c * NB + w], start=True, stop=not mine)
                        at = (i % 4) * P
                        last = nc.tensor.matmul(logit[:, b + i // 4, at:at + P], lhsT=ident16[:], rhs=future16[:],
                                                start=False, stop=True)
                        last.then_inc(scored, 1)

                    scores(0)
                    for i in range(TT):
                        if i + 1 < TT:
                            scores(i + 1)
                        pe.wait_ge(exped, h * TT + i + 2)
                        for r in range((i + 4) // 4):
                            n = first_round(i) + r
                            pe.wait_ge(left, h * ROUNDS + n + 1)
                            for j in range(4 * r, min(4 * r + 4, i + 1)):
                                last = nc.tensor.transpose(turn[:, n % 2, (j % 4) * P:(j % 4 + 1) * P],
                                                           prob[:, i % 2, j * P:(j + 1) * P], ident[:])
                            last.then_inc(turned, 1)
                        if i == 0:
                            pe.wait_ge(o_left, h + 1)
                        for j in range(i + 1):
                            n = first_round(i) + j // 4
                            if j % 4 == 0:
                                pe.wait_ge(left, h * ROUNDS + n + 3)
                            last = nc.tensor.matmul(po[:, i * HD:(i + 1) * HD], lhsT=pT[:, n % 4, (j % 4) * P:(j % 4 + 1) * P],
                                                    rhs=qkv[:, j, bass.ds(2 * D + h * HD, HD)],
                                                    start=(j == 0), stop=(j == i))
                        last.then_inc(ov, 1)


def stage_out(nc, tag, src, w, xres, gate, ident, room):
    with Scope(nc, tag) as s:
        sT = room[:, 0:KT * S].rearrange("p (k t) -> p k t", k=KT)
        ws = room[:, KT * S:2 * KT * S].rearrange("p (n k c) -> p n k c", n=2, k=KT)
        tmp = s.sb("tmp", [P, 2, NB])
        pt = s.ps("pt", [P, 4, NB])
        py = s.ps("py", [P, 4, NB])
        w_in = [s.sem("w_in0"), s.sem("w_in1")]
        turned, taken, mm, gated, added = s.sem("turned"), s.sem("taken"), s.sem("mm"), s.sem("gated"), s.sem("added")
        with nc.Block() as block:
            @block.sync
            def _(sp):
                for n in range(2):
                    sp.dma_start(ws[:, n, :, :], w[n]).then_inc(w_in[n], 16)

            @block.scalar
            def _(act):
                for r in range(2 * KT):
                    act.wait_ge(turned, r + 1)
                    nc.scalar.copy(sT[:, r // 2, (r % 2) * NB:(r % 2 + 1) * NB], pt[:, r % 4, :]).then_inc(taken, 1)

            @block.tensor
            def _(pe):
                for r in range(2 * KT):
                    if r >= 4:
                        pe.wait_ge(taken, r - 3)
                    for j in range(4):
                        last = nc.tensor.transpose(pt[:, r % 4, j * P:(j + 1) * P],
                                                   src[:, 4 * (r % 2) + j, (r // 2) * P:(r // 2 + 1) * P], ident[:])
                    last.then_inc(turned, 1)
                pe.wait_ge(taken, 2 * KT)
                for n in range(2):
                    pe.wait_ge(w_in[n], 16)
                    for t in range(TT):
                        m = n * TT + t
                        if m >= 4:
                            pe.wait_ge(gated, m - 3)
                        for k in range(KT):
                            last = nc.tensor.matmul(py[:, m % 4, :], lhsT=sT[:, k, t * P:(t + 1) * P],
                                                    rhs=ws[:, n, k, :], start=(k == 0), stop=(k == KT - 1))
                        last.then_inc(mm, 1)

            @block.vector
            def _(dve):
                for n in range(2):
                    for t in range(TT):
                        m = n * TT + t
                        dve.wait_ge(mm, m + 1)
                        if m >= 2:
                            dve.wait_ge(added, m - 1)
                        cs = slice(n * NB, (n + 1) * NB)
                        nc.vector.tensor_tensor(tmp[:, m % 2, :], py[:, m % 4, :], gate[:, cs], ALU.mult).then_inc(gated, 1)
                        dve.wait_ge(gated, m + 1)
                        nc.vector.tensor_tensor(xres[:, t, cs], xres[:, t, cs], tmp[:, m % 2, :], ALU.add).then_inc(added, 1)
                dve.wait_ge(added, 2 * TT)


def stage_mlp(nc, hT, w1, w2, xres, gate, ident):
    with Scope(nc, "mlp") as s:
        hid = s.sb("hid", [P, FT, NB])
        w1s = s.sb("w1s", [P, 4, KT, P])
        w2s = s.sb("w2s", [P, 4, D])
        rel = s.sb("rel", [P, 2, NB])
        yT = s.sb("yT", [P, KT, NB])
        tmp = s.sb("tmp", [P, 2, NB])
        ps = s.ps("ps", [P, 8, NB])
        w1_in = [s.sem(f"w1_in{n}") for n in range(4)]
        w2_in = [s.sem(f"w2_in{n}") for n in range(4)]
        up, down, relu, squared, y_left = s.sem("up"), s.sem("down"), s.sem("relu"), s.sem("squared"), s.sem("y_left")
        turned, gated, added = s.sem("turned"), s.sem("gated"), s.sem("added")
        with nc.Block() as block:
            @block.sync
            def _(sp):
                sp.sem_inc(up, 4)
                sp.sem_inc(down, 4)
                for half in range(2):
                    with sp.Fori(0, FT // 4) as g:
                        for n in range(4):
                            sp.wait_ge(up, half * FT + 4 * g + n + 1)
                            sp.dma_start(w1s[:, n, :, :], w1[4 * g + n]).then_inc(w1_in[n], 16)
                    with sp.Fori(0, FT // 4) as g:
                        for n in range(4):
                            sp.wait_ge(down, half * FT + 4 * g + n + 1)
                            sp.dma_start(w2s[:, n, :], w2[4 * g + n]).then_inc(w2_in[n], 16)

            @block.tensor
            def _(pe):
                for half in range(2):
                    if half:
                        pe.wait_ge(gated, 8)
                    with pe.Fori(0, FT // 4) as g:
                        for n in range(4):
                            m = half * FT + 4 * g + n
                            pe.wait_ge(w1_in[n], 16 * (half * (FT // 4) + g + 1))
                            pe.wait_ge(relu, m + 1)
                            for k in range(KT):
                                last = nc.tensor.matmul(ps[:, n, :], lhsT=w1s[:, n, k, :],
                                                        rhs=hT[:, k, half * NB:(half + 1) * NB],
                                                        start=(k == 0), stop=(k == KT - 1))
                            last.then_inc(up, 1)
                    pe.wait_ge(relu, (half + 1) * FT + 4)

                    def down_group(g, first, end):
                        for n in range(4):
                            pe.wait_ge(squared, half * FT + 4 * g + n + 3)
                            pe.wait_ge(w2_in[n], 16 * (half * (FT // 4) + g + 1))
                            for c in range(KT):
                                last = nc.tensor.matmul(ps[:, c, :], lhsT=w2s[:, n, c * P:(c + 1) * P],
                                                        rhs=hid[:, 4 * g + n, :], start=first and n == 0,
                                                        stop=end and n == 3)
                            last.then_inc(down, 1)

                    down_group(0, True, False)
                    with pe.Fori(1, FT // 4 - 1) as g:
                        down_group(g, False, False)
                    down_group(FT // 4 - 1, False, True)
                    pe.wait_ge(y_left, 8 * (half + 1))
                    for r in range(8):
                        t, c0 = r // 2, 4 * (r % 2)
                        for j in range(4):
                            last = nc.tensor.transpose(ps[:, r, j * P:(j + 1) * P], yT[:, c0 + j, t * P:(t + 1) * P],
                                                       ident[:])
                        last.then_inc(turned, 1)

            @block.scalar
            def _(act):
                act.sem_inc(relu, 4)
                for half in range(2):
                    with act.Fori(0, FT // 4) as g:
                        for n in range(4):
                            m = half * FT + 4 * g + n
                            act.wait_ge(up, m + 5)
                            act.wait_ge(squared, m + 1)
                            nc.scalar.activation(rel[:, n % 2, :], ps[:, n, :], ACT.Relu).then_inc(relu, 1)
                    act.wait_ge(down, (half + 1) * FT + 4)
                    if half:
                        act.wait_ge(turned, 8)
                    for c in range(KT):
                        nc.scalar.copy(yT[:, c, :], ps[:, c, :]).then_inc(y_left, 1)

            @block.vector
            def _(dve):
                dve.sem_inc(squared, 2)
                for half in range(2):
                    if half:
                        dve.wait_ge(down, FT + 4)
                    with dve.Fori(0, FT // 4) as g:
                        for n in range(4):
                            m = half * FT + 4 * g + n
                            dve.wait_ge(relu, m + 5)
                            nc.vector.tensor_tensor(hid[:, bass.ds(4 * g + n, 1), :], rel[:, n % 2:n % 2 + 1, :],
                                                    rel[:, n % 2:n % 2 + 1, :], ALU.mult).then_inc(squared, 1)
                    for r in range(8):
                        m = half * 8 + r
                        t, cs = half * 4 + r // 2, slice((r % 2) * NB, (r % 2 + 1) * NB)
                        dve.wait_ge(turned, m + 1)
                        if m >= 2:
                            dve.wait_ge(added, m - 1)
                        nc.vector.tensor_tensor(tmp[:, m % 2, :], ps[:, r, :], gate[:, cs], ALU.mult).then_inc(gated, 1)
                        dve.wait_ge(gated, m + 1)
                        nc.vector.tensor_tensor(xres[:, t, cs], xres[:, t, cs], tmp[:, m % 2, :],
                                                ALU.add).then_inc(added, 1)
                dve.wait_ge(added, 16)


PAIRS = 6
HS = 64
NPAR = 10
MU_R, MU_K, MU_V, W0, A0, K_K, K_A, R_K, LNX_G, LNX_B = range(NPAR)
WIN = 128
WPAIRS = S // WIN // 2
LEVELS = 7
LN_EPS = 1e-5
LNX_EPS = 64e-5
ALPHA = 2.0 ** 0.25
DECAY = -0.6065306597126334


class Steps:

    def __init__(self, sem, names):
        self.sem, self.names = sem, names.split()

    def at(self, i, name):
        return i * len(self.names) + self.names.index(name) + 1


def stage_turn(nc, tag, src, dst, ident):
    with Scope(nc, tag) as s:
        pt = s.ps("pt", [P, 8, NB])
        turned, taken = s.sem("turned"), s.sem("taken")
        with nc.Block() as block:
            @block.tensor
            def _(pe):
                for r in range(2 * KT):
                    if r >= 8:
                        pe.wait_ge(taken, r - 7)
                    for j in range(4):
                        last = nc.tensor.transpose(pt[:, r % 8, j * P:(j + 1) * P],
                                                   src[:, 4 * (r % 2) + j, (r // 2) * P:(r // 2 + 1) * P], ident[:])
                    last.then_inc(turned, 1)

            @block.vector
            def _(dve):
                for r in range(2 * KT):
                    dve.wait_ge(turned, r + 1)
                    nc.vector.tensor_copy(dst[:, r // 2, (r % 2) * NB:(r % 2 + 1) * NB],
                                          pt[:, r % 8, :]).then_inc(taken, 1)
                dve.wait_ge(taken, 2 * KT)


def stage_pool(nc, xT, w_head, head_cols, pool_w, inv_count, mixT, lora_in):
    PAD = 16
    with Scope(nc, "pool") as s:
        ws = s.sb("ws", [P, 4, KT, P])
        hc = s.sb("hc", [P, 6])
        pw = s.sb("pw", [P, 2, P])
        ic = s.sb("ic", [P, 2, PAD])
        z = s.sb("z", [P, 4, PAD + S])
        acc = s.sb("acc", [P, 2, PAD + S])
        dif = s.sb("dif", [P, 2, S])
        ps = s.ps("ps", [P, 8, NB])
        w_in, c_in, mm, copied, cleared = s.sem("w_in"), s.sem("c_in"), s.sem("mm"), s.sem("copied"), s.sem("cleared")
        v, mapped, ends = s.sem("vector_step"), s.sem("mapped"), s.sem("ends")
        with nc.Block() as block:
            @block.sync
            def _(sp):
                sp.dma_start(ws[:], w_head).then_inc(w_in, 16)
                sp.dma_start(hc[:], head_cols).then_inc(c_in, 16)
                sp.dma_start(pw[:], pool_w).then_inc(c_in, 16)
                sp.dma_start(ic[:], inv_count).then_inc(c_in, 16)

            @block.tensor
            def _(pe):
                pe.wait_ge(w_in, 16)
                for n in range(4):
                    for half in range(2):
                        for k in range(KT):
                            last = nc.tensor.matmul(ps[:, 2 * n + half, :], lhsT=ws[:, n, k, :],
                                                    rhs=xT[:, k, half * NB:(half + 1) * NB],
                                                    start=(k == 0), stop=(k == KT - 1))
                    last.then_inc(mm, 1)
                pe.wait_ge(copied, 4)
                pe.wait_ge(c_in, 48)
                for n in range(2):
                    pe.wait_ge(mapped, n + 1)
                    for half in range(2):
                        last = nc.tensor.matmul(ps[:, 2 * n + half, :], lhsT=pw[:, n, :],
                                                rhs=dif[:, n, half * NB:(half + 1) * NB], start=True, stop=True)
                    last.then_inc(mm, 1)

            @block.scalar
            def _(act):
                for n in range(4):
                    act.wait_ge(mm, n + 1)
                    nc.scalar.copy(z[:, n, PAD:], ps[:, 2 * n:2 * n + 2, :].rearrange("p a b -> p (a b)")).then_inc(copied, 1)
                act.wait_ge(v, 4)
                nc.scalar.activation(lora_in[0:HS, 0, :], lora_in[0:HS, 0, :], ACT.Tanh).then_inc(ends, 1)
                nc.scalar.activation(lora_in[:, 1, :], lora_in[:, 1, :], ACT.Sigmoid).then_inc(ends, 1)
                act.wait_ge(ends, 2)

            @block.vector
            def _(dve):
                step = [0]

                def done(ins):
                    step[0] += 1
                    ins.then_inc(v, 1)
                    dve.wait_ge(v, step[0])

                nc.vector.memset(z[:, :, 0:PAD], 0.0).then_inc(cleared, 1)
                nc.vector.memset(acc[:, :, 0:PAD], 0.0).then_inc(cleared, 1)
                dve.wait_ge(cleared, 2)
                dve.wait_ge(c_in, 48)
                dve.wait_ge(copied, 4)
                for n in range(2):
                    cur = z[:, 2 + n, PAD:]
                    done(nc.vector.tensor_tensor(dif[:, 0, :], z[:, 2 + n, PAD - 1:PAD - 1 + S], cur, ALU.subtract))
                    done(nc.vector.scalar_tensor_tensor(out=lora_in[:, n, :], in0=dif[:, 0, :], scalar=hc[:, n:n + 1],
                                                        in1=cur, op0=ALU.mult, op1=ALU.add))
                for n in range(2):
                    src, dst, lag = z[:, n, :], acc[:, 0, :], 1
                    for level in range(1 + 2 * n):
                        done(nc.vector.tensor_tensor(dst[:, PAD:], src[:, PAD:], src[:, PAD - lag:PAD - lag + S], ALU.add))
                        src, dst, lag = dst, acc[:, (level + 1) % 2, :], 2 * lag
                    done(nc.vector.tensor_tensor(dst[HS:P, PAD:], src[HS:P, PAD:], src[HS:P, PAD - lag:PAD - lag + S], ALU.add))
                    done(nc.vector.tensor_copy(dst[0:HS, PAD:], src[0:HS, PAD:]))
                    done(nc.vector.tensor_tensor(src[:, PAD:2 * PAD], dst[:, PAD:2 * PAD], ic[:, n, :], ALU.mult))
                    done(nc.vector.tensor_tensor(dif[:, n, 0:PAD], src[:, PAD:2 * PAD], z[:, n, PAD:2 * PAD], ALU.subtract))
                    nc.vector.scalar_tensor_tensor(out=dif[:, n, PAD:], in0=dst[:, 2 * PAD:], scalar=hc[:, 4 + n:5 + n],
                                                   in1=z[:, n, 2 * PAD:], op0=ALU.mult, op1=ALU.subtract).then_inc(mapped, 1)
                    dve.wait_ge(mapped, n + 1)
                for n in range(2):
                    dve.wait_ge(mm, 5 + n)
                    done(nc.vector.tensor_scalar(mixT[:, n, :], ps[:, 2 * n:2 * n + 2, :].rearrange("p a b -> p (a b)"),
                                                 hc[:, 2 + n:3 + n], None, ALU.mult))


def stage_rwkv(nc, xT, w_rkv, lora_up, unit_cols, consts, scan_keep, lora_in, mixT, ident):
    UT = 2 * WIN
    UNITS = PAIRS * WPAIRS
    TOP = LEVELS - 1
    with Scope(nc, "rwkv") as s:
        ws = s.sb("ws", [P, 3, KT, P])
        up = s.sb("up", [P, 3, P])
        par_all = s.sb("par_all", [P, UNITS * NPAR])
        par = s.sb("par", [P, NPAR + 1])
        par_y = s.sb("par_y", [P, 2])
        cst = s.sb("cst", [P, 4 + LEVELS + 2, P])
        causal = cst[:, 0:4, :].rearrange("p a b -> p (a b)")
        level = [cst[:, 4 + n, :] for n in range(LEVELS)]
        head_sum, head_mean = cst[:, 4 + LEVELS, :], cst[:, 5 + LEVELS, :]
        keep = s.sb("keep", [P, UT])
        Z = s.sb("Z", [P, 3, UT + 1])
        rkv = s.sb("rkv", [P, 3, UT])
        R, K, V = (rkv[:, n, :] for n in range(3))
        T0, LW, L, LM, SA, AG, RK, BON, KK, SQ, NR, EP, EN, EX, Y, YC, YS = (
            s.sb(n, [P, UT]) for n in "T0 LW L LM SA AG RK BON KK SQ NR EP EN EX Y YC YS".split())
        ends = s.sb("ends", [P, 3])
        fac_log = s.sb("fac_log", [P, 2])
        fac_exp = s.sb("fac_exp", [P, 2])
        fac_in = s.sb("fac_in", [P, 1])
        AR = s.sb("AR", [P, 2, 2, WIN])
        KB = s.sb("KB", [P, 2, 2, WIN])
        tm = s.sb("tm", [P, 2, 4, P])
        GM = s.sb("GM", [P, 4, 4, WIN])
        ML = s.sb("ML", [P, 3, 4, WIN])
        TI = s.sb("TI", [P, 4, WIN])
        TX = s.sb("TX", [P, 4, WIN])
        XS = s.sb("XS", [P, 4, WIN])
        AW = s.sb("AW", [P, 4, 2, HS])
        GH = s.sb("GH", [P, 4, 2, HS])
        QT = s.sb("QT", [P, 2, WIN])
        ZT = s.sb("ZT", [P, 2, HS])
        ST = s.sb("ST", [P, 2, HS])
        STF = s.sb("STF", [P, HS])
        ps = s.ps("ps", [P, 8, NB])
        mix_flat = mixT[:].rearrange("p k t -> p (k t)")

        w_in = [s.sem("w_in_r"), s.sem("w_in_k"), s.sem("w_in_v")]
        up_in, c_in, cleared, zeroed = s.sem("up_in"), s.sem("c_in"), s.sem("cleared"), s.sem("zeroed")
        passed, state_here = s.sem("passed"), s.sem("state_here")
        pe_a = Steps(s.sem("pe_make"), "w a k r kk_sum v g")
        act_a = Steps(s.sem("act_make"), "w a k kk_sq ep en r ex fac root v g")
        dve_a = Steps(s.sem("dve_make"), "par one_ka lw scan k_d k kk lm lx ends fac ends_on ag k2 sq_max r_d r inv kkn b A B K "
                      "v_d v carry rk R rk2 fac_in")
        pe_w = Steps(s.sem("pe_win"), "turn0 turn1 gram0 gram1 gram2 gram3 ak_v ti0 " +
                     " ".join(f"x{l}{' bonus' if l == 5 else ''} t{l} u{l}" for l in range(1, TOP)) + f" x{TOP} u{TOP} gh q z e0 y0 e1 y1")
        act_w = Steps(s.sem("act_win"), "tm0 tm1 a_tm w_tm ti0 " + " ".join(f"x{l}" for l in range(1, LEVELS)) + " gh z y0 y1")
        dve_w = Steps(s.sem("dve_win"), "gm0 gm1 gm2 gm3 ab0 tx0 " + " ".join(f"ti{l} tx{l}" for l in range(1, TOP)) +
                      f" bon tx{TOP} stf0 q st0 stf1 st1")
        pool_w = Steps(s.sem("pool_win"), " ".join(f"m{l}" for l in range(1, LEVELS)))
        pe_y = Steps(s.sem("pe_norm"), "mean var")
        act_y = Steps(s.sem("act_norm"), "y_sq y_root")
        dve_y = Steps(s.sem("dve_norm"), "y_c y_par y_eps y_inv y_n y_gb y_b y_out")

        def four():
            return [(2 * w + h, w, h) for w in range(2) for h in range(2)]

        def wait(eng, steps, unit, name):
            if not (isinstance(unit, int) and unit < 0):
                eng.wait_ge(steps.sem, steps.at(unit, name))

        def each_unit(eng, body):
            def one(p, wp, prev=True, nxt=True):
                last = isinstance(wp, int) and wp == WPAIRS - 1
                body(p * WPAIRS + wp, 0 if last else (wp + 1) * UT, p + 1 if last and nxt else None, prev, True, nxt)

            body(-1, 0, 0, False, False, True)
            one(0, 0, prev=False)
            with eng.Fori(1, WPAIRS - 1) as wp:
                one(0, wp)
            one(0, WPAIRS - 1)
            with eng.Fori(1, PAIRS - 1) as p:
                with eng.Fori(0, WPAIRS - 1) as wp:
                    one(p, wp)
                one(p, WPAIRS - 1)
            with eng.Fori(0, WPAIRS - 1) as wp:
                one(PAIRS - 1, wp)
            one(PAIRS - 1, WPAIRS - 1, nxt=False)
            body(UNITS, 0, None, True, False, False)

        with nc.Block() as block:
            @block.sync
            def _(sp):
                sp.dma_start(par_all[:], unit_cols).then_inc(c_in, 16)
                sp.dma_start(up[:], lora_up[0]).then_inc(up_in, 16)
                for n in (1, 0, 2):
                    sp.dma_start(ws[:, n, :, :], w_rkv[0][:, n, :, :]).then_inc(w_in[n], 16)
                sp.dma_start(cst[:], consts).then_inc(c_in, 16)
                sp.dma_start(keep[:], scan_keep).then_inc(c_in, 16)
                with sp.Fori(1, PAIRS) as p:
                    for n in (1, 0, 2):
                        sp.wait_ge(pe_a.sem, pe_a.at((p - 1) * WPAIRS + WPAIRS - 1, "rkv"[n]))
                        sp.sem_inc(passed, 1)
                        sp.dma_start(ws[:, n, :, :], w_rkv[p][:, n, :, :]).then_inc(w_in[n], 16)
                    sp.wait_ge(pe_a.sem, pe_a.at((p - 1) * WPAIRS + WPAIRS - 1, "g"))
                    sp.sem_inc(passed, 1)
                    sp.dma_start(up[:], lora_up[p]).then_inc(up_in, 16)

            @block.tensor
            def _(pe):
                A_BANK, B_BANK = 6, 7

                def body(q, col, new_pair, prev, win, nxt):
                    u, y = q + 1, q - 1

                    def project(n, ks, bank):
                        if not nxt:
                            return
                        if new_pair is not None and 0 in ks:
                            pe.wait_ge(w_in[n], 16 * new_pair + 16)
                        for k in ks:
                            last = nc.tensor.matmul(ps[:, bank, 0:UT], lhsT=ws[:, n, k, :], rhs=xT[:, k, bass.ds(col, UT)],
                                                    start=(k == 0), stop=(k == KT - 1))
                        if KT - 1 in ks:
                            last.then_inc(pe_a.sem, 1)

                    def turn_units():
                        wait(pe, dve_a, q, "R")
                        wait(pe, dve_w, y, "st1")
                        wait(pe, act_w, y, "y1")
                        for w in range(2):
                            for n, src in enumerate((AR[:, w, 0, :], KB[:, w, 1, :], KB[:, w, 0, :],
                                                     V[:, w * WIN:(w + 1) * WIN])):
                                last = nc.tensor.transpose(ps[:, w, n * P:(n + 1) * P], src, ident[:])
                            last.then_inc(pe_w.sem, 1)

                    if win:
                        turn_units()
                        for i, w, h in four():
                            hp = slice(h * HS, (h + 1) * HS)
                            both = AR[hp, w, :, :].rearrange("p a b -> p (a b)")
                            nc.tensor.matmul(ps[:, 2 + i, 0:2 * WIN], lhsT=KB[hp, w, 1, :], rhs=both, start=True, stop=True)
                            nc.tensor.matmul(ps[:, 2 + i, 2 * WIN:4 * WIN], lhsT=KB[hp, w, 0, :], rhs=both,
                                             start=True, stop=True).then_inc(pe_w.sem, 1)
                    if prev:
                        wait(pe, act_w, y, "y1")
                        wait(pe, act_a, q if win else q - 1, "v")
                        nc.tensor.matmul(ps[:, A_BANK, 0:UT], lhsT=head_mean, rhs=Y[:], start=True,
                                         stop=True).then_inc(pe_y.sem, 1)
                    if nxt:
                        if new_pair is not None:
                            pe.wait_ge(up_in, 16 * new_pair + 16)
                        wait(pe, act_a, u - 1, "g")
                        nc.tensor.matmul(ps[:, B_BANK, 0:UT], lhsT=up[:, 0, :], rhs=lora_in[:, 0, bass.ds(col, UT)],
                                         start=True, stop=True).then_inc(pe_a.sem, 1)
                        if prev:
                            wait(pe, dve_y, y, "y_c")
                        else:
                            wait(pe, act_a, u - 1, "v")
                        nc.tensor.matmul(ps[:, A_BANK, 0:UT], lhsT=up[:, 1, :], rhs=lora_in[:, 0, bass.ds(col, UT)],
                                         start=True, stop=True).then_inc(pe_a.sem, 1)
                    if win:
                        wait(pe, act_w, q, "a_tm")
                        wait(pe, dve_w, q, "gm3")
                        for i, w, h in four():
                            last = nc.tensor.matmul(ps[:, 0, i * HS:(i + 1) * HS], lhsT=GM[:, i, 2, :],
                                                    rhs=tm[:, w, 3, h * HS:(h + 1) * HS], start=True, stop=True)
                        last.then_inc(pe_w.sem, 1)
                    if nxt:
                        wait(pe, act_a, u, "w")
                        project(1, range(0, 4), B_BANK)
                    if win:
                        wait(pe, dve_w, q, "tx0")
                        for i in range(4):
                            last = nc.tensor.transpose(ps[:, 1, i * P:(i + 1) * P], TX[:, i, :], ident[:])
                        last.then_inc(pe_w.sem, 1)
                    project(1, range(4, 6), B_BANK)

                    def while_x(l):
                        if l == 1:
                            project(1, range(6, 8), B_BANK)
                        if l == 2:
                            if prev:
                                wait(pe, act_y, y, "y_sq")
                                if nxt:
                                    wait(pe, act_a, u, "a")
                                else:
                                    wait(pe, dve_y, y, "y_c")
                                nc.tensor.matmul(ps[:, A_BANK, 0:UT], lhsT=head_mean, rhs=YS[:], start=True,
                                                 stop=True).then_inc(pe_y.sem, 1)
                            if nxt:
                                wait(pe, act_a, u, "k")
                                project(0, range(0, 2), B_BANK)
                        if l == 3:
                            project(0, range(2, 5), B_BANK)
                        if l == 4:
                            project(0, range(5, 8), B_BANK)
                        if l == 5:
                            if win:
                                if nxt:
                                    wait(pe, act_a, u, "r")
                                else:
                                    wait(pe, act_a, q, "g")
                                wait(pe, dve_a, q, "rk2")
                                nc.tensor.matmul(ps[:, B_BANK, 0:UT], lhsT=head_sum, rhs=RK[:], start=True,
                                                 stop=True).then_inc(pe_w.sem, 1)
                            if nxt:
                                wait(pe, dve_a, u, "sq_max")
                                project(2, range(0, 2), A_BANK)
                        if l == 6:
                            project(2, range(2, 5), A_BANK)

                    def while_t(l):
                        if l == 4 and nxt:
                            wait(pe, act_a, u, "kk_sq")
                            if prev:
                                wait(pe, dve_y, y, "y_eps")
                            else:
                                wait(pe, act_a, u, "a")
                            nc.tensor.matmul(ps[:, A_BANK, 0:UT], lhsT=head_sum, rhs=SQ[:], start=True,
                                             stop=True).then_inc(pe_a.sem, 1)
                        if l == 6:
                            project(2, range(5, 8), A_BANK)

                    for l in range(1, LEVELS):
                        if win:
                            wait(pe, pool_w, q, f"m{l}")
                            if l == 1:
                                wait(pe, act_w, q, "ti0")
                            else:
                                wait(pe, dve_w, q, f"ti{l - 1}")
                            for i in range(4):
                                last = nc.tensor.matmul(ps[:, 2, i * P:(i + 1) * P], lhsT=ML[:, l % 3, i, :], rhs=TI[:, i, :],
                                                        start=True, stop=True)
                            last.then_inc(pe_w.sem, 1)
                        while_x(l)
                        if win:
                            wait(pe, act_w, q, f"x{l}")
                            wait(pe, dve_w, q, f"tx{l - 1}")
                            if l < TOP:
                                for i in range(4):
                                    last = nc.tensor.matmul(ps[:, 3, i * P:(i + 1) * P], lhsT=TX[:, i, :], rhs=XS[:, i, :],
                                                            start=True, stop=True)
                                last.then_inc(pe_w.sem, 1)
                            for i in range(4):
                                last = nc.tensor.matmul(ps[:, 4, i * P:(i + 1) * P], lhsT=XS[:, i, :], rhs=TX[:, i, :],
                                                        start=True, stop=True)
                            last.then_inc(pe_w.sem, 1)
                        while_t(l)
                    if win:
                        wait(pe, dve_w, q, f"tx{TOP}")
                        wait(pe, act_w, q, "w_tm")
                        for i in range(4):
                            last = nc.tensor.matmul(ps[:, 5, i * P:(i + 1) * P], lhsT=TX[:, i, :],
                                                    rhs=AW[:, i, :, :].rearrange("p a b -> p (a b)"), start=True, stop=True)
                        last.then_inc(pe_w.sem, 1)
                    if nxt:
                        if win:
                            wait(pe, dve_w, q, "bon")
                        else:
                            wait(pe, act_a, u, "r")
                        nc.tensor.matmul(ps[:, B_BANK, 0:UT], lhsT=up[:, 2, :], rhs=lora_in[:, 1, bass.ds(col, UT)],
                                         start=True, stop=True).then_inc(pe_a.sem, 1)
                    if win:
                        wait(pe, act_w, q, "gh")
                        for i, w, h in four():
                            last = nc.tensor.matmul(ps[h * HS:(h + 1) * HS, 2, w * WIN:(w + 1) * WIN], lhsT=GH[:, i, 0, :],
                                                    rhs=GM[:, i, 1, :], start=True, stop=True)
                        last.then_inc(pe_w.sem, 1)
                        for i, w, h in four():
                            last = nc.tensor.matmul(ps[h * HS:(h + 1) * HS, 3, w * HS:(w + 1) * HS], lhsT=GH[:, i, 0, :],
                                                    rhs=tm[:, w, 1, h * HS:(h + 1) * HS], start=True, stop=True)
                        last.then_inc(pe_w.sem, 1)
                        for w in range(2):
                            e_out = [ps[h * HS:(h + 1) * HS, 4 * w, 0:HS] for h in range(2)]
                            y_out = [ps[h * HS:(h + 1) * HS, 4 * w + 1, 0:WIN] for h in range(2)]

                            def stateless(h):
                                i, hp = 2 * w + h, slice(h * HS, (h + 1) * HS)
                                nc.tensor.matmul(e_out[h], lhsT=tm[:, w, 1, hp], rhs=GH[:, i, 1, :], start=True, stop=False)
                                nc.tensor.matmul(e_out[h], lhsT=tm[:, w, 2, hp], rhs=tm[:, w, 3, hp], start=False, stop=False)
                                nc.tensor.matmul(y_out[h], lhsT=GH[:, i, 1, :], rhs=GM[:, i, 1, :], start=True, stop=False)
                                nc.tensor.matmul(y_out[h], lhsT=tm[:, w, 3, hp], rhs=GM[:, i, 3, :], start=False, stop=False)

                            for h in range(2):
                                stateless(h)
                            if w == 0:
                                wait(pe, act_w, q, "z")
                                wait(pe, dve_w, y, "st1")
                            else:
                                wait(pe, dve_w, q, "st0")
                            pe.sem_inc(state_here, 1)
                            for h in range(2):
                                hp = slice(h * HS, (h + 1) * HS)
                                last = nc.tensor.matmul(e_out[h], lhsT=ZT[hp, w, :], rhs=ST[hp, w, :], start=False, stop=True)
                            last.then_inc(pe_w.sem, 1)
                            if w == 0:
                                wait(pe, dve_w, q, "q")
                                pe.sem_inc(state_here, 1)
                            for h in range(2):
                                hp = slice(h * HS, (h + 1) * HS)
                                last = nc.tensor.matmul(y_out[h], lhsT=ST[hp, w, :], rhs=QT[hp, w, :], start=False, stop=True)
                            last.then_inc(pe_w.sem, 1)

                pe.wait_ge(c_in, 48)
                pe.wait_ge(cleared, 3)
                each_unit(pe, body)

            @block.scalar
            def _(act):
                def body(q, col, new_pair, prev, win, nxt):
                    u, y = q + 1, q - 1

                    def make(*args, **kw):
                        if nxt:
                            nc.scalar.activation(*args, **kw).then_inc(act_a.sem, 1)

                    def copy(steps, dst, src):
                        nc.scalar.copy(dst, src).then_inc(steps.sem, 1)

                    def bank(b):
                        return ps[:, b, 0:UT]

                    def x_out(l):
                        if win:
                            wait(act, pe_w, q, f"x{l}")
                            copy(act_w, XS[:].rearrange("p u t -> p (u t)"), ps[:, 2, :])

                    if win:
                        for w in range(2):
                            wait(act, pe_w, q, f"turn{w}")
                            copy(act_w, tm[:, w, :, :], ps[:, w, :].rearrange("p (a b) -> p a b", a=4))
                        wait(act, act_w, q, "tm1")
                        copy(act_w, AW[:, :, 0, :].rearrange("p (w h) d -> p w h d", w=2),
                             tm[:, :, 0, :].rearrange("p w (h d) -> p w h d", h=2))
                    if nxt:
                        wait(act, dve_a, u, "par")
                        wait(act, pe_a, u, "w")
                        make(LW[:], bank(7), ACT.Sigmoid, bias=par[:, W0:W0 + 1])
                        wait(act, pe_a, u, "a")
                        make(SA[:], bank(6), ACT.Sigmoid, bias=par[:, A0:A0 + 1])
                    if win:
                        wait(act, pe_w, q, "ak_v")
                        copy(act_w, AW[:, :, 1, :], ps[:, 0, 0:4 * HS].rearrange("p (u d) -> p u d", u=4))
                        wait(act, pe_w, q, "ti0")
                        copy(act_w, TI[:].rearrange("p u t -> p (u t)"), ps[:, 1, :])
                    x_out(1)
                    if nxt:
                        wait(act, pe_a, u, "k")
                        wait(act, dve_a, u - 1, "carry")
                        copy(act_a, Z[:, 1, 1:], bank(7))
                    if prev:
                        wait(act, dve_y, y, "y_c")
                        nc.scalar.activation(YS[:], YC[:], ACT.Square).then_inc(act_y.sem, 1)
                    x_out(2)
                    x_out(3)
                    if prev:
                        wait(act, dve_y, y, "y_eps")
                        nc.scalar.activation(YS[:], YS[:], ACT.Sqrt).then_inc(act_y.sem, 1)
                    if nxt:
                        wait(act, dve_a, u, "kk")
                        make(SQ[:], KK[:], ACT.Square)
                    x_out(4)
                    if nxt:
                        wait(act, dve_a, u, "lx")
                        make(EP[:], LM[:], ACT.Exp)
                        make(EN[:], LM[:], ACT.Exp, scale=-1.0)
                        wait(act, pe_a, u, "r")
                        copy(act_a, Z[:, 0, 1:], bank(7))
                    x_out(5)
                    if nxt:
                        make(EX[:], EX[:], ACT.Exp)
                        wait(act, dve_a, u, "fac")
                        make(fac_exp[:], fac_log[:], ACT.Exp)
                        wait(act, dve_a, u, "sq_max")
                        make(NR[:], NR[:], ACT.Sqrt)
                    x_out(6)
                    if nxt:
                        wait(act, pe_a, u, "v")
                        copy(act_a, Z[:, 2, 1:], bank(6))
                    if win:
                        wait(act, pe_w, q, "gh")
                        copy(act_w, GH[:].rearrange("p u a d -> p (u a d)"), ps[:, 5, :])
                    if nxt:
                        wait(act, pe_a, u, "g")
                        copy(act_a, mix_flat[:, bass.ds(2 * S + u * UT, UT)], bank(7))
                    if win:
                        wait(act, pe_w, q, "z")
                        copy(act_w, ZT[:].rearrange("p w d -> p (w d)"), ps[:, 3, 0:2 * HS])
                        for w in range(2):
                            wait(act, pe_w, q, f"y{w}")
                            if prev:
                                wait(act, dve_y, y, "y_c")
                            copy(act_w, Y[:, w * WIN:(w + 1) * WIN], ps[:, 4 * w + 1, 0:WIN])

                each_unit(act, body)

            @block.gpsimd
            def _(pool):
                pool.wait_ge(c_in, 48)
                with pool.Fori(0, UNITS) as q:
                    for l in range(1, LEVELS):
                        if l == 1:
                            pool.wait_ge(dve_w.sem, dve_w.at(q, "gm3"))
                        if l > 3:
                            pool.wait_ge(pe_w.sem, pe_w.at(q, f"x{l - 3}"))
                        nc.gpsimd.tensor_tensor(ML[:, l % 3, :, :], GM[:, :, 0, :],
                                                level[l].unsqueeze(1).to_broadcast([P, 4, WIN]), ALU.mult).then_inc(pool_w.sem, 1)

            @block.vector
            def _(dve):
                tt, ts, stt = nc.vector.tensor_tensor, nc.vector.tensor_scalar, nc.vector.scalar_tensor_tensor
                copy, rec = nc.vector.tensor_copy, nc.vector.reciprocal

                def windows(a):
                    return a[:].rearrange("p (w t) -> p w t", w=2)

                def col_of(n):
                    return par[:, n:n + 1]

                def body(q, col, new_pair, prev, win, nxt):
                    u, y = q + 1, q - 1

                    def make(need, ins_of, *args, **kw):
                        if nxt:
                            if need:
                                wait(dve, dve_a, u, need)
                            ins_of(*args, **kw).then_inc(dve_a.sem, 1)

                    def norm(need, ins_of, *args, **kw):
                        if prev:
                            if need:
                                wait(dve, dve_y, y, need)
                            ins_of(*args, **kw).then_inc(dve_y.sem, 1)

                    def window(need, ins_of, *args, **kw):
                        if win:
                            if need:
                                wait(dve, dve_w, q, need)
                            ins_of(*args, **kw).then_inc(dve_w.sem, 1)

                    def get(steps, unit, name, exists):
                        if exists:
                            wait(dve, steps, unit, name)

                    def t_in(l):
                        if l < TOP:
                            get(pe_w, q, f"t{l}", win)
                            window(None, tt, TI[:], ps[:, 3, :].rearrange("p (u t) -> p u t", u=4), TI[:], ALU.add)
                        get(pe_w, q, f"u{l}", win)
                        window(f"tx{l - 1}", tt, TX[:], ps[:, 4, :].rearrange("p (u t) -> p u t", u=4), TX[:], ALU.add)

                    for i in range(4):
                        get(pe_w, q, f"gram{i}", win)
                        window(None, tt, GM[:, i, :, :].rearrange("p a b -> p (a b)"), ps[:, 2 + i, :], causal, ALU.mult)
                    window("gm3", tt, TX[:], GM[:, :, 0, :], level[0].unsqueeze(1).to_broadcast([P, 4, WIN]), ALU.mult)
                    window("ab0", tt, TX[:], TX[:], ident[:].unsqueeze(1).to_broadcast([P, 4, WIN]), ALU.add)
                    get(pe_y, y, "mean", prev)
                    norm(None, tt, YC[:], Y[:], ps[:, 6, 0:UT], ALU.subtract)
                    get(act_a, u - 1, "a", nxt)
                    if nxt:
                        wait(dve, dve_a, u - 1, "fac_in")
                        make(None, copy, par[:, 0:NPAR], par_all[:, bass.ds(u * NPAR, NPAR)])
                    make("par", ts, par[:, NPAR:NPAR + 1], col_of(K_A), -1.0, 1.0, ALU.mult, ALU.add)
                    get(act_a, u, "w", nxt)
                    make(None, ts, LW[:], LW[:], DECAY, None, ALU.mult)
                    t_in(1)
                    make("lw", nc.vector.tensor_tensor_scan, L[:], keep[:], LW[:], 0.0, ALU.mult, ALU.add)
                    if prev:
                        norm("y_c", copy, par_y[:], par_all[:, bass.ds(y * NPAR + LNX_G, 2)])
                    if new_pair is not None:
                        wait(dve, dve_a, u - 1, "carry")
                        nc.vector.memset(Z[:, :, 0:1], 0.0).then_inc(zeroed, 1)
                        dve.wait_ge(zeroed, new_pair + 1)
                    get(act_a, u, "k", nxt)
                    make(None, tt, T0[:], Z[:, 1, 0:UT], Z[:, 1, 1:], ALU.subtract)
                    t_in(2)
                    make("k_d", stt, out=K, in0=T0[:], scalar=col_of(MU_K), in1=Z[:, 1, 1:], op0=ALU.mult, op1=ALU.add)
                    make("k", ts, KK[:], K, col_of(K_K), None, ALU.mult)
                    make("scan", tt, windows(LM), windows(L), windows(L)[:, :, HS - 1:HS].to_broadcast([P, 2, WIN]), ALU.subtract)
                    make("lm", tt, EX[:], LM[:], LW[:], ALU.subtract)
                    get(pe_y, y, "var", prev)
                    norm(None, ts, YS[:], ps[:, 6, 0:UT], LNX_EPS, None, ALU.add)
                    t_in(3)
                    make("lm", copy, ends[:, 1:3], windows(LM)[:, :, WIN - 1])
                    make("ends", tt, fac_log[:], ends[:, 0:2], windows(L)[:, :, HS - 1], ALU.add)
                    make("fac", copy, ends[:, 0:1], ends[:, 2:3])
                    get(act_a, u, "a", nxt)
                    make("one_ka", ts, AG[:], SA[:], col_of(K_A), col_of(NPAR), ALU.mult, ALU.add)
                    get(act_y, y, "y_root", prev)
                    norm(None, rec, YS[:], YS[:])
                    make("ag", tt, K, K, AG[:], ALU.mult)
                    t_in(4)
                    norm("y_inv", tt, YC[:], YC[:], YS[:], ALU.mult)
                    get(pe_a, u, "kk_sum", nxt)
                    make(None, ts, NR[:], ps[:, 6, 0:UT], 1e-24, None, ALU.max)
                    get(act_a, u, "r", nxt)
                    make(None, tt, T0[:], Z[:, 0, 0:UT], Z[:, 0, 1:], ALU.subtract)
                    norm("y_n", ts, YC[:], YC[:], par_y[:, 0:1], par_y[:, 1:2], ALU.mult, ALU.add)
                    t_in(5)
                    norm("y_gb", tt, YC[:], YC[:], BON[:], ALU.add)
                    make("r_d", stt, out=R, in0=T0[:], scalar=col_of(MU_R), in1=Z[:, 0, 1:], op0=ALU.mult, op1=ALU.add)
                    get(act_a, u, "root", nxt)
                    make(None, rec, NR[:], NR[:])
                    get(pe_w, q, "bonus", win)
                    get(dve_y, y, "y_b", prev)
                    window(None, tt, BON[:], ps[:, 7, 0:UT], V, ALU.mult)
                    t_in(6)
                    get(dve_a, q, "fac_in", win)
                    window(None, ts, STF[:], ST[:, 0, :], fac_in[:], None, ALU.mult)
                    make("inv", tt, KK[:], KK[:], NR[:], ALU.mult)
                    if prev:
                        gate_then_out = mix_flat[:, bass.ds(2 * S + y * UT, UT)]
                        wait(dve, act_a, y, "g")
                        norm("y_b", tt, gate_then_out, gate_then_out, YC[:], ALU.mult)
                    make("kkn", tt, SA[:], SA[:], KK[:], ALU.mult)
                    make("kkn", stt, out=AR[:, :, 0, :], in0=windows(KK), scalar=-1.0, in1=windows(EX), op0=ALU.mult, op1=ALU.mult)
                    make("b", tt, KB[:, :, 1, :], windows(SA), windows(EN), ALU.mult)
                    make("k2", tt, KB[:, :, 0, :], K.rearrange("p (w t) -> p w t", w=2), windows(EN), ALU.mult)
                    get(pe_w, q, "q", win)
                    window(None, tt, QT[:], ps[:, 2, 0:2 * WIN].rearrange("p (w t) -> p w t", w=2), AR[:, :, 1, :], ALU.add)
                    get(act_a, u, "v", nxt)
                    get(dve_w, q, "bon", win)
                    get(dve_y, y, "y_out", prev)
                    make(None, tt, T0[:], Z[:, 2, 0:UT], Z[:, 2, 1:], ALU.subtract)
                    make("v_d", stt, out=V, in0=T0[:], scalar=col_of(MU_V), in1=Z[:, 2, 1:], op0=ALU.mult, op1=ALU.add)
                    get(pe_w, q, "e0", win)
                    window("stf0", stt, out=ST[:, 1, :], in0=ps[:, 0, 0:HS], scalar=fac_in[:], in1=STF[:], op0=ALU.mult, op1=ALU.add)
                    make("v", copy, Z[:, :, 0:1], Z[:, :, UT:UT + 1])
                    make("r", tt, RK[:], R, K, ALU.mult)
                    get(dve_w, q, "q", win)
                    make("r", tt, AR[:, :, 1, :], R.rearrange("p (w t) -> p w t", w=2), windows(EP), ALU.mult)
                    make("rk", ts, RK[:], RK[:], col_of(R_K), None, ALU.mult)
                    if new_pair is not None or not nxt:
                        window("st0", nc.vector.memset, STF[:], 0.0)
                        get(pe_w, q, "e1", win)
                        window(None, nc.vector.memset, ST[:, 0, :], 0.0)
                    else:
                        window("st0", ts, STF[:], ST[:, 1, :], fac_exp[:, 0:1], None, ALU.mult)
                        get(pe_w, q, "e1", win)
                        window("stf1", stt, out=ST[:, 0, :], in0=ps[:, 4, 0:HS], scalar=fac_exp[:, 0:1], in1=STF[:], op0=ALU.mult,
                               op1=ALU.add)
                    get(act_a, u, "fac", nxt)
                    make(None, copy, fac_in[:], fac_exp[:, 1:2])

                nc.vector.memset(ends[:], 0.0).then_inc(cleared, 1)
                nc.vector.memset(ST[:], 0.0).then_inc(cleared, 1)
                nc.vector.memset(BON[:], 0.0).then_inc(cleared, 1)
                dve.wait_ge(cleared, 3)
                dve.wait_ge(c_in, 48)
                each_unit(dve, body)
                dve.wait_ge(dve_y.sem, dve_y.at(UNITS - 1, "y_out"))


def layer_norm_steps(nc, dve, src, stats, mv, g_row, b_row, n, done, root_ready, rooted):
    for c in range(2):
        done(nc.vector.bn_stats(stats[:, c, :], src[:, c * NB:(c + 1) * NB]))
    done(nc.vector.bn_aggr(mv[:, 0:2], stats[:].rearrange("p a b -> p (a b)")))
    nc.vector.tensor_scalar(mv[:, 2:3], mv[:, 1:2], LN_EPS, None, ALU.add).then_inc(root_ready, 1)
    dve.wait_ge(rooted, n + 1)
    done(nc.vector.reciprocal(mv[:, 2:3], mv[:, 2:3]))
    done(nc.vector.tensor_scalar(src, src, mv[:, 0:1], mv[:, 2:3], ALU.subtract, ALU.mult))
    done(nc.vector.tensor_tensor(src, src, g_row, ALU.mult))
    done(nc.vector.tensor_tensor(src, src, b_row, ALU.add))


def stage_mix_out(nc, mixT, w_out, x_dram, ln_rows, hres, h_dram):
    with Scope(nc, "mixo") as s:
        ws = s.sb("ws", [P, 2, KT, NB])
        rows = s.sb("rows", [P, 2, D])
        stats = s.sb("stats", [P, 2, 6])
        mv = s.sb("mv", [P, 3])
        ps = s.ps("ps", [P, 8, NB])
        w_in, r_in, x_in = s.sem("w_in"), s.sem("r_in"), s.sem("x_in")
        mm, v, root_ready, rooted, h_ready, h_out = (s.sem(n) for n in "mm vector_step root_ready rooted h_ready h_out".split())
        with nc.Block() as block:
            @block.sync
            def _(sp):
                for n in range(2):
                    sp.dma_start(ws[:, n, :, :], w_out[n]).then_inc(w_in, 16)
                sp.dma_start(hres[:], x_dram.rearrange("(t p) d -> p t d", p=P)).then_inc(x_in, 16)
                for n in range(2):
                    sp.dma_start(rows[:, n, :], ln_rows[n].partition_broadcast(P)).then_inc(r_in, 16)
                for t in range(TT):
                    sp.wait_ge(h_ready, t + 1)
                    sp.dma_start(h_dram[t * P:(t + 1) * P, :], hres[:, t, :]).then_inc(h_out, 16)
                sp.wait_ge(h_out, 16 * TT)

            @block.tensor
            def _(pe):
                pe.wait_ge(w_in, 32)
                for t in range(TT):
                    b = 2 * (t % 4)
                    if t >= 4:
                        pe.wait_ge(h_ready, t - 3)
                    for n in range(2):
                        for k in range(KT):
                            last = nc.tensor.matmul(ps[:, b + n, :], lhsT=mixT[:, k, t * P:(t + 1) * P], rhs=ws[:, n, k, :],
                                                    start=(k == 0), stop=(k == KT - 1))
                    last.then_inc(mm, 1)

            @block.scalar
            def _(act):
                for t in range(TT):
                    act.wait_ge(root_ready, t + 1)
                    nc.scalar.activation(mv[:, 2:3], mv[:, 2:3], ACT.Sqrt).then_inc(rooted, 1)

            @block.vector
            def _(dve):
                step = [0]

                def done(ins):
                    step[0] += 1
                    ins.then_inc(v, 1)
                    dve.wait_ge(v, step[0])

                dve.wait_ge(x_in, 16)
                dve.wait_ge(r_in, 32)
                for t in range(TT):
                    dve.wait_ge(mm, t + 1)
                    b = 2 * (t % 4)
                    h = hres[:, t, :]
                    done(nc.vector.scalar_tensor_tensor(out=h, in0=h, scalar=ALPHA, in1=ps[:, b:b + 2, :].rearrange("p a b -> p (a b)"),
                                                        op0=ALU.mult, op1=ALU.add))
                    layer_norm_steps(nc, dve, h, stats, mv, rows[:, 0, :], rows[:, 1, :], t, done, root_ready, rooted)
                    dve.sem_inc(h_ready, 1)


GROUPS = 4
PER_GROUP = 8
EXPERTS = GROUPS * PER_GROUP
D_EXP = D // 4
LOGITS = GROUPS + EXPERTS
MAX_MORE = S // P - 1
OVERFLOW = 2 * S // P - 1
BLOCKS = EXPERTS + OVERFLOW
ROWS = BLOCKS * P
FAR = 1e30


def stage_router(nc, hT, w_router, b_router, counts_in, dest, wgt, over, row_tok, tok_of_row, y_dram, ones, cumul,
                 ident):
    IG, IE, IB, IJ = 0, GROUPS, GROUPS + EXPERTS, GROUPS + EXPERTS + OVERFLOW
    with Scope(nc, "rt") as s:
        wr = s.sb("wr", [P, KT, LOGITS])
        br = s.sb("br", [P, LOGITS])
        cnt = s.sb("cnt", [P, GROUPS + EXPERTS + OVERFLOW + MAX_MORE])
        lg = s.sb("lg", [P, TT, LOGITS])
        a1 = s.sb("a1", [P, TT, 12])
        g4 = s.sb("g4", [P, 3, TT, GROUPS])
        em = s.sb("em", [P, TT, EXPERTS])
        e32 = s.sb("e32", [P, TT, EXPERTS])
        oh = s.sb("oh", [P, 2, TT, EXPERTS])
        both = s.sb("both", [P, TT, EXPERTS])
        cum = s.sb("cum", [P, TT, EXPERTS])
        row = s.sb("row", [P, 6, EXPERTS])
        more = s.sb("more", [P, EXPERTS, MAX_MORE])
        ble = s.sb("ble", [P, OVERFLOW, EXPERTS])
        blk = s.sb("blk", [P, OVERFLOW + 1])
        dst = s.sb("dst", [P, 2, TT])
        tok = s.sb("tok", [P, TT], I32)
        zero = s.sb("zero", [BLOCKS, P], I32)
        back = s.sb("back", [BLOCKS, P], I32)
        backf = s.sb("backf", [BLOCKS, P])
        blank = s.sb("blank", [P, D])
        pl = s.ps("pl", [P, TT, 64])
        pc = s.ps("pc", [P, TT, EXPERTS])
        pn = s.ps("pn", [P, EXPERTS])
        pt = s.ps("pt", [P, BLOCKS])
        cleared = s.sem("cleared")
        w_in, mm, v, exp_in, exps = s.sem("w_in"), s.sem("mm"), s.sem("vector_step"), s.sem("exp_in"), s.sem("exps")
        both_ready, placed, tok_ready, zero_ready = s.sem("both_ready"), s.sem("placed"), s.sem("tok_ready"), s.sem("zero_ready")
        zeroed, scattered, back_in, backf_ready, turned, ready = (s.sem(n) for n in "zeroed scattered back_in backf_ready turned ready".split())
        with nc.Block() as block:
            @block.sync
            def _(sp):
                sp.dma_start(wr[:], w_router).then_inc(w_in, 16)
                sp.dma_start(br[:], b_router.partition_broadcast(P)).then_inc(w_in, 16)
                sp.dma_start(cnt[:], counts_in.partition_broadcast(P)).then_inc(w_in, 16)
                sp.wait_ge(zero_ready, 2)
                sp.dma_start(row_tok.rearrange("(b p) a -> b (p a)", p=P), zero[:]).then_inc(zeroed, 16)
                sp.wait_ge(scattered, 16 * 2 * TT)
                sp.dma_start(back[:], row_tok.rearrange("(b p) a -> b (p a)", p=P)).then_inc(back_in, 16)

            @block.tensor
            def _(pe):
                pe.wait_ge(w_in, 48)
                for t in range(TT):
                    for k in range(KT):
                        last = nc.tensor.matmul(pl[:, t, 0:LOGITS], lhsT=hT[:, k, t * P:(t + 1) * P], rhs=wr[:, k, :],
                                                start=(k == 0), stop=(k == KT - 1))
                last.then_inc(mm, 1)
                pe.wait_ge(both_ready, 1)
                for t in range(TT):
                    for j in range(t + 1):
                        last = nc.tensor.matmul(pc[:, t, :], lhsT=(cumul if j == t else ones)[:], rhs=both[:, j, :],
                                                start=(j == 0), stop=(j == t))
                for j in range(TT):
                    last = nc.tensor.matmul(pn[:], lhsT=ones[:], rhs=both[:, j, :], start=(j == 0), stop=(j == TT - 1))
                last.then_inc(mm, 1)
                pe.wait_ge(backf_ready, 1)
                nc.tensor.transpose(pt[:], backf[:], ident[0:BLOCKS, 0:BLOCKS]).then_inc(turned, 1)

            @block.scalar
            def _(act):
                act.wait_ge(zero_ready, 2)
                for n in range(EXPERTS, BLOCKS):
                    act.dma_start(y_dram[n * P:(n + 1) * P, :], blank[:]).then_inc(cleared, 16)
                act.wait_ge(exp_in, 1)
                nc.scalar.activation(g4[:, 1, :, :], g4[:, 1, :, :], ACT.Exp).then_inc(exps, 1)
                act.wait_ge(exp_in, 2)
                nc.scalar.activation(a1[:, :, 5], a1[:, :, 5], ACT.Exp).then_inc(exps, 1)
                act.wait_ge(cleared, 16 * OVERFLOW)

            @block.gpsimd
            def _(pool):
                nc.gpsimd.iota(tok[:], pattern=[[P, TT]], base=0, channel_multiplier=1).then_inc(tok_ready, 1)
                nc.gpsimd.memset(zero[:], 0).then_inc(zero_ready, 1)
                nc.gpsimd.memset(blank[:], 0.0).then_inc(zero_ready, 1)
                pool.wait_ge(tok_ready, 1)
                pool.wait_ge(zeroed, 16)
                pool.wait_ge(placed, 1)
                for c in range(2):
                    for t in range(TT):
                        nc.gpsimd.indirect_dma_start(out=row_tok, out_offset=bass.IndirectOffsetOnAxis(ap=dest[:, c, t:t + 1], axis=0),
                                                     in_=tok[:, t:t + 1], in_offset=None).then_inc(scattered, 16)

            @block.vector
            def _(dve):
                step = [0]
                tt, ts, stt, red = (nc.vector.tensor_tensor, nc.vector.tensor_scalar, nc.vector.scalar_tensor_tensor,
                                    nc.vector.tensor_reduce)

                def done(ins):
                    step[0] += 1
                    ins.then_inc(v, 1)
                    dve.wait_ge(v, step[0])

                def over_tokens(a, n):
                    return a.unsqueeze(1).to_broadcast([P, TT, n])

                def over_last(a, n):
                    return a.unsqueeze(2).to_broadcast([P, TT, n])

                def first_max(vals, n, iota, scratch, top, index, onehot):
                    done(red(top, vals, AX.X, ALU.max))
                    done(tt(scratch, vals, over_last(top, n), ALU.is_lt))
                    done(stt(out=scratch, in0=scratch, scalar=1000.0, in1=over_tokens(iota, n), op0=ALU.mult, op1=ALU.add))
                    done(red(index, scratch, AX.X, ALU.min))
                    done(tt(onehot, over_tokens(iota, n), over_last(index, n), ALU.is_equal))

                dve.wait_ge(w_in, 48)
                dve.wait_ge(mm, 1)
                done(tt(lg[:], pl[:, :, 0:LOGITS], over_tokens(br[:], LOGITS), ALU.add))
                iota_g, iota_e = cnt[:, IG:IG + GROUPS], cnt[:, IE:IE + EXPERTS]
                gl, el = lg[:, :, 0:GROUPS], lg[:, :, GROUPS:]
                first_max(gl, GROUPS, iota_g, g4[:, 0], a1[:, :, 0], a1[:, :, 1], g4[:, 2])
                tt(g4[:, 1], gl, over_last(a1[:, :, 0], GROUPS), ALU.subtract).then_inc(exp_in, 1)
                grp = g4[:, 2].unsqueeze(3).to_broadcast([P, TT, GROUPS, PER_GROUP])
                done(tt(em[:].rearrange("p t (g e) -> p t g e", g=GROUPS), el.rearrange("p t (g e) -> p t g e", g=GROUPS), grp,
                        ALU.mult))
                done(ts(g4[:, 0], g4[:, 2], -1.0, FAR, ALU.add, ALU.mult))
                done(tt(em[:].rearrange("p t (g e) -> p t g e", g=GROUPS), em[:].rearrange("p t (g e) -> p t g e", g=GROUPS),
                        g4[:, 0].unsqueeze(3).to_broadcast([P, TT, GROUPS, PER_GROUP]), ALU.add))
                first_max(em[:], EXPERTS, iota_e, e32[:], a1[:, :, 2], a1[:, :, 3], oh[:, 0])
                done(stt(out=em[:], in0=oh[:, 0], scalar=-3.0 * FAR, in1=em[:], op0=ALU.mult, op1=ALU.add))
                first_max(em[:], EXPERTS, iota_e, e32[:], a1[:, :, 4], a1[:, :, 6], oh[:, 1])
                tt(a1[:, :, 5], a1[:, :, 4], a1[:, :, 2], ALU.subtract).then_inc(exp_in, 1)
                tt(both[:], oh[:, 0], oh[:, 1], ALU.add).then_inc(both_ready, 1)
                dve.wait_ge(exps, 1)
                done(red(a1[:, :, 7], g4[:, 1], AX.X, ALU.add))
                dve.wait_ge(exps, 2)
                done(ts(a1[:, :, 8], a1[:, :, 5], 1.0, None, ALU.add))
                done(tt(a1[:, :, 7], a1[:, :, 7], a1[:, :, 8], ALU.mult))
                done(nc.vector.reciprocal(wgt[:, 0, :], a1[:, :, 7]))
                done(tt(wgt[:, 1, :], wgt[:, 0, :], a1[:, :, 5], ALU.mult))
                dve.wait_ge(mm, 2)
                done(nc.vector.tensor_copy(row[:, 0, :], pn[:]))
                done(tt(more[:], row[:, 0, :].unsqueeze(2).to_broadcast([P, EXPERTS, MAX_MORE]),
                        cnt[:, IJ:IJ + MAX_MORE].unsqueeze(1).to_broadcast([P, EXPERTS, MAX_MORE]), ALU.is_gt))
                done(red(row[:, 1, :], more[:], AX.X, ALU.add))
                done(nc.vector.memset(row[:, 2, :], 1.0))
                done(nc.vector.tensor_tensor_scan(row[:, 3, :], row[:, 2, :], row[:, 1, :], 0.0, ALU.mult, ALU.add))
                done(tt(row[:, 4, :], row[:, 3, :], row[:, 1, :], ALU.subtract))
                done(ts(row[:, 5, :], row[:, 4, :], float(P), float((EXPERTS - 1) * P), ALU.mult, ALU.add))
                done(tt(ble[:], row[:, 3, :].unsqueeze(1).to_broadcast([P, OVERFLOW, EXPERTS]),
                        cnt[:, IB:IB + OVERFLOW].unsqueeze(2).to_broadcast([P, OVERFLOW, EXPERTS]), ALU.is_le))
                done(red(blk[:, 0:OVERFLOW], ble[:], AX.X, ALU.add))
                done(ts(blk[:, 0:OVERFLOW], blk[:, 0:OVERFLOW], float(EXPERTS - 1), None, ALU.min))
                done(nc.vector.tensor_copy(blk[:, OVERFLOW:], row[:, 3, EXPERTS - 1:]))
                done(nc.vector.tensor_copy(over[:], blk[0:1, :]))
                done(nc.vector.tensor_copy(cum[:], pc[:]))
                for c in range(2):
                    e = a1[:, :, 3] if c == 0 else a1[:, :, 6]
                    done(tt(e32[:], oh[:, c], cum[:], ALU.mult))
                    done(red(a1[:, :, 9], e32[:], AX.X, ALU.add))
                    done(ts(a1[:, :, 9], a1[:, :, 9], -1.0, None, ALU.add))
                    done(tt(e32[:], oh[:, c], over_tokens(row[:, 5, :], EXPERTS), ALU.mult))
                    done(red(a1[:, :, 10], e32[:], AX.X, ALU.add))
                    done(stt(out=a1[:, :, 10], in0=e, scalar=-float(P), in1=a1[:, :, 10], op0=ALU.mult, op1=ALU.add))
                    done(ts(a1[:, :, 11], a1[:, :, 9], float(P), None, ALU.is_ge))
                    done(tt(a1[:, :, 10], a1[:, :, 10], a1[:, :, 11], ALU.mult))
                    done(stt(out=a1[:, :, 9], in0=e, scalar=float(P), in1=a1[:, :, 9], op0=ALU.mult, op1=ALU.add))
                    done(tt(dst[:, c, :], a1[:, :, 9], a1[:, :, 10], ALU.add))
                nc.vector.tensor_copy(dest[:], dst[:]).then_inc(placed, 1)
                dve.wait_ge(back_in, 16)
                nc.vector.tensor_copy(backf[:], back[:]).then_inc(backf_ready, 1)
                dve.wait_ge(turned, 1)
                nc.vector.tensor_copy(tok_of_row[:], pt[:]).then_inc(ready, 1)
                dve.wait_ge(ready, 1)


def stage_experts(nc, h_dram, w_gu, w_d, over, tok_of_row, y_dram, ident):
    NW = 4
    with Scope(nc, "ex") as s:
        gu = s.sb("gu", [P, NW, KT, 2 * D_EXP])
        dn = s.sb("dn", [P, NW, 2, D])
        idx = s.sb("idx", [P, NW], I32)
        xg = s.sb("xg", [P, NW, D])
        xT = s.sb("xT", [P, 2, KT, P])
        sil = s.sb("sil", [P, 2, D_EXP])
        hid = s.sb("hid", [P, 2, D_EXP])
        hT = s.sb("hT", [P, 2, 2, P])
        y = s.sb("y", [P, 2, D])
        px = s.ps("px", [P, 2, NB])
        pg = s.ps("pg", [P, 2, NB])
        ph = s.ps("ph", [P, 2, NB])
        py = s.ps("py", [P, 2, NB])
        names = "x_turned x_taken gated silu hidden h_turned h_taken downed y_taken_a y_taken_v"

        class Ring:
            pass

        pipe, more = Ring(), Ring()
        for ring, tag in ((pipe, "p"), (more, "o")):
            (ring.x_turned, ring.x_taken, ring.gated, ring.silu, ring.hidden, ring.h_turned, ring.h_taken, ring.downed,
             ring.y_taken_a, ring.y_taken_v) = (s.sem(f"{tag}_{n}") for n in names.split())
        w_in = [s.sem(f"w_in{n}") for n in range(NW)]
        x_in = [s.sem(f"x_in{n}") for n in range(NW)]
        y_out = [s.sem("y_out0"), s.sem("y_out1")]
        idx_ready, gate = s.sem("idx_ready"), s.sem("pool_gate")
        o_w_in, o_x_in, o_y_out, o_idx, o_stored = (s.sem(n) for n in "o_w_in o_x_in o_y_out o_idx o_stored".split())
        y_rows = y_dram.rearrange("(b p) d -> b p d", p=P)

        def number_of_overflow(eng):
            return eng.value_load(over[0:1, OVERFLOW:OVERFLOW + 1], min_val=0, max_val=OVERFLOW)

        with nc.Block() as block:
            @block.sync
            def _(sp):
                def load(b, n):
                    sp.dma_start(gu[:, n, :, :], w_gu[b]).then_inc(w_in[n], 16)
                    sp.dma_start(dn[:, n, :, :], w_d[b]).then_inc(w_in[n], 16)

                def store(b, n):
                    sp.wait_ge(pipe.y_taken_a, b + 2)
                    sp.wait_ge(pipe.y_taken_v, b + 2)
                    sp.dma_start(y_rows[b], y[:, n % 2, :]).then_inc(y_out[n % 2], 16)

                for n in range(NW):
                    load(n, n)
                with sp.Fori(0, EXPERTS // NW - 1) as j:
                    for n in range(NW):
                        store(NW * j + n, n)
                        sp.wait_ge(pipe.downed, NW * j + n + 3)
                        load(NW * j + n + NW, n)
                for b in range(EXPERTS - NW, EXPERTS):
                    store(b, b % NW)
                sp.wait_ge(pipe.downed, EXPERTS + 2)
                n_over = number_of_overflow(sp)
                with sp.Fori(0, OVERFLOW) as b:
                    with sp.If(b < n_over):
                        e = sp.value_load(over[0:1, bass.ds(b, 1)], min_val=0, max_val=EXPERTS - 1)
                        sp.wait_ge(more.downed, b + 1)
                        sp.dma_start(gu[:, 0, :, :], w_gu[e]).then_inc(o_w_in, 16)
                        sp.dma_start(dn[:, 0, :, :], w_d[e]).then_inc(o_w_in, 16)
                        sp.wait_ge(more.y_taken_a, b + 1)
                        sp.wait_ge(more.y_taken_v, b + 1)
                        sp.dma_start(y_rows[EXPERTS + b], y[:, 0, :]).then_inc(o_y_out, 16)
                        sp.wait_ge(o_y_out, 16 * b + 16)
                        sp.sem_inc(o_stored, 1)
                for n in range(2):
                    sp.wait_ge(y_out[n], 16 * (EXPERTS // 2 + 1))

            @block.gpsimd
            def _(pool):
                def gather(b, n, index):
                    nc.gpsimd.tensor_copy(idx[:, n:n + 1], tok_of_row[:, index]).then_inc(idx_ready, 1)
                    pool.wait_ge(idx_ready, b + 1)
                    pool.sem_inc(gate, 1)
                    nc.gpsimd.indirect_dma_start(out=xg[:, n, :], out_offset=None, in_=h_dram,
                                                 in_offset=bass.IndirectOffsetOnAxis(ap=idx[:, n:n + 1], axis=0)
                                                 ).then_inc(x_in[n], 16)

                for n in range(NW):
                    gather(n, n, slice(n, n + 1))
                with pool.Fori(1, EXPERTS // NW) as j:
                    for n in range(NW):
                        pool.wait_ge(pipe.x_turned, NW * j + n - NW + 1)
                        pool.sem_inc(gate, 1)
                        gather(NW * j + n, n, bass.ds(NW * j + n, 1))
                pool.wait_ge(pipe.x_turned, EXPERTS)
                n_over = number_of_overflow(pool)
                with pool.Fori(0, OVERFLOW) as b:
                    with pool.If(b < n_over):
                        pool.wait_ge(more.x_turned, b + 1)
                        pool.sem_inc(gate, 1)
                        nc.gpsimd.tensor_copy(idx[:, 0:1], tok_of_row[:, bass.ds(b + EXPERTS, 1)]).then_inc(o_idx, 1)
                        pool.wait_ge(o_idx, b + 1)
                        pool.sem_inc(gate, 1)
                        nc.gpsimd.indirect_dma_start(out=xg[:, 0, :], out_offset=None, in_=h_dram,
                                                     in_offset=bass.IndirectOffsetOnAxis(ap=idx[:, 0:1], axis=0)
                                                     ).then_inc(o_x_in, 16)

            @block.tensor
            def _(pe):
                def turn_x(ring, b, n):
                    for k in range(KT):
                        last = nc.tensor.transpose(px[:, k // 4, (k % 4) * P:(k % 4 + 1) * P], xg[:, n, k * P:(k + 1) * P],
                                                   ident[:])
                    last.then_inc(ring.x_turned, 1)

                def up(ring, b, n):
                    for k in range(KT):
                        last = nc.tensor.matmul(pg[:, n % 2, :], lhsT=xT[:, n % 2, k, :], rhs=gu[:, n, k, :], start=(k == 0),
                                                stop=(k == KT - 1))
                    last.then_inc(ring.gated, 1)

                def turn_h(ring, b, n):
                    for j in range(2):
                        last = nc.tensor.transpose(ph[:, n % 2, j * P:(j + 1) * P], hid[:, n % 2, j * P:(j + 1) * P], ident[:])
                    last.then_inc(ring.h_turned, 1)

                def down(ring, b, n):
                    for half in range(2):
                        for j in range(2):
                            last = nc.tensor.matmul(py[:, half, :], lhsT=hT[:, n % 2, j, :],
                                                    rhs=dn[:, n, j, half * NB:(half + 1) * NB], start=(j == 0), stop=(j == 1))
                    last.then_inc(ring.downed, 1)

                def p_turn_x(b, n, turn):
                    pe.wait_ge(x_in[n], 16 * turn)
                    pe.wait_ge(pipe.x_taken, b + 1)
                    turn_x(pipe, b, n)

                def p_up(b, n, turn):
                    pe.wait_ge(w_in[n], 32 * turn)
                    pe.wait_ge(pipe.x_taken, b + 2)
                    pe.wait_ge(pipe.hidden, b + 1)
                    up(pipe, b, n)

                def p_turn_h(b, n):
                    pe.wait_ge(pipe.hidden, b + 3)
                    pe.wait_ge(pipe.h_taken, b + 1)
                    turn_h(pipe, b, n)

                def p_down(b, n):
                    pe.wait_ge(pipe.h_taken, b + 3)
                    pe.wait_ge(pipe.y_taken_a, b + 1)
                    pe.wait_ge(pipe.y_taken_v, b + 1)
                    down(pipe, b, n)

                pe.sem_inc(pipe.gated, 2)
                pe.sem_inc(pipe.h_turned, 2)
                pe.sem_inc(pipe.downed, 2)
                pe.sem_inc(more.downed, 1)
                pe.sem_inc(more.x_turned, 1)
                p_turn_x(0, 0, 1)
                p_turn_x(1, 1, 1)
                p_up(0, 0, 1)
                with pe.Fori(0, EXPERTS // NW - 1) as j:
                    for n in range(NW):
                        b = NW * j + n
                        p_up(b + 1, (n + 1) % NW, j + 1 + (n + 1) // NW)
                        p_turn_h(b, n)
                        p_turn_x(b + 2, (n + 2) % NW, j + 1 + (n + 2) // NW)
                        p_down(b, n)
                for b in range(EXPERTS - NW, EXPERTS):
                    if b + 1 < EXPERTS:
                        p_up(b + 1, (b + 1) % NW, EXPERTS // NW)
                    p_turn_h(b, b % NW)
                    if b + 2 < EXPERTS:
                        p_turn_x(b + 2, (b + 2) % NW, EXPERTS // NW)
                    p_down(b, b % NW)
                pe.wait_ge(pipe.y_taken_a, EXPERTS + 1)
                pe.wait_ge(pipe.y_taken_v, EXPERTS + 1)
                n_over = number_of_overflow(pe)
                with pe.Fori(0, OVERFLOW) as b:
                    with pe.If(b < n_over):
                        pe.wait_ge(o_x_in, 16 * b + 16)
                        turn_x(more, b, 0)
                        pe.wait_ge(o_w_in, 32 * b + 32)
                        pe.wait_ge(more.x_taken, b + 1)
                        up(more, b, 0)
                        pe.wait_ge(more.hidden, b + 1)
                        turn_h(more, b, 0)
                        pe.wait_ge(more.h_taken, b + 1)
                        down(more, b, 0)

            @block.scalar
            def _(act):
                def take_x(ring, b, n):
                    nc.scalar.copy(xT[:, n % 2, :, :].rearrange("p a b -> p (a b)"),
                                   px[:].rearrange("p a b -> p (a b)")).then_inc(ring.x_taken, 1)

                def silu(ring, b, n):
                    nc.scalar.activation(sil[:, n % 2, :], pg[:, n % 2, 0:D_EXP], ACT.Silu).then_inc(ring.silu, 1)

                def take_y(ring, b, n):
                    nc.scalar.copy(y[:, n % 2, NB:], py[:, 1, :]).then_inc(ring.y_taken_a, 1)

                def p_take_x(b, n):
                    act.wait_ge(pipe.x_turned, b + 1)
                    act.wait_ge(pipe.gated, b + 1)
                    take_x(pipe, b, n)

                def p_silu(b, n):
                    act.wait_ge(pipe.gated, b + 3)
                    act.wait_ge(pipe.hidden, b + 1)
                    silu(pipe, b, n)

                def p_take_y(b, n, turn):
                    act.wait_ge(pipe.downed, b + 3)
                    act.wait_ge(y_out[n % 2], 16 * turn)
                    take_y(pipe, b, n)

                act.sem_inc(pipe.x_taken, 1)
                act.sem_inc(pipe.y_taken_a, 1)
                p_take_x(0, 0)
                p_take_x(1, 1)
                p_silu(0, 0)
                with act.Fori(0, EXPERTS // NW - 1) as j:
                    for n in range(NW):
                        b = NW * j + n
                        p_silu(b + 1, n + 1)
                        p_take_x(b + 2, n)
                        p_take_y(b, n, 2 * j + n // 2 + 1)
                for b in range(EXPERTS - NW, EXPERTS):
                    if b + 1 < EXPERTS:
                        p_silu(b + 1, b + 1)
                    if b + 2 < EXPERTS:
                        p_take_x(b + 2, b)
                    p_take_y(b, b, b // 2 + 1)
                act.wait_ge(y_out[0], 16 * (EXPERTS // 2 + 1))
                n_over = number_of_overflow(act)
                with act.Fori(0, OVERFLOW) as b:
                    with act.If(b < n_over):
                        act.wait_ge(more.x_turned, b + 2)
                        take_x(more, b, 0)
                        act.wait_ge(more.gated, b + 1)
                        silu(more, b, 0)
                        act.wait_ge(more.downed, b + 2)
                        act.wait_ge(o_stored, b + 1)
                        take_y(more, b, 0)

            @block.vector
            def _(dve):
                def hidden(ring, b, n):
                    nc.vector.tensor_tensor(hid[:, n % 2, :], pg[:, n % 2, D_EXP:], sil[:, n % 2, :], ALU.mult
                                            ).then_inc(ring.hidden, 1)

                def take_h(ring, b, n):
                    nc.vector.tensor_copy(hT[:, n % 2, :, :].rearrange("p a b -> p (a b)"), ph[:, n % 2, 0:2 * P]
                                          ).then_inc(ring.h_taken, 1)

                def take_y(ring, b, n):
                    nc.vector.tensor_copy(y[:, n % 2, 0:NB], py[:, 0, :]).then_inc(ring.y_taken_v, 1)

                def p_hidden(b, n):
                    dve.wait_ge(pipe.silu, b + 1)
                    dve.wait_ge(pipe.h_turned, b + 1)
                    hidden(pipe, b, n)

                def p_take_h(b, n):
                    dve.wait_ge(pipe.h_turned, b + 3)
                    dve.wait_ge(pipe.downed, b + 1)
                    take_h(pipe, b, n)

                def p_take_y(b, n, turn):
                    dve.wait_ge(pipe.downed, b + 3)
                    dve.wait_ge(y_out[n % 2], 16 * turn)
                    take_y(pipe, b, n)

                dve.sem_inc(pipe.hidden, 2)
                dve.sem_inc(pipe.h_taken, 2)
                dve.sem_inc(pipe.y_taken_v, 1)
                dve.sem_inc(y_out[0], 16)
                dve.sem_inc(y_out[1], 16)
                dve.sem_inc(o_stored, 1)
                p_hidden(0, 0)
                with dve.Fori(0, EXPERTS // NW - 1) as j:
                    for n in range(NW):
                        b = NW * j + n
                        p_hidden(b + 1, n + 1)
                        p_take_h(b, n)
                        p_take_y(b, n, 2 * j + n // 2 + 1)
                for b in range(EXPERTS - NW, EXPERTS):
                    if b + 1 < EXPERTS:
                        p_hidden(b + 1, b + 1)
                    p_take_h(b, b)
                    p_take_y(b, b, b // 2 + 1)
                dve.wait_ge(y_out[0], 16 * (EXPERTS // 2 + 1))
                n_over = number_of_overflow(dve)
                with dve.Fori(0, OVERFLOW) as b:
                    with dve.If(b < n_over):
                        dve.wait_ge(more.silu, b + 1)
                        hidden(more, b, 0)
                        dve.wait_ge(more.h_turned, b + 1)
                        take_h(more, b, 0)
                        dve.wait_ge(more.downed, b + 2)
                        dve.wait_ge(o_stored, b + 1)
                        take_y(more, b, 0)


def stage_combine(nc, hres, y_dram, dest, wgt, ln_rows, out_rows):
    with Scope(nc, "cmb") as s:
        rows = s.sb("rows", [P, 2, D])
        yg = s.sb("yg", [P, 4, 2, D])
        stats = s.sb("stats", [P, 2, 6])
        mv = s.sb("mv", [P, 3])
        r_in, g_in = s.sem("r_in"), [s.sem(f"g_in{n}") for n in range(4)]
        v, root_ready, rooted, ready, stored = (s.sem(n) for n in "vector_step root_ready rooted ready stored".split())
        with nc.Block() as block:
            @block.sync
            def _(sp):
                for n in range(2):
                    sp.dma_start(rows[:, n, :], ln_rows[n].partition_broadcast(P)).then_inc(r_in, 16)
                for t in range(TT):
                    sp.wait_ge(ready, t + 1)
                    sp.dma_start(out_rows[t * P:(t + 1) * P, :], hres[:, t, :]).then_inc(stored, 16)
                sp.wait_ge(stored, 16 * TT)

            @block.gpsimd
            def _(pool):
                for t in range(TT):
                    if t >= 4:
                        pool.wait_ge(ready, t - 3)
                    for c in range(2):
                        nc.gpsimd.indirect_dma_start(out=yg[:, t % 4, c, :], out_offset=None, in_=y_dram,
                                                     in_offset=bass.IndirectOffsetOnAxis(ap=dest[:, c, t:t + 1], axis=0)
                                                     ).then_inc(g_in[t % 4], 16)

            @block.scalar
            def _(act):
                for t in range(TT):
                    act.wait_ge(root_ready, t + 1)
                    nc.scalar.activation(mv[:, 2:3], mv[:, 2:3], ACT.Sqrt).then_inc(rooted, 1)

            @block.vector
            def _(dve):
                step = [0]

                def done(ins):
                    step[0] += 1
                    ins.then_inc(v, 1)
                    dve.wait_ge(v, step[0])

                dve.wait_ge(r_in, 32)
                for t in range(TT):
                    h = hres[:, t, :]
                    done(nc.vector.tensor_scalar(h, h, ALPHA, None, ALU.mult))
                    dve.wait_ge(g_in[t % 4], 32 * (t // 4 + 1))
                    for c in range(2):
                        done(nc.vector.scalar_tensor_tensor(out=h, in0=yg[:, t % 4, c, :], scalar=wgt[:, c, t:t + 1], in1=h,
                                                            op0=ALU.mult, op1=ALU.add))
                    layer_norm_steps(nc, dve, h, stats, mv, rows[:, 0, :], rows[:, 1, :], t, done, root_ready, rooted)
                    dve.sem_inc(ready, 1)


def first_program(nc, A, x_dram, consts):
    ident, ones, cumul, ident16, future16 = consts
    with Scope(nc, "first") as g:
        xres = g.sb("xres", [P, TT, D])
        with Scope(nc, "b1") as b:
            gates = b.sb("gates", [P, 2, D])
            modc = b.sb("modc", [P, 2, 2, KT])
            stage_modulation(nc, A["x"], A["cols1"], A["w_ada"], A["b_ada"], xres, modc, gates, ones)
            with Scope(nc, "att_data") as a:
                qkv = a.sb("qkv", [P, TT, QKV])
                ss = a.sb("ss", [P, TT, 3 * HEADS])
                neg_f = a.sb("neg_f", [P, TT, HEADS])
                with Scope(nc, "h1") as h:
                    hT = h.sb("hT", [P, KT, S])
                    stage_norm(nc, "norm1", xres, hT, modc[:, 0], ident)
                    stage_qkv(nc, hT, A["w_qkv"], A["w_f"], A["b_f"], qkv, ss, neg_f, cumul, ones)
                with Scope(nc, "o") as o:
                    o_all = o.sb("o_all", [P, TT, D])
                    stage_attention(nc, qkv, ss, neg_f, A["qk_gain"], o_all, ident, ident16, future16)
                    stage_out(nc, "out1", o_all, A["w_o"], xres, gates[:, 0, :], ident,
                              qkv[:].rearrange("p t c -> p (t c)"))
            with Scope(nc, "h2") as h:
                hT = h.sb("hT", [P, KT, S])
                stage_norm(nc, "norm2", xres, hT, modc[:, 1], ident)
                stage_mlp(nc, hT, A["w1"], A["w2"], xres, gates[:, 1, :], ident)
        with Scope(nc, "end") as e, nc.Block() as block:
            done = e.sem("done")

            @block.sync
            def _(sp):
                sp.dma_start(x_dram.rearrange("(t p) d -> p t d", p=P), xres[:]).then_inc(done, 16)
                sp.wait_ge(done, 16)


def third_program(nc, A, hres, h_dram, row_tok, y_dram, out_rows, ident, ones, cumul):
    with Scope(nc, "b3") as b:
        dest = b.sb("dest", [P, 2, TT], I32)
        wgt = b.sb("wgt", [P, 2, TT])
        over = b.sb("over", [1, OVERFLOW + 1], I32)
        tok_of_row = b.sb("tok_of_row", [P, BLOCKS], I32)
        with Scope(nc, "rh") as r:
            hT = r.sb("hT", [P, KT, S])
            stage_turn(nc, "turn3", hres, hT, ident)
            stage_router(nc, hT, A["w_router"], A["b_router"], A["counts"], dest, wgt, over, row_tok, tok_of_row, y_dram, ones,
                         cumul, ident)
        stage_experts(nc, h_dram, A["w_gu"], A["w_d"], over, tok_of_row, y_dram, ident)
        stage_combine(nc, hres, y_dram, dest, wgt, A["ln2"], out_rows)


def second_program(nc, A, x_dram, h_dram, row_tok, y_dram, out_rows, consts):
    ident, ones, cumul = consts[:3]
    with Scope(nc, "b2") as b:
        with Scope(nc, "mx") as m:
            mixT = m.sb("mixT", [P, KT, S])
            with Scope(nc, "x2") as x2:
                xT = x2.sb("xT", [P, KT, S])
                lora_in = x2.sb("lora_in", [P, 2, S])
                with Scope(nc, "xr") as xr:
                    xres = xr.sb("xres", [P, TT, D])
                    load_rows(nc, "ld", x_dram, xres)
                    stage_turn(nc, "turn2", xres, xT, ident)
                stage_pool(nc, xT, A["w_head"], A["head_cols"], A["pool_w"], A["inv_count"], mixT, lora_in)
                stage_rwkv(nc, xT, A["w_rkv"], A["lora_up"], A["unit_cols"], A["window_consts"], A["scan_keep"], lora_in,
                           mixT, ident)
            hres = m.sb("hres", [P, TT, D])
            stage_mix_out(nc, mixT, A["w_mix"], x_dram, A["ln1"], hres, h_dram)
            third_program(nc, A, hres, h_dram, row_tok, y_dram, out_rows, ident, ones, cumul)


def load_rows(nc, tag, dram, tile):
    with Scope(nc, tag) as s, nc.Block() as block:
        rows_in = s.sem("rows_in")

        @block.sync
        def _(sp):
            sp.dma_start(tile[:], dram.rearrange("(t p) d -> p t d", p=P)).then_inc(rows_in, 16)
            sp.wait_ge(rows_in, 16)


def col(v):
    return v.reshape(-1, P).T


def chunks(w, n):
    k, m = w.shape
    return w.reshape(k // P, P, m // n, n).transpose(2, 1, 0, 3)


def layouts_second(np, I):
    wi = I["w_in_2"][0]
    pool, rw = wi[:, :256], wi[:, 256:]
    dr = PAIRS * P
    r, k, v = (rw[:, n * dr:(n + 1) * dr] for n in range(3))
    head = np.concatenate([pool, rw[:, 3 * dr:]], axis=1)
    mu = I["mu_shift_2"][0]
    windows = (2, 4, 8, 16)
    t = np.arange(S)
    w_of = np.repeat(np.array(windows), 64).reshape(2, P)
    inv_count = (1.0 / np.minimum(t[None, None, :16] + 1, w_of[:, :, None])).astype(np.float32).transpose(1, 0, 2)
    head_cols = np.concatenate([col(mu[3 * dr:]), col(I["pool_scale_2"][0]), (1.0 / w_of).astype(np.float32).T], axis=1)
    pool_w = np.zeros((P, 2, P), np.float32)
    for g in range(4):
        h = slice(64 * (g % 2), 64 * (g % 2) + 64)
        pool_w[h, g // 2, h] = I["pool_w_2"][0, g]
    rkv = np.stack([np.stack([chunks(w, P)[p] for w in (r, k, v)], axis=1) for p in range(PAIRS)])
    up = np.zeros((PAIRS, P, 3, P), np.float32)
    for p in range(PAIRS):
        c = slice(p * P, (p + 1) * P)
        up[p, :64, 0], up[p, 64:, 1], up[p, :, 2] = I["w_up_2"][0][:, c], I["a_up_2"][0][:, c], I["g_up_2"][0][:, c]
    per = [mu[0:dr], mu[dr:2 * dr], mu[2 * dr:3 * dr], I["w0_2"][0], I["a0_2"][0], I["k_k_2"][0], I["k_a_2"][0],
           I["r_k_2"][0].reshape(-1), I["lnx_g_2"][0], I["lnx_b_2"][0]]
    unit_cols = np.repeat(np.stack([col(a) for a in per], axis=2), WPAIRS, axis=1).reshape(P, PAIRS * WPAIRS * NPAR)
    a = np.arange(P)
    src, dst = a[:, None], a[None, :]
    masks = [src < dst, src <= dst, src < dst, src <= dst]
    for l in range(LEVELS):
        n = 1 << l
        masks.append((src // (2 * n) == dst // (2 * n)) & (src // n < dst // n))
    same = src // 64 == dst // 64
    cst = np.stack([m.astype(np.float32) for m in masks + [same]] + [same.astype(np.float32) / 64], axis=1)
    keep = np.broadcast_to((t[:2 * WIN] % WIN != 0).astype(np.float32), (P, 2 * WIN))
    return {
        "w_head": chunks(head, P).transpose(1, 0, 2, 3), "head_cols": head_cols, "pool_w": pool_w, "inv_count": inv_count,
        "w_rkv": rkv, "lora_up": up, "unit_cols": unit_cols, "window_consts": cst, "scan_keep": keep,
        "w_mix": chunks(I["w_out_2"][0], NB), "ln1": np.stack([I["ln1_g_2"][0], I["ln1_b_2"][0]]),
    }


def layouts_third(np, I):
    gu = np.concatenate([I["exp_gate_2"][0], I["exp_up_2"][0]], axis=2)
    counts = np.concatenate([np.arange(GROUPS), np.arange(EXPERTS), np.arange(OVERFLOW), P * np.arange(1, MAX_MORE + 1)])
    return {
        "w_router": np.concatenate([I["router_group_2"][0], I["router_expert_2"][0]], axis=1).reshape(KT, P, LOGITS)
        .transpose(1, 0, 2),
        "b_router": np.concatenate([I["router_group_b_2"][0], I["router_expert_b_2"][0]]),
        "counts": counts.astype(np.float32),
        "w_gu": gu.reshape(EXPERTS, KT, P, 2 * D_EXP).transpose(0, 2, 1, 3),
        "w_d": I["exp_down_2"][0].reshape(EXPERTS, 2, P, D).transpose(0, 2, 1, 3),
        "ln2": np.stack([I["ln2_g_2"][0], I["ln2_b_2"][0]]),
    }


def layouts_first(np, I):
    wi = I["fox_w_in"][0]
    return {
        "x": I["x"][0],
        "cols1": np.concatenate([col(I["c"][0]), col(I["b_ada"][0]), col(I["norm_mix"][0]), col(I["norm_mlp"][0])], axis=1),
        "w_ada": I["w_ada"][0],
        "b_ada": I["b_ada"][0],
        "w_qkv": chunks(wi[:, :QKV], QN),
        "w_f": wi[:, QKV:].reshape(KT, P, HEADS).transpose(1, 0, 2),
        "b_f": I["fox_b_f"][0],
        "qk_gain": np.stack([I["fox_q_norm"][0], I["fox_k_norm"][0]], axis=1),
        "w_o": chunks(I["fox_w_out"][0], NB),
        "w1": chunks(I["w_mlp_in"][0], P),
        "w2": I["w_mlp_out"][0].reshape(FT, P, D),
    }


def kernel(**inputs):
    import numpy as np
    import concourse.bacc as _bacc
    from concourse.bass_utils import run_bass_kernel_spmd as _run

    I = {k: np.asarray(v) for k, v in inputs.items()}
    L = {**layouts_first(np, I), **layouts_second(np, I), **layouts_third(np, I)}
    nc = _bacc.Bacc("TRN2", target_bir_lowering=False, num_devices=1)
    arrays, A = {}, {}
    for name, a in L.items():
        a = np.ascontiguousarray(a)
        arrays[f"in_{name}"] = a
        A[name] = nc.dram_tensor(f"in_{name}", a.shape, mybir.dt.from_np(a.dtype), kind="ExternalInput").ap()
    out = nc.dram_tensor("out_0", (1, S, D), F32, kind="ExternalOutput").ap()
    x_mid = nc.dram_tensor("x_mid", (S, D), F32, kind="Internal").ap()
    h_rows = nc.dram_tensor("h_rows", (S, D), F32, kind="Internal").ap()
    row_tok = nc.dram_tensor("row_tok", (ROWS, 1), I32, kind="Internal").ap()
    y_rows = nc.dram_tensor("y_rows", (ROWS, D), F32, kind="Internal").ap()
    USED.clear()
    with Scope(nc, "all") as g:
        consts = constants(nc, g)
        first_program(nc, A, x_mid, consts)
        clear_semaphores(nc)
        second_program(nc, A, x_mid, h_rows, row_tok, y_rows, out.rearrange("b s d -> (b s) d"), consts)
    r = _run(nc, [arrays], core_ids=[0])
    return r.results[0]["out_0"]
```

```python
from contextlib import ExitStack

import concourse.bass as bass
from concourse import mybir

F32 = mybir.dt.float32
BF16 = mybir.dt.bfloat16
I32 = mybir.dt.int32
U32 = mybir.dt.uint32
ALU = mybir.AluOpType
ACT = mybir.ActivationFunctionType
AX = mybir.AxisListType

P = 128
S = 1024
D = 1024
TT = S // P
KT = D // P
NB = 512
HEADS = 16
HD = D // HEADS
QKV = 3 * D
QN = 384
D_FF = 4 * D
FT = D_FF // P
EPS = 1e-6


class Scope:

    def __init__(self, nc, tag):
        self.nc, self.tag, self.stack = nc, tag, ExitStack()

    def __enter__(self):
        self.stack.__enter__()
        return self

    def __exit__(self, *a):
        return self.stack.__exit__(*a)

    def sb(self, name, shape, dt=F32):
        return self.stack.enter_context(self.nc.sbuf_tensor(f"{self.tag}_{name}", shape, dt))

    def ps(self, name, shape, dt=F32):
        return self.stack.enter_context(self.nc.psum_tensor(f"{self.tag}_{name}", shape, dt))

    def sem(self, name):
        handle = self.stack.enter_context(self.nc.semaphore(f"{self.tag}_{name}"))
        USED.append(handle)
        return handle


USED = []


def clear_semaphores(nc):
    numbers = sorted({handle.num for handle in USED})
    USED.clear()
    with nc.Block() as block:
        @block.gpsimd
        def _(pool):
            at = 0
            while at < len(numbers):
                end = at
                while end + 1 < len(numbers) and numbers[end + 1] == numbers[end] + 1:
                    end += 1
                pool.sem_clear(range(numbers[at], numbers[end] + 1))
                at = end + 1


def constants(nc, scope):
    ident = scope.sb("ident", [P, P])
    ones = scope.sb("ones", [P, P])
    cumul = scope.sb("cumul", [P, P])
    ident16 = scope.sb("ident16", [P, P], BF16)
    future16 = scope.sb("future16", [P, P], BF16)
    with Scope(nc, "cst") as c, nc.Block() as block:
        cleared = c.sem("cleared")
        built = c.sem("built")

        @block.gpsimd
        def _(pool):
            nc.gpsimd.memset(ident[:], 0.0).then_inc(cleared, 1)
            nc.gpsimd.memset(ones[:], 1.0).then_inc(cleared, 1)
            nc.gpsimd.memset(cumul[:], 1.0).then_inc(cleared, 1)
            nc.gpsimd.memset(ident16[:], 0.0).then_inc(cleared, 1)
            nc.gpsimd.memset(future16[:], 0.0).then_inc(cleared, 1)
            pool.wait_ge(cleared, 5)
            for m in (ident, ident16):
                nc.gpsimd.affine_select(out=m[:], in_=m[:], compare_op=ALU.not_equal, fill=1.0, base=0,
                                        pattern=[[-1, P]], channel_multiplier=1).then_inc(built, 1)
            nc.gpsimd.affine_select(out=cumul[:], in_=cumul[:], compare_op=ALU.is_ge, fill=0.0, base=0,
                                    pattern=[[1, P]], channel_multiplier=-1).then_inc(built, 1)
            nc.gpsimd.affine_select(out=future16[:], in_=future16[:], compare_op=ALU.is_ge, fill=-1e30, base=0,
                                    pattern=[[-1, P]], channel_multiplier=1).then_inc(built, 1)
            pool.wait_ge(built, 4)
    return ident, ones, cumul, ident16, future16


def stage_modulation(nc, x, cols1, w_ada, xres, modc, cols, silu, ones):
    with Scope(nc, "mod") as s:
        wa = s.sb("wa", [P, 2, 2, 2 * D])
        acc = s.sb("acc", [P, 2 * D])
        pmod = s.ps("pmod", [P, 2 * KT])
        work = s.sb("work", [P, 2, KT])
        cols_in, x_in = s.sem("cols_in"), s.sem("x_in")
        w_in = [s.sem("w_in0"), s.sem("w_in1")]
        w_used, silu_st, silu_exp, mm_mod, finished = (s.sem(n) for n in "w_used silu_st silu_exp mm_mod finished".split())
        with nc.Block() as block:
            @block.sync
            def _(sp):
                sp.dma_start(cols[:], cols1).then_inc(cols_in, 16)
                for g in range(KT // 2):
                    if g >= 2:
                        sp.wait_ge(w_used, 2 * g - 2)
                    sp.dma_start(wa[:, g % 2, :, :], w_ada[2 * g * P:(2 * g + 2) * P, 0:2 * D].rearrange("(k p) c -> p k c", p=P)
                                 ).then_inc(w_in[g % 2], 16)

            @block.scalar
            def _(act):
                act.wait_ge(cols_in, 16)
                nc.scalar.activation(work[:, 0, :], cols[:, 0:KT], ACT.Exp, scale=-1.0).then_inc(silu_exp, 1)
                act.wait_ge(w_in[1], 16)
                act.dma_start(xres[:], x.rearrange("(t p) d -> p t d", p=P)).then_inc(x_in, 16)
                act.wait_ge(x_in, 16)

            @block.vector
            def _(dve):
                dve.wait_ge(silu_exp, 1)
                nc.vector.tensor_scalar_add(work[:, 1, :], work[:, 0, :], 1.0).then_inc(silu_st, 1)
                dve.wait_ge(silu_st, 1)
                nc.vector.reciprocal(work[:, 0, :], work[:, 1, :]).then_inc(silu_st, 1)
                dve.wait_ge(silu_st, 2)
                nc.vector.tensor_tensor(silu[:], work[:, 0, :], cols[:, 0:KT], ALU.mult).then_inc(silu_st, 1)
                dve.wait_ge(silu_st, 3)
                for k in range(KT):
                    g = k // 2
                    dve.wait_ge(w_in[g % 2], 16 * (g // 2 + 1))
                    if k == 0:
                        nc.vector.tensor_scalar(acc[:], wa[:, 0, 0, :], silu[:, 0:1], None, ALU.mult).then_inc(w_used, 1)
                    else:
                        dve.wait_ge(w_used, k)
                        nc.vector.scalar_tensor_tensor(out=acc[:], in0=wa[:, g % 2, k % 2, :], scalar=silu[:, k:k + 1],
                                                       in1=acc[:], op0=ALU.mult, op1=ALU.add).then_inc(w_used, 1)
                dve.wait_ge(mm_mod, 1)
                modulation_columns(nc, dve, pmod, cols, 0, modc, finished)

            @block.tensor
            def _(pe):
                pe.wait_ge(w_used, KT)
                column_sums(nc, acc, 0, pmod, ones).then_inc(mm_mod, 1)


def column_sums(nc, acc, first, pmod, ones):
    for m in range(2 * KT):
        last = nc.tensor.matmul(pmod[:, m:m + 1], lhsT=acc[:, first + m * P:first + (m + 1) * P],
                                rhs=ones[:, 0:1], start=True, stop=True)
    return last


def modulation_columns(nc, dve, pmod, cols, n, modc, finished):
    bias, norm = KT + 3 * n * KT, KT + (6 + n) * KT
    nc.vector.tensor_tensor(modc[:, n, 1, :], pmod[:, 0:KT], cols[:, bias:bias + KT], ALU.add).then_inc(finished, 1)
    nc.vector.tensor_tensor(modc[:, n, 0, :], pmod[:, KT:2 * KT], cols[:, bias + KT:bias + 2 * KT], ALU.add).then_inc(finished, 1)
    dve.wait_ge(finished, 2)
    nc.vector.scalar_tensor_tensor(out=modc[:, n, 0, :], in0=modc[:, n, 0, :], scalar=1.0, in1=cols[:, norm:norm + KT],
                                   op0=ALU.add, op1=ALU.mult).then_inc(finished, 1)
    dve.wait_ge(finished, 3)


def stage_modulation_rest(nc, acc, b_ada, cols, modc, gates, ones):
    with Scope(nc, "modr") as s:
        brow = s.sb("brow", [P, 2, D])
        pmod = s.ps("pmod", [P, 2 * KT])
        pgate = s.ps("pgate", [P, 4, NB])
        brow_in, mm_mod, mm_gate, finished, gated = (s.sem(n) for n in "brow_in mm_mod mm_gate finished gated".split())
        with nc.Block() as block:
            @block.sync
            def _(sp):
                for g, off in enumerate((2 * D, 5 * D)):
                    sp.dma_start(brow[:, g, :], b_ada[off:off + D].partition_broadcast(P)).then_inc(brow_in, 16)

            @block.tensor
            def _(pe):
                column_sums(nc, acc, D, pmod, ones).then_inc(mm_mod, 1)
                for g, off in enumerate((0, 3 * D)):
                    for h in range(2):
                        last = nc.tensor.matmul(pgate[:, 2 * g + h, :], lhsT=ones[:],
                                                rhs=acc[:, off + h * NB:off + (h + 1) * NB], start=True, stop=True)
                last.then_inc(mm_gate, 1)

            @block.vector
            def _(dve):
                dve.wait_ge(mm_mod, 1)
                modulation_columns(nc, dve, pmod, cols, 1, modc, finished)
                dve.wait_ge(mm_gate, 1)
                dve.wait_ge(brow_in, 32)
                for g in range(2):
                    nc.vector.tensor_tensor(gates[:, g, :], pgate[:, 2 * g:2 * g + 2, :].rearrange("p a b -> p (a b)"),
                                            brow[:, g, :], ALU.add).then_inc(gated, 1)
                dve.wait_ge(gated, 2)


def stage_norm(nc, tag, xres, hT, modc, ident):
    with Scope(nc, tag) as s:
        xn = s.sb("xn", [P, TT, D])
        ss = s.sb("ss", [P, TT])
        st = s.sb("st", [P, 3, TT])
        pt = s.ps("pt", [P, 4, NB])
        sq_done, var_ok, root, rstd_ok = s.sem("sq_done"), s.sem("var_ok"), s.sem("root"), s.sem("rstd_ok")
        xn_done, turned, taken_a, taken_v = s.sem("xn_done"), s.sem("turned"), s.sem("taken_a"), s.sem("taken_v")
        HT = TT // 2
        with nc.Block() as block:
            @block.scalar
            def _(act):
                def shift_scale(half, c, bank):
                    nc.scalar.activation(hT[:, c, half * NB:(half + 1) * NB], pt[:, bank, :], ACT.Identity,
                                         scale=modc[:, 0, c:c + 1], bias=modc[:, 1, c:c + 1]).then_inc(taken_a, 1)

                for half in range(2):
                    for t in range(half * HT, (half + 1) * HT):
                        nc.scalar.activation(xn[:, t, :], xres[:, t, :], ACT.Square,
                                             accum_out=ss[:, t:t + 1]).then_inc(sq_done, 1)
                    act.wait_ge(var_ok, half + 1)
                    hs = slice(half * HT, (half + 1) * HT)
                    nc.scalar.activation(st[:, 1, hs], st[:, 0, hs], ACT.Sqrt).then_inc(root, 1)
                for c in range(KT):
                    act.wait_ge(turned, c + 1)
                    shift_scale(0, c, c % 4)
                for c in range(1, KT, 2):
                    act.wait_ge(turned, KT + c + 1)
                    shift_scale(1, c, c % 4)
                act.wait_ge(taken_a, KT + KT // 2)

            @block.vector
            def _(dve):
                for half in range(2):
                    hs = slice(half * HT, (half + 1) * HT)
                    dve.wait_ge(sq_done, (half + 1) * HT)
                    nc.vector.tensor_scalar(st[:, 0, hs], ss[:, hs], 1.0 / D, EPS, ALU.mult, ALU.add).then_inc(var_ok, 1)
                    dve.wait_ge(root, half + 1)
                    nc.vector.reciprocal(st[:, 2, hs], st[:, 1, hs]).then_inc(rstd_ok, 1)
                    dve.wait_ge(rstd_ok, half + 1)
                    for t in range(half * HT, (half + 1) * HT):
                        nc.vector.tensor_scalar(xn[:, t, :], xres[:, t, :], st[:, 2, t:t + 1], None,
                                                ALU.mult).then_inc(xn_done, 1)
                for c in range(0, KT, 2):
                    dve.wait_ge(turned, KT + c + 1)
                    nc.vector.tensor_scalar(hT[:, c, NB:2 * NB], pt[:, c % 4, :], modc[:, 0, c:c + 1],
                                            modc[:, 1, c:c + 1], ALU.mult, ALU.add).then_inc(taken_v, 1)
                dve.wait_ge(taken_v, KT // 2)

            @block.tensor
            def _(pe):
                for half in range(2):
                    pe.wait_ge(xn_done, HT * (half + 1))
                    for c in range(KT):
                        before = half * KT + c - 4
                        if 0 <= before < KT:
                            pe.wait_ge(taken_a, before + 1)
                        elif before >= KT and c % 2:
                            pe.wait_ge(taken_a, KT + (before - KT) // 2 + 1)
                        elif before >= KT:
                            pe.wait_ge(taken_v, (before - KT) // 2 + 1)
                        for j in range(HT):
                            last = nc.tensor.transpose(pt[:, c % 4, j * P:(j + 1) * P],
                                                       xn[:, HT * half + j, c * P:(c + 1) * P], ident[:])
                        last.then_inc(turned, 1)


def stage_qkv(nc, hT, w_qkv, w_f, bf_row, qkv, ss, neg_f, cumul, ones):
    CH = QKV // QN
    HPC = QN // HD
    with Scope(nc, "qkv") as s:
        wq = s.sb("wq", [P, 2, KT, QN])
        wf = s.sb("wf", [P, KT, HEADS])
        fb = s.sb("fb", [P, HEADS])
        lf = s.sb("lf", [P, 4, TT, HEADS])
        sq = s.sb("sq", [P, 2, QN])
        pq = s.ps("pq", [P, 4, NB])
        pf = s.ps("pf", [P, TT, HEADS])
        pc = s.ps("pc", [P, TT, HEADS])
        w_in = [s.sem("w_in0"), s.sem("w_in1")]
        wf_in, mm, copied, squared, summed = s.sem("wf_in"), s.sem("mm"), s.sem("copied"), s.sem("squared"), s.sem("summed")
        mm_f, f_st, f_act, f_lin, mm_c, ends = s.sem("mm_f"), s.sem("f_st"), s.sem("f_act"), s.sem("f_lin"), s.sem("mm_c"), s.sem("ends")
        with nc.Block() as block:
            @block.sync
            def _(sp):
                sp.dma_start(wf[:], w_f).then_inc(wf_in, 16)
                sp.dma_start(fb[:], bf_row.partition_broadcast(P)).then_inc(wf_in, 16)
                for n in range(2):
                    sp.dma_start(wq[:, n, :, :], w_qkv[n]).then_inc(w_in[n], 16)
                with sp.Fori(1, CH // 2) as i:
                    for n in range(2):
                        sp.wait_ge(mm, (2 * i + n - 1) * TT)
                        sp.dma_start(wq[:, n, :, :], w_qkv[2 * i + n]).then_inc(w_in[n], 16)

            @block.tensor
            def _(pe):
                pe.wait_ge(wf_in, 32)
                for t in range(TT):
                    for k in range(KT):
                        last = nc.tensor.matmul(pf[:, t, :], lhsT=hT[:, k, t * P:(t + 1) * P], rhs=wf[:, k, :],
                                                start=(k == 0), stop=(k == KT - 1))
                last.then_inc(mm_f, 1)
                with pe.Fori(0, CH // 2) as i:
                    for n in range(2):
                        pe.wait_ge(w_in[n], 16 * i + 16)
                        for t in range(TT):
                            b = t % 4
                            pe.wait_ge(copied, (2 * i + n) * TT + t + 1)
                            for k in range(KT):
                                last = nc.tensor.matmul(pq[:, b, 0:QN], lhsT=hT[:, k, t * P:(t + 1) * P],
                                                        rhs=wq[:, n, k, :], start=(k == 0), stop=(k == KT - 1))
                            last.then_inc(mm, 1)
                pe.wait_ge(f_st, 1)
                for t in range(TT):
                    for j in range(t + 1):
                        last = nc.tensor.matmul(pc[:, t, :], lhsT=(cumul if j == t else ones)[:], rhs=lf[:, 3, j, :],
                                                start=(j == 0), stop=(j == t))
                last.then_inc(mm_c, 1)

            @block.scalar
            def _(act):
                act.wait_ge(f_lin, 3)
                nc.scalar.activation(lf[:, 2, :, :], lf[:, 1, :, :], ACT.Exp).then_inc(f_act, 1)
                act.wait_ge(f_act, 1)
                nc.scalar.activation(lf[:, 1, :, :], lf[:, 2, :, :], ACT.Ln, bias=1.0).then_inc(f_act, 1)
                with act.Fori(0, CH // 2) as i:
                    for n in range(2):
                        for t in range(TT):
                            m = (2 * i + n) * TT + t
                            act.wait_ge(copied, m + 5)
                            act.wait_ge(summed, m + 1)
                            nc.scalar.activation(sq[:, t % 2, :], qkv[:, t, bass.ds((2 * i + n) * QN, QN)],
                                                 ACT.Square).then_inc(squared, 1)

            @block.vector
            def _(dve):
                dve.sem_inc(copied, 4)
                dve.sem_inc(summed, 2)
                dve.wait_ge(mm_f, 1)
                nc.vector.tensor_tensor(lf[:, 0, :, :], pf[:], fb[:].unsqueeze(1).to_broadcast([P, TT, HEADS]),
                                        ALU.add).then_inc(f_lin, 1)
                dve.wait_ge(f_lin, 1)
                nc.vector.tensor_scalar(lf[:, 2, :, :], lf[:, 0, :, :], -1.0, None, ALU.mult).then_inc(f_lin, 1)
                dve.wait_ge(f_lin, 2)
                nc.vector.tensor_tensor(lf[:, 1, :, :], lf[:, 0, :, :], lf[:, 2, :, :], ALU.min).then_inc(f_lin, 1)
                dve.wait_ge(f_act, 2)
                nc.vector.scalar_tensor_tensor(out=lf[:, 3, :, :], in0=lf[:, 0, :, :], scalar=0.0,
                                               in1=lf[:, 1, :, :], op0=ALU.min, op1=ALU.subtract).then_inc(f_st, 1)
                with dve.Fori(0, CH // 2) as i:
                    for n in range(2):
                        for t in range(TT):
                            m = (2 * i + n) * TT + t
                            dve.wait_ge(mm, m + 1)
                            nc.vector.tensor_copy(qkv[:, t, bass.ds((2 * i + n) * QN, QN)],
                                                  pq[:, t % 4, 0:QN]).then_inc(copied, 1)
                            dve.wait_ge(squared, m + 1)
                            nc.vector.tensor_reduce(ss[:, t, bass.ds((2 * i + n) * HPC, HPC)],
                                                    sq[:, t % 2, :].rearrange("p (h d) -> p h d", d=HD),
                                                    AX.X, ALU.add).then_inc(summed, 1)
                dve.wait_ge(copied, CH * TT + 4)
                dve.wait_ge(summed, CH * TT + 2)
                dve.wait_ge(mm_c, 1)
                nc.vector.tensor_scalar(neg_f[:], pc[:], -1.0, None, ALU.mult).then_inc(ends, 1)
                dve.wait_ge(ends, 1)


def stage_attention(nc, qkv, ss, neg_f, qk_gain, o_all, w_ada, silu, ada_sum, ident, ident16, future16):
    HA = HD + 1
    TURN_AT = 4
    FIRST_ADA = 2
    with Scope(nc, "att") as s:
        norm = s.sb("norm", [P, 3, TT, 2 * HEADS])
        qk = s.sb("qk", [P, 2, TT, HA])
        qkT = s.sb("qkT", [HA, 2, 2, S])
        gain = s.sb("gain", [HA, 2])
        gq = s.sb("gq", [HA, 3])
        prob = s.sb("prob", [P, 2, S])
        pT = s.sb("pT", [P, 4, NB])
        nmax = s.sb("nmax", [P, 2, TT])
        rsum = s.sb("rsum", [P, 2, TT])
        rinv = s.sb("rinv", [P, TT])
        logit = s.ps("logit", [P, 4, NB])
        turn = s.ps("turn", [P, 2, NB])
        po = s.ps("po", [P, 2, TT * HD])
        wa = s.sb("wa", [P, 2, D])
        wa_in = [s.sem("wa_in0"), s.sem("wa_in1")]
        scaled, wa_used, ada_added, go_sp, go_pool = s.sem("scaled"), s.sem("wa_used"), s.sem("ada_added"), s.sem("go_sp"), s.sem("go_pool")
        gain_in, prep, root, set_up = s.sem("gain_in"), s.sem("prep"), s.sem("root"), s.sem("set_up")
        staged, turned, left, scored = s.sem("staged"), s.sem("turned"), s.sem("left"), s.sem("scored")
        maxed, exped, ov, o_left, inv = s.sem("maxed"), s.sem("exped"), s.sem("ov"), s.sem("o_left"), s.sem("inv")

        def p_rounds(i):
            return (i + 4) // 4

        def p_round(i, r=0):
            return sum(p_rounds(j) for j in range(i)) + r

        ROUNDS = 4 + p_round(TT)
        K_ROUND = p_round(TURN_AT + 1)

        def round_at(h, i, r, last):
            return 4 + h * ROUNDS + p_round(i, r) + (4 if i > TURN_AT and not last else 0)

        def k_round(h, r):
            return 4 + (h - 1) * ROUNDS + K_ROUND + r if not (isinstance(h, int) and h == 0) else r

        def each_head(eng, body):
            body(0, 0, True, False)
            with eng.Fori(0, HEADS // 2 - 1) as g:
                body(2 * g + 1, 1, False, False)
                body(2 * g + 2, 0, False, False)
            body(HEADS - 1, 1, False, True)

        with nc.Block() as block:
            @block.sync
            def _(sp):
                sp.dma_start(gq[0:HD, 0:2], qk_gain).then_inc(gain_in, 16)
                sp.sem_inc(wa_used, 2)
                with sp.Fori(0, KT) as k:
                    for c in range(4):
                        sp.wait_ge(wa_used, 4 * k + c + 1)
                        sp.sem_inc(go_sp, 1)
                        sp.dma_start(wa[:, c % 2, :], w_ada[bass.ds(k * P, P), (2 + c) * D:(3 + c) * D]).then_inc(wa_in[c % 2], 16)

            @block.vector
            def _(dve):
                nc.vector.memset(gq[:, 2:3], HD ** -0.5).then_inc(prep, 1)
                nc.vector.memset(gain[:], 1.0).then_inc(prep, 1)
                nc.vector.tensor_scalar(norm[:, 0, :, :], ss[:, :, 0:2 * HEADS], 1.0 / HD, EPS, ALU.mult,
                                        ALU.add).then_inc(prep, 1)
                dve.wait_ge(gain_in, 16)
                dve.wait_ge(prep, 3)
                nc.vector.scalar_tensor_tensor(out=gain[0:HD, 0:1], in0=gq[0:HD, 0:1], scalar=gq[0:HD, 1:2],
                                               in1=gq[0:HD, 2:3], op0=ALU.mult, op1=ALU.mult).then_inc(set_up, 1)
                dve.wait_ge(root, 1)
                nc.vector.reciprocal(norm[:, 2, :, :], norm[:, 1, :, :]).then_inc(set_up, 1)
                dve.wait_ge(set_up, 2)
                dve.sem_inc(o_left, 1)

                def take_qk(h, odd):
                    for r in range(4):
                        dve.wait_ge(turned, k_round(h, r) + 1)
                        half = slice((r % 2) * NB, (r % 2 + 1) * NB)
                        if r < 2:
                            ins = nc.vector.tensor_copy(qkT[:, odd, 0, half], turn[0:HA, r % 2, :])
                        else:
                            ins = nc.vector.tensor_scalar(qkT[:, odd, 1, half], turn[0:HA, r % 2, :], gain[:, 0:1], None,
                                                          ALU.mult)
                        ins.then_inc(left, 1)

                def row_max(h, odd, i):
                    dve.wait_ge(scored, h * TT + i + 1)
                    b = 2 * (i % 2)
                    nc.vector.tensor_reduce(nmax[:, odd, i:i + 1],
                                            logit[:, b:b + 2, :].rearrange("p a b -> p (a b)")[:, 0:(i + 1) * P],
                                            AX.X, ALU.max, negate=True).then_inc(maxed, 1)

                def head_out(h, odd):
                    dve.wait_ge(exped, h * TT + TT)
                    dve.wait_ge(o_left, h + 1)
                    nc.vector.reciprocal(rinv[:], rsum[:, odd, :]).then_inc(inv, 1)
                    dve.wait_ge(inv, h + 1)
                    dve.wait_ge(ov, h * TT + TT)
                    nc.vector.tensor_tensor(o_all[:, :, bass.ds(h * HD, HD)],
                                            po[:, odd, :].rearrange("p (t d) -> p t d", d=HD),
                                            rinv[:].unsqueeze(2).to_broadcast([P, TT, HD]), ALU.mult).then_inc(o_left, 1)

                def body(h, odd, first, last):
                    for i in range(TT):
                        if i + 1 < TT:
                            row_max(h, odd, i + 1)
                        elif not last:
                            row_max(h + 1, 1 - odd, 0)
                        for r in range(p_rounds(i)):
                            n = round_at(h, i, r, last)
                            w = min(4, i + 1 - 4 * r) * P
                            dve.wait_ge(turned, n + 1)
                            nc.vector.tensor_copy(pT[:, p_round(i, r) % 4, 0:w], turn[:, p_round(i, r) % 2, 0:w]).then_inc(left, 1)
                        if i == 1 and not first:
                            head_out(h - 1, 1 - odd)
                        if i == TURN_AT and not last:
                            take_qk(h + 1, 1 - odd)

                take_qk(0, 0)
                row_max(0, 0, 0)
                each_head(dve, body)
                head_out(HEADS - 1, 1)
                dve.wait_ge(o_left, HEADS + 1)

            @block.scalar
            def _(act):
                act.wait_ge(prep, 3)
                nc.scalar.activation(norm[:, 1, :, :], norm[:, 0, :, :], ACT.Sqrt).then_inc(root, 1)

                def body(h, odd, first, last):
                    for i in range(TT):
                        act.wait_ge(maxed, h * TT + i + 1)
                        if i >= 2:
                            act.wait_ge(turned, round_at(h, i - 2, p_rounds(i - 2) - 1, last) + 1)
                        elif not first:
                            j = TT - 2 + i
                            act.wait_ge(turned, round_at(h - 1, j, p_rounds(j) - 1, False) + 1)
                        b = 2 * (i % 2)
                        nc.scalar.activation(prob[:, i % 2, 0:(i + 1) * P],
                                             logit[:, b:b + 2, :].rearrange("p a b -> p (a b)")[:, 0:(i + 1) * P],
                                             ACT.Exp, bias=nmax[:, odd, i:i + 1],
                                             accum_out=rsum[:, odd, i:i + 1]).then_inc(exped, 1)

                each_head(act, body)

            @block.gpsimd
            def _(pool):
                def stage(h):
                    for w in range(2):
                        nc.gpsimd.tensor_tensor(qk[:, w, :, 0:HD], qkv[:, :, bass.ds(w * D + h * HD, HD)],
                                                norm[:, 2, :, bass.ds(w * HEADS + h, 1)].to_broadcast([P, TT, HD]),
                                                ALU.mult).then_inc(staged, 1)
                    nc.gpsimd.tensor_copy(qk[:, 1, :, HD:HA], neg_f[:, :, bass.ds(h, 1)]).then_inc(staged, 1)

                nc.gpsimd.memset(qk[:], 1.0).then_inc(staged, 1)
                pool.wait_ge(staged, 1)
                pool.wait_ge(set_up, 2)
                stage(0)
                pool.wait_ge(turned, k_round(0, 3) + 1)
                stage(1)
                nc.gpsimd.memset(ada_sum[:], 0.0).then_inc(ada_added, 1)
                with pool.Fori(FIRST_ADA, FIRST_ADA + KT) as h:
                    pool.wait_ge(turned, k_round(h - 1, 3) + 1)
                    stage(h)
                    k = h - FIRST_ADA
                    for c in range(4):
                        pool.wait_ge(wa_in[c % 2], 16 * (2 * k + c // 2) + 16)
                        pool.wait_ge(ada_added, k + 1)
                        pool.sem_inc(go_pool, 1)
                        nc.gpsimd.tensor_tensor(wa[:, c % 2, :], wa[:, c % 2, :], silu[:, bass.ds(k, 1)].to_broadcast([P, D]),
                                                ALU.mult).then_inc(scaled, 1)
                        pool.wait_ge(scaled, 4 * k + c + 1)
                        part = ada_sum[:, c * D:(c + 1) * D]
                        nc.gpsimd.tensor_tensor(part, part, wa[:, c % 2, :], ALU.add).then_inc(wa_used, 1)
                    pool.wait_ge(wa_used, 4 * k + 6)
                    pool.sem_inc(ada_added, 1)
                with pool.Fori(FIRST_ADA + KT, HEADS) as h:
                    pool.wait_ge(turned, k_round(h - 1, 3) + 1)
                    stage(h)

            @block.tensor
            def _(pe):
                def turn_qk(h):
                    pe.wait_ge(staged, 3 * h + 4)
                    for r in range(4):
                        if not (isinstance(h, int) and h == 0 and r < 2):
                            pe.wait_ge(left, k_round(h, r) - 1)
                        for j in range(4):
                            last = nc.tensor.transpose(turn[0:HA, r % 2, j * P:(j + 1) * P],
                                                       qk[:, r // 2, (r % 2) * 4 + j, :], ident[:])
                        last.then_inc(turned, 1)

                def scores(h, odd, i):
                    if i == 0:
                        pe.wait_ge(left, k_round(h, 3) + 1)
                    if not (isinstance(h, int) and h == 0 and i < 2):
                        pe.wait_ge(exped, h * TT + i - 1)
                    b = 2 * (i % 2)
                    for c in range((i + 4) // 4):
                        w = min(NB, (i + 1) * P - c * NB)
                        nc.tensor.matmul(logit[:, b + c, 0:w], lhsT=qkT[:, odd, 0, i * P:(i + 1) * P],
                                         rhs=qkT[:, odd, 1, c * NB:c * NB + w], start=True, stop=c != i // 4)
                    at = (i % 4) * P
                    nc.tensor.matmul(logit[:, b + i // 4, at:at + P], lhsT=ident16[:], rhs=future16[:],
                                     start=False, stop=True).then_inc(scored, 1)

                def with_v(h, odd, i, last_head):
                    if i == 0 and not (isinstance(h, int) and h == 0):
                        pe.wait_ge(o_left, h)
                    for j in range(i + 1):
                        if j % 4 == 0:
                            pe.wait_ge(left, round_at(h, i, j // 4, last_head) + 1)
                        last = nc.tensor.matmul(po[:, odd, i * HD:(i + 1) * HD],
                                                lhsT=pT[:, p_round(i, j // 4) % 4, (j % 4) * P:(j % 4 + 1) * P],
                                                rhs=qkv[:, j, bass.ds(2 * D + h * HD, HD)], start=(j == 0), stop=(j == i))
                    last.then_inc(ov, 1)

                def body(h, odd, first, last_head):
                    for i in range(TT):
                        if i + 1 < TT:
                            scores(h, odd, i + 1)
                        elif not last_head:
                            scores(h + 1, 1 - odd, 0)
                        if i:
                            with_v(h, odd, i - 1, last_head)
                        elif not first:
                            with_v(h - 1, 1 - odd, TT - 1, False)
                        pe.wait_ge(exped, h * TT + i + 1)
                        for r in range(p_rounds(i)):
                            pe.wait_ge(left, round_at(h, i, r, last_head) - 1)
                            for j in range(4 * r, min(4 * r + 4, i + 1)):
                                last = nc.tensor.transpose(turn[:, p_round(i, r) % 2, (j % 4) * P:(j % 4 + 1) * P],
                                                           prob[:, i % 2, j * P:(j + 1) * P], ident[:])
                            last.then_inc(turned, 1)
                        if i == TURN_AT and not last_head:
                            turn_qk(h + 1)

                turn_qk(0)
                scores(0, 0, 0)
                each_head(pe, body)
                with_v(HEADS - 1, 1, TT - 1, True)


def stage_out(nc, tag, src, w, xres, gate, ident, tmp):
    with Scope(nc, tag) as s:
        sT = s.sb("sT", [P, KT, S])
        ws = s.sb("ws", [P, 2, KT, NB])
        pt = s.ps("pt", [P, 4, NB])
        py = s.ps("py", [P, 4, NB])
        w_in = [s.sem("w_in0"), s.sem("w_in1")]
        turned, taken, mm, gated, added = s.sem("turned"), s.sem("taken"), s.sem("mm"), s.sem("gated"), s.sem("added")
        with nc.Block() as block:
            @block.sync
            def _(sp):
                for n in range(2):
                    sp.dma_start(ws[:, n, :, :], w[n]).then_inc(w_in[n], 16)

            @block.scalar
            def _(act):
                for r in range(2 * KT):
                    act.wait_ge(turned, r + 1)
                    nc.scalar.copy(sT[:, r // 2, (r % 2) * NB:(r % 2 + 1) * NB], pt[:, r % 4, :]).then_inc(taken, 1)

            @block.tensor
            def _(pe):
                for r in range(2 * KT):
                    if r >= 4:
                        pe.wait_ge(taken, r - 3)
                    for j in range(4):
                        last = nc.tensor.transpose(pt[:, r % 4, j * P:(j + 1) * P],
                                                   src[:, 4 * (r % 2) + j, (r // 2) * P:(r // 2 + 1) * P], ident[:])
                    last.then_inc(turned, 1)
                pe.wait_ge(taken, 2 * KT)
                for n in range(2):
                    pe.wait_ge(w_in[n], 16)
                    for t in range(TT):
                        m = n * TT + t
                        if m >= 4:
                            pe.wait_ge(gated, m - 3)
                        for k in range(KT):
                            last = nc.tensor.matmul(py[:, m % 4, :], lhsT=sT[:, k, t * P:(t + 1) * P],
                                                    rhs=ws[:, n, k, :], start=(k == 0), stop=(k == KT - 1))
                        last.then_inc(mm, 1)

            @block.vector
            def _(dve):
                for n in range(2):
                    for t in range(TT):
                        m = n * TT + t
                        dve.wait_ge(mm, m + 1)
                        if m >= 2:
                            dve.wait_ge(added, m - 1)
                        cs = slice(n * NB, (n + 1) * NB)
                        nc.vector.tensor_tensor(tmp[:, m % 2, :], py[:, m % 4, :], gate[:, cs], ALU.mult).then_inc(gated, 1)
                        dve.wait_ge(gated, m + 1)
                        nc.vector.tensor_tensor(xres[:, t, cs], xres[:, t, cs], tmp[:, m % 2, :], ALU.add).then_inc(added, 1)
                dve.wait_ge(added, 2 * TT)


def stage_mlp(nc, hT, w1, w2, xres, gate, ident):
    with Scope(nc, "mlp") as s:
        hid = s.sb("hid", [P, FT, NB])
        w1s = s.sb("w1s", [P, 4, KT, P])
        w2s = s.sb("w2s", [P, 4, D])
        rel = s.sb("rel", [P, 2, NB])
        yT = s.sb("yT", [P, KT, NB])
        tmp = s.sb("tmp", [P, 2, NB])
        ps = s.ps("ps", [P, 8, NB])
        w1_in = [s.sem(f"w1_in{n}") for n in range(4)]
        w2_in = [s.sem(f"w2_in{n}") for n in range(4)]
        up, down, relu, squared, y_left = s.sem("up"), s.sem("down"), s.sem("relu"), s.sem("squared"), s.sem("y_left")
        turned, gated, added = s.sem("turned"), s.sem("gated"), s.sem("added")
        with nc.Block() as block:
            @block.sync
            def _(sp):
                sp.sem_inc(up, 4)
                sp.sem_inc(down, 4)
                for half in range(2):
                    with sp.Fori(0, FT // 4) as g:
                        for n in range(4):
                            sp.wait_ge(up, half * FT + 4 * g + n + 1)
                            sp.dma_start(w1s[:, n, :, :], w1[4 * g + n]).then_inc(w1_in[n], 16)
                    with sp.Fori(0, FT // 4) as g:
                        for n in range(4):
                            sp.wait_ge(down, half * FT + 4 * g + n + 1)
                            sp.dma_start(w2s[:, n, :], w2[4 * g + n]).then_inc(w2_in[n], 16)

            @block.tensor
            def _(pe):
                for half in range(2):
                    if half:
                        pe.wait_ge(gated, 8)
                    with pe.Fori(0, FT // 4) as g:
                        for n in range(4):
                            m = half * FT + 4 * g + n
                            pe.wait_ge(w1_in[n], 16 * (half * (FT // 4) + g + 1))
                            pe.wait_ge(relu, m + 1)
                            for k in range(KT):
                                last = nc.tensor.matmul(ps[:, n, :], lhsT=w1s[:, n, k, :],
                                                        rhs=hT[:, k, half * NB:(half + 1) * NB],
                                                        start=(k == 0), stop=(k == KT - 1))
                            last.then_inc(up, 1)
                    pe.wait_ge(relu, (half + 1) * FT + 4)

                    def down_group(g, first, end):
                        for n in range(4):
                            pe.wait_ge(squared, half * FT + 4 * g + n + 3)
                            pe.wait_ge(w2_in[n], 16 * (half * (FT // 4) + g + 1))
                            for c in range(KT):
                                last = nc.tensor.matmul(ps[:, c, :], lhsT=w2s[:, n, c * P:(c + 1) * P],
                                                        rhs=hid[:, 4 * g + n, :], start=first and n == 0,
                                                        stop=end and n == 3)
                            last.then_inc(down, 1)

                    down_group(0, True, False)
                    with pe.Fori(1, FT // 4 - 1) as g:
                        down_group(g, False, False)
                    down_group(FT // 4 - 1, False, True)
                    pe.wait_ge(y_left, 8 * (half + 1))
                    for r in range(8):
                        t, c0 = r // 2, 4 * (r % 2)
                        for j in range(4):
                            last = nc.tensor.transpose(ps[:, r, j * P:(j + 1) * P], yT[:, c0 + j, t * P:(t + 1) * P],
                                                       ident[:])
                        last.then_inc(turned, 1)

            @block.scalar
            def _(act):
                act.sem_inc(relu, 4)
                for half in range(2):
                    with act.Fori(0, FT // 4) as g:
                        for n in range(4):
                            m = half * FT + 4 * g + n
                            act.wait_ge(up, m + 5)
                            act.wait_ge(squared, m + 1)
                            nc.scalar.activation(rel[:, n % 2, :], ps[:, n, :], ACT.Relu).then_inc(relu, 1)
                    act.wait_ge(down, (half + 1) * FT + 4)
                    if half:
                        act.wait_ge(turned, 8)
                    for c in range(KT):
                        nc.scalar.copy(yT[:, c, :], ps[:, c, :]).then_inc(y_left, 1)

            @block.vector
            def _(dve):
                dve.sem_inc(squared, 2)
                for half in range(2):
                    if half:
                        dve.wait_ge(down, FT + 4)
                    with dve.Fori(0, FT // 4) as g:
                        for n in range(4):
                            m = half * FT + 4 * g + n
                            dve.wait_ge(relu, m + 5)
                            nc.vector.tensor_tensor(hid[:, bass.ds(4 * g + n, 1), :], rel[:, n % 2:n % 2 + 1, :],
                                                    rel[:, n % 2:n % 2 + 1, :], ALU.mult).then_inc(squared, 1)
                    for r in range(8):
                        m = half * 8 + r
                        t, cs = half * 4 + r // 2, slice((r % 2) * NB, (r % 2 + 1) * NB)
                        dve.wait_ge(turned, m + 1)
                        if m >= 2:
                            dve.wait_ge(added, m - 1)
                        nc.vector.tensor_tensor(tmp[:, m % 2, :], ps[:, r, :], gate[:, cs], ALU.mult).then_inc(gated, 1)
                        dve.wait_ge(gated, m + 1)
                        nc.vector.tensor_tensor(xres[:, t, cs], xres[:, t, cs], tmp[:, m % 2, :],
                                                ALU.add).then_inc(added, 1)
                dve.wait_ge(added, 16)


PAIRS = 6
HS = 64
NPAR = 10
MU_R, MU_K, MU_V, W0, A0, K_K, K_A, R_K, LNX_G, LNX_B = range(NPAR)
WIN = 128
WPAIRS = S // WIN // 2
LEVELS = 7
LN_EPS = 1e-5
LNX_EPS = 64e-5
ALPHA = 2.0 ** 0.25
DECAY = -0.6065306597126334


class Steps:

    def __init__(self, sem, names):
        self.sem, self.names = sem, names.split()

    def at(self, i, name):
        return i * len(self.names) + self.names.index(name) + 1


def stage_turn(nc, tag, src, dst, ident):
    with Scope(nc, tag) as s:
        pt = s.ps("pt", [P, 8, NB])
        turned, taken = s.sem("turned"), s.sem("taken")
        with nc.Block() as block:
            @block.tensor
            def _(pe):
                for r in range(2 * KT):
                    if r >= 8:
                        pe.wait_ge(taken, r - 7)
                    for j in range(4):
                        last = nc.tensor.transpose(pt[:, r % 8, j * P:(j + 1) * P],
                                                   src[:, 4 * (r % 2) + j, (r // 2) * P:(r // 2 + 1) * P], ident[:])
                    last.then_inc(turned, 1)

            @block.vector
            def _(dve):
                for r in range(2 * KT):
                    dve.wait_ge(turned, r + 1)
                    nc.vector.tensor_copy(dst[:, r // 2, (r % 2) * NB:(r % 2 + 1) * NB],
                                          pt[:, r % 8, :]).then_inc(taken, 1)
                dve.wait_ge(taken, 2 * KT)


def stage_pool(nc, xT, w_head, head_cols, pool_w, inv_count, mixT, lora_in):
    PAD = 16
    with Scope(nc, "pool") as s:
        ws = s.sb("ws", [P, 4, KT, P])
        hc = s.sb("hc", [P, 6])
        pw = s.sb("pw", [P, 2, P])
        ic = s.sb("ic", [P, 2, PAD])
        z = s.sb("z", [P, 4, PAD + S])
        acc = s.sb("acc", [P, 2, PAD + S])
        dif = s.sb("dif", [P, 2, S])
        ps = s.ps("ps", [P, 8, NB])
        w_in, c_in, mm, copied, cleared = s.sem("w_in"), s.sem("c_in"), s.sem("mm"), s.sem("copied"), s.sem("cleared")
        v, mapped, ends = s.sem("vector_step"), s.sem("mapped"), s.sem("ends")
        with nc.Block() as block:
            @block.sync
            def _(sp):
                sp.dma_start(ws[:], w_head).then_inc(w_in, 16)
                sp.dma_start(hc[:], head_cols).then_inc(c_in, 16)
                sp.dma_start(pw[:], pool_w).then_inc(c_in, 16)
                sp.dma_start(ic[:], inv_count).then_inc(c_in, 16)

            @block.tensor
            def _(pe):
                pe.wait_ge(w_in, 16)
                for n in range(4):
                    for half in range(2):
                        for k in range(KT):
                            last = nc.tensor.matmul(ps[:, 2 * n + half, :], lhsT=ws[:, n, k, :],
                                                    rhs=xT[:, k, half * NB:(half + 1) * NB],
                                                    start=(k == 0), stop=(k == KT - 1))
                    last.then_inc(mm, 1)
                pe.wait_ge(copied, 4)
                pe.wait_ge(c_in, 48)
                for n in range(2):
                    pe.wait_ge(mapped, n + 1)
                    for half in range(2):
                        last = nc.tensor.matmul(ps[:, 2 * n + half, :], lhsT=pw[:, n, :],
                                                rhs=dif[:, n, half * NB:(half + 1) * NB], start=True, stop=True)
                    last.then_inc(mm, 1)

            @block.scalar
            def _(act):
                for n in range(4):
                    act.wait_ge(mm, n + 1)
                    nc.scalar.copy(z[:, n, PAD:], ps[:, 2 * n:2 * n + 2, :].rearrange("p a b -> p (a b)")).then_inc(copied, 1)
                act.wait_ge(v, 4)
                nc.scalar.activation(lora_in[0:HS, 0, :], lora_in[0:HS, 0, :], ACT.Tanh).then_inc(ends, 1)
                nc.scalar.activation(lora_in[:, 1, :], lora_in[:, 1, :], ACT.Sigmoid).then_inc(ends, 1)
                act.wait_ge(ends, 2)

            @block.vector
            def _(dve):
                step = [0]

                def done(ins):
                    step[0] += 1
                    ins.then_inc(v, 1)
                    dve.wait_ge(v, step[0])

                nc.vector.memset(z[:, :, 0:PAD], 0.0).then_inc(cleared, 1)
                nc.vector.memset(acc[:, :, 0:PAD], 0.0).then_inc(cleared, 1)
                dve.wait_ge(cleared, 2)
                dve.wait_ge(c_in, 48)
                dve.wait_ge(copied, 4)
                for n in range(2):
                    cur = z[:, 2 + n, PAD:]
                    done(nc.vector.tensor_tensor(dif[:, 0, :], z[:, 2 + n, PAD - 1:PAD - 1 + S], cur, ALU.subtract))
                    done(nc.vector.scalar_tensor_tensor(out=lora_in[:, n, :], in0=dif[:, 0, :], scalar=hc[:, n:n + 1],
                                                        in1=cur, op0=ALU.mult, op1=ALU.add))
                for n in range(2):
                    src, dst, lag = z[:, n, :], acc[:, 0, :], 1
                    for level in range(1 + 2 * n):
                        done(nc.vector.tensor_tensor(dst[:, PAD:], src[:, PAD:], src[:, PAD - lag:PAD - lag + S], ALU.add))
                        src, dst, lag = dst, acc[:, (level + 1) % 2, :], 2 * lag
                    done(nc.vector.tensor_tensor(dst[HS:P, PAD:], src[HS:P, PAD:], src[HS:P, PAD - lag:PAD - lag + S], ALU.add))
                    done(nc.vector.tensor_copy(dst[0:HS, PAD:], src[0:HS, PAD:]))
                    done(nc.vector.tensor_tensor(src[:, PAD:2 * PAD], dst[:, PAD:2 * PAD], ic[:, n, :], ALU.mult))
                    done(nc.vector.tensor_tensor(dif[:, n, 0:PAD], src[:, PAD:2 * PAD], z[:, n, PAD:2 * PAD], ALU.subtract))
                    nc.vector.scalar_tensor_tensor(out=dif[:, n, PAD:], in0=dst[:, 2 * PAD:], scalar=hc[:, 4 + n:5 + n],
                                                   in1=z[:, n, 2 * PAD:], op0=ALU.mult, op1=ALU.subtract).then_inc(mapped, 1)
                    dve.wait_ge(mapped, n + 1)
                for n in range(2):
                    dve.wait_ge(mm, 5 + n)
                    done(nc.vector.tensor_scalar(mixT[:, n, :], ps[:, 2 * n:2 * n + 2, :].rearrange("p a b -> p (a b)"),
                                                 hc[:, 2 + n:3 + n], None, ALU.mult))


def stage_rwkv(nc, xT, w_rkv, lora_up, unit_cols, consts, scan_keep, lora_in, mixT, ident):
    UT = 2 * WIN
    UNITS = PAIRS * WPAIRS
    TOP = LEVELS - 1
    with Scope(nc, "rwkv") as s:
        ws = s.sb("ws", [P, 3, KT, P])
        up = s.sb("up", [P, 3, P])
        par_all = s.sb("par_all", [P, UNITS * NPAR])
        par = s.sb("par", [P, NPAR + 1])
        par_y = s.sb("par_y", [P, 2])
        cst = s.sb("cst", [P, 4 + LEVELS + 2, P])
        causal = cst[:, 0:4, :].rearrange("p a b -> p (a b)")
        level = [cst[:, 4 + n, :] for n in range(LEVELS)]
        head_sum, head_mean = cst[:, 4 + LEVELS, :], cst[:, 5 + LEVELS, :]
        keep = s.sb("keep", [P, UT])
        Z = s.sb("Z", [P, 3, UT + 1])
        rkv = s.sb("rkv", [P, 3, UT])
        R, K, V = (rkv[:, n, :] for n in range(3))
        T0, LW, L, LM, SA, AG, RK, BON, KK, SQ, NR, EP, EN, EX, Y, YC, YS = (
            s.sb(n, [P, UT]) for n in "T0 LW L LM SA AG RK BON KK SQ NR EP EN EX Y YC YS".split())
        ends = s.sb("ends", [P, 3])
        fac_log = s.sb("fac_log", [P, 2])
        fac_exp = s.sb("fac_exp", [P, 2])
        fac_in = s.sb("fac_in", [P, 1])
        AR = s.sb("AR", [P, 2, 2, WIN])
        KB = s.sb("KB", [P, 2, 2, WIN])
        tm = s.sb("tm", [P, 2, 4, P])
        GM = s.sb("GM", [P, 4, 4, WIN])
        ML = s.sb("ML", [P, 3, 4, WIN])
        TI = s.sb("TI", [P, 4, WIN])
        TX = s.sb("TX", [P, 4, WIN])
        XS = s.sb("XS", [P, 4, WIN])
        AW = s.sb("AW", [P, 4, 2, HS])
        GH = s.sb("GH", [P, 4, 2, HS])
        QT = s.sb("QT", [P, 2, WIN])
        ZT = s.sb("ZT", [P, 2, HS])
        ST = s.sb("ST", [P, 2, HS])
        STF = s.sb("STF", [P, HS])
        ps = s.ps("ps", [P, 8, NB])
        mix_flat = mixT[:].rearrange("p k t -> p (k t)")

        w_in = [s.sem("w_in_r"), s.sem("w_in_k"), s.sem("w_in_v")]
        up_in, c_in, cleared, zeroed = s.sem("up_in"), s.sem("c_in"), s.sem("cleared"), s.sem("zeroed")
        passed, state_here = s.sem("passed"), s.sem("state_here")
        pe_a = Steps(s.sem("pe_make"), "w a k r kk_sum v g")
        act_a = Steps(s.sem("act_make"), "w a k kk_sq ep en r ex fac root v g")
        dve_a = Steps(s.sem("dve_make"), "par one_ka lw scan k_d k kk lm lx ends fac ends_on ag k2 sq_max r_d r inv kkn b A B K "
                      "v_d v carry rk R rk2 fac_in")
        pe_w = Steps(s.sem("pe_win"), "turn0 turn1 gram0 gram1 gram2 gram3 ak_v ti0 " +
                     " ".join(f"x{l}{' bonus' if l == 5 else ''} t{l} u{l}" for l in range(1, TOP)) + f" x{TOP} u{TOP} gh q z e0 y0 e1 y1")
        act_w = Steps(s.sem("act_win"), "tm0 tm1 a_tm w_tm ti0 " + " ".join(f"x{l}" for l in range(1, LEVELS)) + " gh z y0 y1")
        dve_w = Steps(s.sem("dve_win"), "gm0 gm1 gm2 gm3 ab0 tx0 " + " ".join(f"ti{l} tx{l}" for l in range(1, TOP)) +
                      f" bon tx{TOP} stf0 q st0 stf1 st1")
        pool_w = Steps(s.sem("pool_win"), " ".join(f"m{l}" for l in range(1, LEVELS)))
        pe_y = Steps(s.sem("pe_norm"), "mean var")
        act_y = Steps(s.sem("act_norm"), "y_sq y_root")
        dve_y = Steps(s.sem("dve_norm"), "y_c y_par y_eps y_inv y_n y_gb y_b y_out")

        def four():
            return [(2 * w + h, w, h) for w in range(2) for h in range(2)]

        def wait(eng, steps, unit, name):
            if not (isinstance(unit, int) and unit < 0):
                eng.wait_ge(steps.sem, steps.at(unit, name))

        def each_unit(eng, body):
            def one(p, wp, prev=True, nxt=True):
                last = isinstance(wp, int) and wp == WPAIRS - 1
                body(p * WPAIRS + wp, 0 if last else (wp + 1) * UT, p + 1 if last and nxt else None, prev, True, nxt)

            body(-1, 0, 0, False, False, True)
            one(0, 0, prev=False)
            with eng.Fori(1, WPAIRS - 1) as wp:
                one(0, wp)
            one(0, WPAIRS - 1)
            with eng.Fori(1, PAIRS - 1) as p:
                with eng.Fori(0, WPAIRS - 1) as wp:
                    one(p, wp)
                one(p, WPAIRS - 1)
            with eng.Fori(0, WPAIRS - 1) as wp:
                one(PAIRS - 1, wp)
            one(PAIRS - 1, WPAIRS - 1, nxt=False)
            body(UNITS, 0, None, True, False, False)

        with nc.Block() as block:
            @block.sync
            def _(sp):
                sp.dma_start(par_all[:], unit_cols).then_inc(c_in, 16)
                sp.dma_start(up[:], lora_up[0]).then_inc(up_in, 16)
                for n in (1, 0, 2):
                    sp.dma_start(ws[:, n, :, :], w_rkv[0][:, n, :, :]).then_inc(w_in[n], 16)
                sp.dma_start(cst[:], consts).then_inc(c_in, 16)
                sp.dma_start(keep[:], scan_keep).then_inc(c_in, 16)
                with sp.Fori(1, PAIRS) as p:
                    for n in (1, 0, 2):
                        sp.wait_ge(pe_a.sem, pe_a.at((p - 1) * WPAIRS + WPAIRS - 1, "rkv"[n]))
                        sp.sem_inc(passed, 1)
                        sp.dma_start(ws[:, n, :, :], w_rkv[p][:, n, :, :]).then_inc(w_in[n], 16)
                    sp.wait_ge(pe_a.sem, pe_a.at((p - 1) * WPAIRS + WPAIRS - 1, "g"))
                    sp.sem_inc(passed, 1)
                    sp.dma_start(up[:], lora_up[p]).then_inc(up_in, 16)

            @block.tensor
            def _(pe):
                A_BANK, B_BANK = 6, 7

                def body(q, col, new_pair, prev, win, nxt):
                    u, y = q + 1, q - 1

                    def project(n, ks, bank):
                        if not nxt:
                            return
                        if new_pair is not None and 0 in ks:
                            pe.wait_ge(w_in[n], 16 * new_pair + 16)
                        for k in ks:
                            last = nc.tensor.matmul(ps[:, bank, 0:UT], lhsT=ws[:, n, k, :], rhs=xT[:, k, bass.ds(col, UT)],
                                                    start=(k == 0), stop=(k == KT - 1))
                        if KT - 1 in ks:
                            last.then_inc(pe_a.sem, 1)

                    def turn_units():
                        wait(pe, dve_a, q, "R")
                        wait(pe, dve_w, y, "st1")
                        wait(pe, act_w, y, "y1")
                        for w in range(2):
                            for n, src in enumerate((AR[:, w, 0, :], KB[:, w, 1, :], KB[:, w, 0, :],
                                                     V[:, w * WIN:(w + 1) * WIN])):
                                last = nc.tensor.transpose(ps[:, w, n * P:(n + 1) * P], src, ident[:])
                            last.then_inc(pe_w.sem, 1)

                    if win:
                        turn_units()
                        for i, w, h in four():
                            hp = slice(h * HS, (h + 1) * HS)
                            both = AR[hp, w, :, :].rearrange("p a b -> p (a b)")
                            nc.tensor.matmul(ps[:, 2 + i, 0:2 * WIN], lhsT=KB[hp, w, 1, :], rhs=both, start=True, stop=True)
                            nc.tensor.matmul(ps[:, 2 + i, 2 * WIN:4 * WIN], lhsT=KB[hp, w, 0, :], rhs=both,
                                             start=True, stop=True).then_inc(pe_w.sem, 1)
                    if prev:
                        wait(pe, act_w, y, "y1")
                        wait(pe, act_a, q if win else q - 1, "v")
                        nc.tensor.matmul(ps[:, A_BANK, 0:UT], lhsT=head_mean, rhs=Y[:], start=True,
                                         stop=True).then_inc(pe_y.sem, 1)
                    if nxt:
                        if new_pair is not None:
                            pe.wait_ge(up_in, 16 * new_pair + 16)
                        wait(pe, act_a, u - 1, "g")
                        nc.tensor.matmul(ps[:, B_BANK, 0:UT], lhsT=up[:, 0, :], rhs=lora_in[:, 0, bass.ds(col, UT)],
                                         start=True, stop=True).then_inc(pe_a.sem, 1)
                        if prev:
                            wait(pe, dve_y, y, "y_c")
                        else:
                            wait(pe, act_a, u - 1, "v")
                        nc.tensor.matmul(ps[:, A_BANK, 0:UT], lhsT=up[:, 1, :], rhs=lora_in[:, 0, bass.ds(col, UT)],
                                         start=True, stop=True).then_inc(pe_a.sem, 1)
                    if win:
                        wait(pe, act_w, q, "a_tm")
                        wait(pe, dve_w, q, "gm3")
                        for i, w, h in four():
                            last = nc.tensor.matmul(ps[:, 0, i * HS:(i + 1) * HS], lhsT=GM[:, i, 2, :],
                                                    rhs=tm[:, w, 3, h * HS:(h + 1) * HS], start=True, stop=True)
                        last.then_inc(pe_w.sem, 1)
                    if nxt:
                        wait(pe, act_a, u, "w")
                        project(1, range(0, 4), B_BANK)
                    if win:
                        wait(pe, dve_w, q, "tx0")
                        for i in range(4):
                            last = nc.tensor.transpose(ps[:, 1, i * P:(i + 1) * P], TX[:, i, :], ident[:])
                        last.then_inc(pe_w.sem, 1)
                    project(1, range(4, 6), B_BANK)

                    def while_x(l):
                        if l == 1:
                            project(1, range(6, 8), B_BANK)
                        if l == 2:
                            if prev:
                                wait(pe, act_y, y, "y_sq")
                                if nxt:
                                    wait(pe, act_a, u, "a")
                                else:
                                    wait(pe, dve_y, y, "y_c")
                                nc.tensor.matmul(ps[:, A_BANK, 0:UT], lhsT=head_mean, rhs=YS[:], start=True,
                                                 stop=True).then_inc(pe_y.sem, 1)
                            if nxt:
                                wait(pe, act_a, u, "k")
                                project(0, range(0, 2), B_BANK)
                        if l == 3:
                            project(0, range(2, 5), B_BANK)
                        if l == 4:
                            project(0, range(5, 8), B_BANK)
                        if l == 5:
                            if win:
                                if nxt:
                                    wait(pe, act_a, u, "r")
                                else:
                                    wait(pe, act_a, q, "g")
                                wait(pe, dve_a, q, "rk2")
                                nc.tensor.matmul(ps[:, B_BANK, 0:UT], lhsT=head_sum, rhs=RK[:], start=True,
                                                 stop=True).then_inc(pe_w.sem, 1)
                            if nxt:
                                wait(pe, dve_a, u, "sq_max")
                                project(2, range(0, 2), A_BANK)
                        if l == 6:
                            project(2, range(2, 5), A_BANK)

                    def while_t(l):
                        if l == 4 and nxt:
                            wait(pe, act_a, u, "kk_sq")
                            if prev:
                                wait(pe, dve_y, y, "y_eps")
                            else:
                                wait(pe, act_a, u, "a")
                            nc.tensor.matmul(ps[:, A_BANK, 0:UT], lhsT=head_sum, rhs=SQ[:], start=True,
                                             stop=True).then_inc(pe_a.sem, 1)
                        if l == 6:
                            project(2, range(5, 8), A_BANK)

                    for l in range(1, LEVELS):
                        if win:
                            wait(pe, pool_w, q, f"m{l}")
                            if l == 1:
                                wait(pe, act_w, q, "ti0")
                            else:
                                wait(pe, dve_w, q, f"ti{l - 1}")
                            for i in range(4):
                                last = nc.tensor.matmul(ps[:, 2, i * P:(i + 1) * P], lhsT=ML[:, l % 3, i, :], rhs=TI[:, i, :],
                                                        start=True, stop=True)
                            last.then_inc(pe_w.sem, 1)
                        while_x(l)
                        if win:
                            wait(pe, act_w, q, f"x{l}")
                            wait(pe, dve_w, q, f"tx{l - 1}")
                            if l < TOP:
                                for i in range(4):
                                    last = nc.tensor.matmul(ps[:, 3, i * P:(i + 1) * P], lhsT=TX[:, i, :], rhs=XS[:, i, :],
                                                            start=True, stop=True)
                                last.then_inc(pe_w.sem, 1)
                            for i in range(4):
                                last = nc.tensor.matmul(ps[:, 4, i * P:(i + 1) * P], lhsT=XS[:, i, :], rhs=TX[:, i, :],
                                                        start=True, stop=True)
                            last.then_inc(pe_w.sem, 1)
                        while_t(l)
                    if win:
                        wait(pe, dve_w, q, f"tx{TOP}")
                        wait(pe, act_w, q, "w_tm")
                        for i in range(4):
                            last = nc.tensor.matmul(ps[:, 5, i * P:(i + 1) * P], lhsT=TX[:, i, :],
                                                    rhs=AW[:, i, :, :].rearrange("p a b -> p (a b)"), start=True, stop=True)
                        last.then_inc(pe_w.sem, 1)
                    if nxt:
                        if win:
                            wait(pe, dve_w, q, "bon")
                        else:
                            wait(pe, act_a, u, "r")
                        nc.tensor.matmul(ps[:, B_BANK, 0:UT], lhsT=up[:, 2, :], rhs=lora_in[:, 1, bass.ds(col, UT)],
                                         start=True, stop=True).then_inc(pe_a.sem, 1)
                    if win:
                        wait(pe, act_w, q, "gh")
                        for i, w, h in four():
                            last = nc.tensor.matmul(ps[h * HS:(h + 1) * HS, 2, w * WIN:(w + 1) * WIN], lhsT=GH[:, i, 0, :],
                                                    rhs=GM[:, i, 1, :], start=True, stop=True)
                        last.then_inc(pe_w.sem, 1)
                        for i, w, h in four():
                            last = nc.tensor.matmul(ps[h * HS:(h + 1) * HS, 3, w * HS:(w + 1) * HS], lhsT=GH[:, i, 0, :],
                                                    rhs=tm[:, w, 1, h * HS:(h + 1) * HS], start=True, stop=True)
                        last.then_inc(pe_w.sem, 1)
                        for w in range(2):
                            e_out = [ps[h * HS:(h + 1) * HS, 4 * w, 0:HS] for h in range(2)]
                            y_out = [ps[h * HS:(h + 1) * HS, 4 * w + 1, 0:WIN] for h in range(2)]

                            def stateless(h):
                                i, hp = 2 * w + h, slice(h * HS, (h + 1) * HS)
                                nc.tensor.matmul(e_out[h], lhsT=tm[:, w, 1, hp], rhs=GH[:, i, 1, :], start=True, stop=False)
                                nc.tensor.matmul(e_out[h], lhsT=tm[:, w, 2, hp], rhs=tm[:, w, 3, hp], start=False, stop=False)
                                nc.tensor.matmul(y_out[h], lhsT=GH[:, i, 1, :], rhs=GM[:, i, 1, :], start=True, stop=False)
                                nc.tensor.matmul(y_out[h], lhsT=tm[:, w, 3, hp], rhs=GM[:, i, 3, :], start=False, stop=False)

                            for h in range(2):
                                stateless(h)
                            if w == 0:
                                wait(pe, act_w, q, "z")
                                wait(pe, dve_w, y, "st1")
                            else:
                                wait(pe, dve_w, q, "st0")
                            pe.sem_inc(state_here, 1)
                            for h in range(2):
                                hp = slice(h * HS, (h + 1) * HS)
                                last = nc.tensor.matmul(e_out[h], lhsT=ZT[hp, w, :], rhs=ST[hp, w, :], start=False, stop=True)
                            last.then_inc(pe_w.sem, 1)
                            if w == 0:
                                wait(pe, dve_w, q, "q")
                                pe.sem_inc(state_here, 1)
                            for h in range(2):
                                hp = slice(h * HS, (h + 1) * HS)
                                last = nc.tensor.matmul(y_out[h], lhsT=ST[hp, w, :], rhs=QT[hp, w, :], start=False, stop=True)
                            last.then_inc(pe_w.sem, 1)

                pe.wait_ge(c_in, 48)
                pe.wait_ge(cleared, 3)
                each_unit(pe, body)

            @block.scalar
            def _(act):
                def body(q, col, new_pair, prev, win, nxt):
                    u, y = q + 1, q - 1

                    def make(*args, **kw):
                        if nxt:
                            nc.scalar.activation(*args, **kw).then_inc(act_a.sem, 1)

                    def copy(steps, dst, src):
                        nc.scalar.copy(dst, src).then_inc(steps.sem, 1)

                    def bank(b):
                        return ps[:, b, 0:UT]

                    def x_out(l):
                        if win:
                            wait(act, pe_w, q, f"x{l}")
                            copy(act_w, XS[:].rearrange("p u t -> p (u t)"), ps[:, 2, :])

                    if win:
                        for w in range(2):
                            wait(act, pe_w, q, f"turn{w}")
                            copy(act_w, tm[:, w, :, :], ps[:, w, :].rearrange("p (a b) -> p a b", a=4))
                        wait(act, act_w, q, "tm1")
                        copy(act_w, AW[:, :, 0, :].rearrange("p (w h) d -> p w h d", w=2),
                             tm[:, :, 0, :].rearrange("p w (h d) -> p w h d", h=2))
                    if nxt:
                        wait(act, dve_a, u, "par")
                        wait(act, pe_a, u, "w")
                        make(LW[:], bank(7), ACT.Sigmoid, bias=par[:, W0:W0 + 1])
                        wait(act, pe_a, u, "a")
                        make(SA[:], bank(6), ACT.Sigmoid, bias=par[:, A0:A0 + 1])
                    if win:
                        wait(act, pe_w, q, "ak_v")
                        copy(act_w, AW[:, :, 1, :], ps[:, 0, 0:4 * HS].rearrange("p (u d) -> p u d", u=4))
                        wait(act, pe_w, q, "ti0")
                        copy(act_w, TI[:].rearrange("p u t -> p (u t)"), ps[:, 1, :])
                    x_out(1)
                    if nxt:
                        wait(act, pe_a, u, "k")
                        wait(act, dve_a, u - 1, "carry")
                        copy(act_a, Z[:, 1, 1:], bank(7))
                    if prev:
                        wait(act, dve_y, y, "y_c")
                        nc.scalar.activation(YS[:], YC[:], ACT.Square).then_inc(act_y.sem, 1)
                    x_out(2)
                    x_out(3)
                    if prev:
                        wait(act, dve_y, y, "y_eps")
                        nc.scalar.activation(YS[:], YS[:], ACT.Sqrt).then_inc(act_y.sem, 1)
                    if nxt:
                        wait(act, dve_a, u, "kk")
                        make(SQ[:], KK[:], ACT.Square)
                    x_out(4)
                    if nxt:
                        wait(act, dve_a, u, "lx")
                        make(EP[:], LM[:], ACT.Exp)
                        make(EN[:], LM[:], ACT.Exp, scale=-1.0)
                        wait(act, pe_a, u, "r")
                        copy(act_a, Z[:, 0, 1:], bank(7))
                    x_out(5)
                    if nxt:
                        make(EX[:], EX[:], ACT.Exp)
                        wait(act, dve_a, u, "fac")
                        make(fac_exp[:], fac_log[:], ACT.Exp)
                        wait(act, dve_a, u, "sq_max")
                        make(NR[:], NR[:], ACT.Sqrt)
                    x_out(6)
                    if nxt:
                        wait(act, pe_a, u, "v")
                        copy(act_a, Z[:, 2, 1:], bank(6))
                    if win:
                        wait(act, pe_w, q, "gh")
                        copy(act_w, GH[:].rearrange("p u a d -> p (u a d)"), ps[:, 5, :])
                    if nxt:
                        wait(act, pe_a, u, "g")
                        copy(act_a, mix_flat[:, bass.ds(2 * S + u * UT, UT)], bank(7))
                    if win:
                        wait(act, pe_w, q, "z")
                        copy(act_w, ZT[:].rearrange("p w d -> p (w d)"), ps[:, 3, 0:2 * HS])
                        for w in range(2):
                            wait(act, pe_w, q, f"y{w}")
                            if prev:
                                wait(act, dve_y, y, "y_c")
                            copy(act_w, Y[:, w * WIN:(w + 1) * WIN], ps[:, 4 * w + 1, 0:WIN])

                each_unit(act, body)

            @block.gpsimd
            def _(pool):
                pool.wait_ge(c_in, 48)
                with pool.Fori(0, UNITS) as q:
                    for l in range(1, LEVELS):
                        if l == 1:
                            pool.wait_ge(dve_w.sem, dve_w.at(q, "gm3"))
                        if l > 3:
                            pool.wait_ge(pe_w.sem, pe_w.at(q, f"x{l - 3}"))
                        nc.gpsimd.tensor_tensor(ML[:, l % 3, :, :], GM[:, :, 0, :],
                                                level[l].unsqueeze(1).to_broadcast([P, 4, WIN]), ALU.mult).then_inc(pool_w.sem, 1)

            @block.vector
            def _(dve):
                tt, ts, stt = nc.vector.tensor_tensor, nc.vector.tensor_scalar, nc.vector.scalar_tensor_tensor
                copy, rec = nc.vector.tensor_copy, nc.vector.reciprocal

                def windows(a):
                    return a[:].rearrange("p (w t) -> p w t", w=2)

                def col_of(n):
                    return par[:, n:n + 1]

                def body(q, col, new_pair, prev, win, nxt):
                    u, y = q + 1, q - 1

                    def make(need, ins_of, *args, **kw):
                        if nxt:
                            if need:
                                wait(dve, dve_a, u, need)
                            ins_of(*args, **kw).then_inc(dve_a.sem, 1)

                    def norm(need, ins_of, *args, **kw):
                        if prev:
                            if need:
                                wait(dve, dve_y, y, need)
                            ins_of(*args, **kw).then_inc(dve_y.sem, 1)

                    def window(need, ins_of, *args, **kw):
                        if win:
                            if need:
                                wait(dve, dve_w, q, need)
                            ins_of(*args, **kw).then_inc(dve_w.sem, 1)

                    def get(steps, unit, name, exists):
                        if exists:
                            wait(dve, steps, unit, name)

                    def t_in(l):
                        if l < TOP:
                            get(pe_w, q, f"t{l}", win)
                            window(None, tt, TI[:], ps[:, 3, :].rearrange("p (u t) -> p u t", u=4), TI[:], ALU.add)
                        get(pe_w, q, f"u{l}", win)
                        window(f"tx{l - 1}", tt, TX[:], ps[:, 4, :].rearrange("p (u t) -> p u t", u=4), TX[:], ALU.add)

                    for i in range(4):
                        get(pe_w, q, f"gram{i}", win)
                        window(None, tt, GM[:, i, :, :].rearrange("p a b -> p (a b)"), ps[:, 2 + i, :], causal, ALU.mult)
                    window("gm3", tt, TX[:], GM[:, :, 0, :], level[0].unsqueeze(1).to_broadcast([P, 4, WIN]), ALU.mult)
                    window("ab0", tt, TX[:], TX[:], ident[:].unsqueeze(1).to_broadcast([P, 4, WIN]), ALU.add)
                    get(pe_y, y, "mean", prev)
                    norm(None, tt, YC[:], Y[:], ps[:, 6, 0:UT], ALU.subtract)
                    get(act_a, u - 1, "a", nxt)
                    if nxt:
                        wait(dve, dve_a, u - 1, "fac_in")
                        make(None, copy, par[:, 0:NPAR], par_all[:, bass.ds(u * NPAR, NPAR)])
                    make("par", ts, par[:, NPAR:NPAR + 1], col_of(K_A), -1.0, 1.0, ALU.mult, ALU.add)
                    get(act_a, u, "w", nxt)
                    make(None, ts, LW[:], LW[:], DECAY, None, ALU.mult)
                    t_in(1)
                    make("lw", nc.vector.tensor_tensor_scan, L[:], keep[:], LW[:], 0.0, ALU.mult, ALU.add)
                    if prev:
                        norm("y_c", copy, par_y[:], par_all[:, bass.ds(y * NPAR + LNX_G, 2)])
                    if new_pair is not None:
                        wait(dve, dve_a, u - 1, "carry")
                        nc.vector.memset(Z[:, :, 0:1], 0.0).then_inc(zeroed, 1)
                        dve.wait_ge(zeroed, new_pair + 1)
                    get(act_a, u, "k", nxt)
                    make(None, tt, T0[:], Z[:, 1, 0:UT], Z[:, 1, 1:], ALU.subtract)
                    t_in(2)
                    make("k_d", stt, out=K, in0=T0[:], scalar=col_of(MU_K), in1=Z[:, 1, 1:], op0=ALU.mult, op1=ALU.add)
                    make("k", ts, KK[:], K, col_of(K_K), None, ALU.mult)
                    make("scan", tt, windows(LM), windows(L), windows(L)[:, :, HS - 1:HS].to_broadcast([P, 2, WIN]), ALU.subtract)
                    make("lm", tt, EX[:], LM[:], LW[:], ALU.subtract)
                    get(pe_y, y, "var", prev)
                    norm(None, ts, YS[:], ps[:, 6, 0:UT], LNX_EPS, None, ALU.add)
                    t_in(3)
                    make("lm", copy, ends[:, 1:3], windows(LM)[:, :, WIN - 1])
                    make("ends", tt, fac_log[:], ends[:, 0:2], windows(L)[:, :, HS - 1], ALU.add)
                    make("fac", copy, ends[:, 0:1], ends[:, 2:3])
                    get(act_a, u, "a", nxt)
                    make("one_ka", ts, AG[:], SA[:], col_of(K_A), col_of(NPAR), ALU.mult, ALU.add)
                    get(act_y, y, "y_root", prev)
                    norm(None, rec, YS[:], YS[:])
                    make("ag", tt, K, K, AG[:], ALU.mult)
                    t_in(4)
                    norm("y_inv", tt, YC[:], YC[:], YS[:], ALU.mult)
                    get(pe_a, u, "kk_sum", nxt)
                    make(None, ts, NR[:], ps[:, 6, 0:UT], 1e-24, None, ALU.max)
                    get(act_a, u, "r", nxt)
                    make(None, tt, T0[:], Z[:, 0, 0:UT], Z[:, 0, 1:], ALU.subtract)
                    norm("y_n", ts, YC[:], YC[:], par_y[:, 0:1], par_y[:, 1:2], ALU.mult, ALU.add)
                    t_in(5)
                    norm("y_gb", tt, YC[:], YC[:], BON[:], ALU.add)
                    make("r_d", stt, out=R, in0=T0[:], scalar=col_of(MU_R), in1=Z[:, 0, 1:], op0=ALU.mult, op1=ALU.add)
                    get(act_a, u, "root", nxt)
                    make(None, rec, NR[:], NR[:])
                    get(pe_w, q, "bonus", win)
                    get(dve_y, y, "y_b", prev)
                    window(None, tt, BON[:], ps[:, 7, 0:UT], V, ALU.mult)
                    t_in(6)
                    get(dve_a, q, "fac_in", win)
                    window(None, ts, STF[:], ST[:, 0, :], fac_in[:], None, ALU.mult)
                    make("inv", tt, KK[:], KK[:], NR[:], ALU.mult)
                    if prev:
                        gate_then_out = mix_flat[:, bass.ds(2 * S + y * UT, UT)]
                        wait(dve, act_a, y, "g")
                        norm("y_b", tt, gate_then_out, gate_then_out, YC[:], ALU.mult)
                    make("kkn", tt, SA[:], SA[:], KK[:], ALU.mult)
                    make("kkn", stt, out=AR[:, :, 0, :], in0=windows(KK), scalar=-1.0, in1=windows(EX), op0=ALU.mult, op1=ALU.mult)
                    make("b", tt, KB[:, :, 1, :], windows(SA), windows(EN), ALU.mult)
                    make("k2", tt, KB[:, :, 0, :], K.rearrange("p (w t) -> p w t", w=2), windows(EN), ALU.mult)
                    get(pe_w, q, "q", win)
                    window(None, tt, QT[:], ps[:, 2, 0:2 * WIN].rearrange("p (w t) -> p w t", w=2), AR[:, :, 1, :], ALU.add)
                    get(act_a, u, "v", nxt)
                    get(dve_w, q, "bon", win)
                    get(dve_y, y, "y_out", prev)
                    make(None, tt, T0[:], Z[:, 2, 0:UT], Z[:, 2, 1:], ALU.subtract)
                    make("v_d", stt, out=V, in0=T0[:], scalar=col_of(MU_V), in1=Z[:, 2, 1:], op0=ALU.mult, op1=ALU.add)
                    get(pe_w, q, "e0", win)
                    window("stf0", stt, out=ST[:, 1, :], in0=ps[:, 0, 0:HS], scalar=fac_in[:], in1=STF[:], op0=ALU.mult, op1=ALU.add)
                    make("v", copy, Z[:, :, 0:1], Z[:, :, UT:UT + 1])
                    make("r", tt, RK[:], R, K, ALU.mult)
                    get(dve_w, q, "q", win)
                    make("r", tt, AR[:, :, 1, :], R.rearrange("p (w t) -> p w t", w=2), windows(EP), ALU.mult)
                    make("rk", ts, RK[:], RK[:], col_of(R_K), None, ALU.mult)
                    if new_pair is not None or not nxt:
                        window("st0", nc.vector.memset, STF[:], 0.0)
                        get(pe_w, q, "e1", win)
                        window(None, nc.vector.memset, ST[:, 0, :], 0.0)
                    else:
                        window("st0", ts, STF[:], ST[:, 1, :], fac_exp[:, 0:1], None, ALU.mult)
                        get(pe_w, q, "e1", win)
                        window("stf1", stt, out=ST[:, 0, :], in0=ps[:, 4, 0:HS], scalar=fac_exp[:, 0:1], in1=STF[:], op0=ALU.mult,
                               op1=ALU.add)
                    get(act_a, u, "fac", nxt)
                    make(None, copy, fac_in[:], fac_exp[:, 1:2])

                nc.vector.memset(ends[:], 0.0).then_inc(cleared, 1)
                nc.vector.memset(ST[:], 0.0).then_inc(cleared, 1)
                nc.vector.memset(BON[:], 0.0).then_inc(cleared, 1)
                dve.wait_ge(cleared, 3)
                dve.wait_ge(c_in, 48)
                each_unit(dve, body)
                dve.wait_ge(dve_y.sem, dve_y.at(UNITS - 1, "y_out"))


def layer_norm_steps(nc, dve, src, stats, mv, g_row, b_row, n, done, root_ready, rooted):
    for c in range(2):
        done(nc.vector.bn_stats(stats[:, c, :], src[:, c * NB:(c + 1) * NB]))
    done(nc.vector.bn_aggr(mv[:, 0:2], stats[:].rearrange("p a b -> p (a b)")))
    nc.vector.tensor_scalar(mv[:, 2:3], mv[:, 1:2], LN_EPS, None, ALU.add).then_inc(root_ready, 1)
    dve.wait_ge(rooted, n + 1)
    done(nc.vector.reciprocal(mv[:, 2:3], mv[:, 2:3]))
    done(nc.vector.tensor_scalar(src, src, mv[:, 0:1], mv[:, 2:3], ALU.subtract, ALU.mult))
    done(nc.vector.tensor_tensor(src, src, g_row, ALU.mult))
    done(nc.vector.tensor_tensor(src, src, b_row, ALU.add))


def stage_mix_out(nc, mixT, w_out, ln_rows, hres, hT, h_dram, ident):
    with Scope(nc, "mixo") as s:
        ws = s.sb("ws", [P, 2, KT, NB])
        rows = s.sb("rows", [P, 2, D])
        stats = s.sb("stats", [P, 2, 6])
        mv = s.sb("mv", [P, 3])
        ps = s.ps("ps", [P, 8, NB])
        w_in, r_in = s.sem("w_in"), s.sem("r_in")
        turned, taken = s.sem("turned"), s.sem("taken")
        mm, v, root_ready, rooted, h_ready, h_out = (s.sem(n) for n in "mm vector_step root_ready rooted h_ready h_out".split())
        with nc.Block() as block:
            @block.sync
            def _(sp):
                for n in range(2):
                    sp.dma_start(ws[:, n, :, :], w_out[n]).then_inc(w_in, 16)
                for n in range(2):
                    sp.dma_start(rows[:, n, :], ln_rows[n].partition_broadcast(P)).then_inc(r_in, 16)
                for t in range(TT):
                    sp.wait_ge(h_ready, t + 1)
                    sp.dma_start(h_dram[t * P:(t + 1) * P, :], hres[:, t, :]).then_inc(h_out, 16)
                sp.wait_ge(h_out, 16 * TT)

            @block.tensor
            def _(pe):
                pe.wait_ge(w_in, 32)
                def turn(t):
                    pe.wait_ge(h_ready, t + 1)
                    if t >= 2:
                        pe.wait_ge(taken, 2 * t - 2)
                    for k in range(KT):
                        last = nc.tensor.transpose(ps[:, 4 + 2 * (t % 2) + k // 4, (k % 4) * P:(k % 4 + 1) * P],
                                                   hres[:, t, k * P:(k + 1) * P], ident[:])
                    last.then_inc(turned, 1)

                for t in range(TT):
                    b = 2 * (t % 2)
                    if t >= 2:
                        pe.wait_ge(h_ready, t - 1)
                    for n in range(2):
                        for k in range(KT):
                            last = nc.tensor.matmul(ps[:, b + n, :], lhsT=mixT[:, k, t * P:(t + 1) * P], rhs=ws[:, n, k, :],
                                                    start=(k == 0), stop=(k == KT - 1))
                    last.then_inc(mm, 1)
                    if t:
                        turn(t - 1)
                turn(TT - 1)

            @block.scalar
            def _(act):
                for t in range(TT + 1):
                    if t < TT:
                        act.wait_ge(root_ready, t + 1)
                        nc.scalar.activation(mv[:, 2:3], mv[:, 2:3], ACT.Sqrt).then_inc(rooted, 1)
                    if t:
                        act.wait_ge(turned, t)
                        for c in range(2):
                            nc.scalar.copy(hT[:, 4 * c:4 * c + 4, (t - 1) * P:t * P],
                                           ps[:, 4 + 2 * ((t - 1) % 2) + c, :].rearrange("p (k t) -> p k t", k=4)).then_inc(taken, 1)
                act.wait_ge(taken, 2 * TT)

            @block.vector
            def _(dve):
                step = [0]

                def done(ins):
                    step[0] += 1
                    ins.then_inc(v, 1)
                    dve.wait_ge(v, step[0])

                dve.wait_ge(r_in, 32)
                for t in range(TT):
                    dve.wait_ge(mm, t + 1)
                    b = 2 * (t % 2)
                    h = hres[:, t, :]
                    done(nc.vector.scalar_tensor_tensor(out=h, in0=h, scalar=ALPHA, in1=ps[:, b:b + 2, :].rearrange("p a b -> p (a b)"),
                                                        op0=ALU.mult, op1=ALU.add))
                    layer_norm_steps(nc, dve, h, stats, mv, rows[:, 0, :], rows[:, 1, :], t, done, root_ready, rooted)
                    dve.sem_inc(h_ready, 1)


GROUPS = 4
PER_GROUP = 8
EXPERTS = GROUPS * PER_GROUP
D_EXP = D // 4
LOGITS = GROUPS + EXPERTS
MAX_MORE = S // P - 1
OVERFLOW = 2 * S // P - 1
BLOCKS = EXPERTS + OVERFLOW
ROWS = BLOCKS * P
FAR = 1e30


def stage_router(nc, hT, w_router, b_router, counts_in, dest, wgt, over, row_tok, tok_of_row, y_dram, ones, cumul,
                 ident):
    IG, IE, IB, IJ = 0, GROUPS, GROUPS + EXPERTS, GROUPS + EXPERTS + OVERFLOW
    with Scope(nc, "rt") as s:
        wr = s.sb("wr", [P, KT, LOGITS])
        br = s.sb("br", [P, LOGITS])
        cnt = s.sb("cnt", [P, GROUPS + EXPERTS + OVERFLOW + MAX_MORE])
        lg = s.sb("lg", [P, TT, LOGITS])
        a1 = s.sb("a1", [P, TT, 12])
        g4 = s.sb("g4", [P, 3, TT, GROUPS])
        em = s.sb("em", [P, TT, EXPERTS])
        e32 = s.sb("e32", [P, TT, EXPERTS])
        oh = s.sb("oh", [P, 2, TT, EXPERTS])
        both = s.sb("both", [P, TT, EXPERTS])
        cum = s.sb("cum", [P, TT, EXPERTS])
        row = s.sb("row", [P, 6, EXPERTS])
        more = s.sb("more", [P, EXPERTS, MAX_MORE])
        ble = s.sb("ble", [P, OVERFLOW, EXPERTS])
        blk = s.sb("blk", [P, OVERFLOW + 1])
        dst = s.sb("dst", [P, 2, TT])
        tok = s.sb("tok", [P, TT], I32)
        zero = s.sb("zero", [BLOCKS, P], I32)
        back = s.sb("back", [BLOCKS, P], I32)
        backf = s.sb("backf", [BLOCKS, P])
        blank = s.sb("blank", [P, D])
        pl = s.ps("pl", [P, TT, 64])
        pc = s.ps("pc", [P, TT, EXPERTS])
        pn = s.ps("pn", [P, EXPERTS])
        pt = s.ps("pt", [P, BLOCKS])
        cleared = s.sem("cleared")
        w_in, mm, v, exp_in, exps = s.sem("w_in"), s.sem("mm"), s.sem("vector_step"), s.sem("exp_in"), s.sem("exps")
        both_ready, placed, tok_ready, zero_ready = s.sem("both_ready"), s.sem("placed"), s.sem("tok_ready"), s.sem("zero_ready")
        zeroed, scattered, back_in, backf_ready, turned, ready = (s.sem(n) for n in "zeroed scattered back_in backf_ready turned ready".split())
        with nc.Block() as block:
            @block.sync
            def _(sp):
                sp.dma_start(wr[:], w_router).then_inc(w_in, 16)
                sp.dma_start(br[:], b_router.partition_broadcast(P)).then_inc(w_in, 16)
                sp.dma_start(cnt[:], counts_in.partition_broadcast(P)).then_inc(w_in, 16)
                sp.wait_ge(zero_ready, 2)
                sp.dma_start(row_tok.rearrange("(b p) a -> b (p a)", p=P), zero[:]).then_inc(zeroed, 16)
                sp.wait_ge(scattered, 16 * 2 * TT)
                sp.dma_start(back[:], row_tok.rearrange("(b p) a -> b (p a)", p=P)).then_inc(back_in, 16)

            @block.tensor
            def _(pe):
                pe.wait_ge(w_in, 48)
                for t in range(TT):
                    for k in range(KT):
                        last = nc.tensor.matmul(pl[:, t, 0:LOGITS], lhsT=hT[:, k, t * P:(t + 1) * P], rhs=wr[:, k, :],
                                                start=(k == 0), stop=(k == KT - 1))
                last.then_inc(mm, 1)
                pe.wait_ge(both_ready, 1)
                for t in range(TT):
                    for j in range(t + 1):
                        last = nc.tensor.matmul(pc[:, t, :], lhsT=(cumul if j == t else ones)[:], rhs=both[:, j, :],
                                                start=(j == 0), stop=(j == t))
                for j in range(TT):
                    last = nc.tensor.matmul(pn[:], lhsT=ones[:], rhs=both[:, j, :], start=(j == 0), stop=(j == TT - 1))
                last.then_inc(mm, 1)
                pe.wait_ge(backf_ready, 1)
                nc.tensor.transpose(pt[:], backf[:], ident[0:BLOCKS, 0:BLOCKS]).then_inc(turned, 1)

            @block.scalar
            def _(act):
                act.wait_ge(zero_ready, 2)
                for n in range(EXPERTS, BLOCKS):
                    act.dma_start(y_dram[n * P:(n + 1) * P, :], blank[:]).then_inc(cleared, 16)
                act.wait_ge(exp_in, 1)
                nc.scalar.activation(g4[:, 1, :, :], g4[:, 1, :, :], ACT.Exp).then_inc(exps, 1)
                act.wait_ge(exp_in, 2)
                nc.scalar.activation(a1[:, :, 5], a1[:, :, 5], ACT.Exp).then_inc(exps, 1)
                act.wait_ge(cleared, 16 * OVERFLOW)

            @block.gpsimd
            def _(pool):
                nc.gpsimd.iota(tok[:], pattern=[[P, TT]], base=0, channel_multiplier=1).then_inc(tok_ready, 1)
                nc.gpsimd.memset(zero[:], 0).then_inc(zero_ready, 1)
                nc.gpsimd.memset(blank[:], 0.0).then_inc(zero_ready, 1)
                pool.wait_ge(tok_ready, 1)
                pool.wait_ge(zeroed, 16)
                pool.wait_ge(placed, 1)
                for c in range(2):
                    for t in range(TT):
                        nc.gpsimd.indirect_dma_start(out=row_tok, out_offset=bass.IndirectOffsetOnAxis(ap=dest[:, c, t:t + 1], axis=0),
                                                     in_=tok[:, t:t + 1], in_offset=None).then_inc(scattered, 16)

            @block.vector
            def _(dve):
                step = [0]
                tt, ts, stt, red = (nc.vector.tensor_tensor, nc.vector.tensor_scalar, nc.vector.scalar_tensor_tensor,
                                    nc.vector.tensor_reduce)

                def done(ins):
                    step[0] += 1
                    ins.then_inc(v, 1)
                    dve.wait_ge(v, step[0])

                def over_tokens(a, n):
                    return a.unsqueeze(1).to_broadcast([P, TT, n])

                def over_last(a, n):
                    return a.unsqueeze(2).to_broadcast([P, TT, n])

                def first_max(vals, n, iota, scratch, top, index, onehot):
                    done(red(top, vals, AX.X, ALU.max))
                    done(tt(scratch, vals, over_last(top, n), ALU.is_lt))
                    done(stt(out=scratch, in0=scratch, scalar=1000.0, in1=over_tokens(iota, n), op0=ALU.mult, op1=ALU.add))
                    done(red(index, scratch, AX.X, ALU.min))
                    done(tt(onehot, over_tokens(iota, n), over_last(index, n), ALU.is_equal))

                dve.wait_ge(w_in, 48)
                dve.wait_ge(mm, 1)
                done(tt(lg[:], pl[:, :, 0:LOGITS], over_tokens(br[:], LOGITS), ALU.add))
                iota_g, iota_e = cnt[:, IG:IG + GROUPS], cnt[:, IE:IE + EXPERTS]
                gl, el = lg[:, :, 0:GROUPS], lg[:, :, GROUPS:]
                first_max(gl, GROUPS, iota_g, g4[:, 0], a1[:, :, 0], a1[:, :, 1], g4[:, 2])
                tt(g4[:, 1], gl, over_last(a1[:, :, 0], GROUPS), ALU.subtract).then_inc(exp_in, 1)
                grp = g4[:, 2].unsqueeze(3).to_broadcast([P, TT, GROUPS, PER_GROUP])
                done(tt(em[:].rearrange("p t (g e) -> p t g e", g=GROUPS), el.rearrange("p t (g e) -> p t g e", g=GROUPS), grp,
                        ALU.mult))
                done(ts(g4[:, 0], g4[:, 2], -1.0, FAR, ALU.add, ALU.mult))
                done(tt(em[:].rearrange("p t (g e) -> p t g e", g=GROUPS), em[:].rearrange("p t (g e) -> p t g e", g=GROUPS),
                        g4[:, 0].unsqueeze(3).to_broadcast([P, TT, GROUPS, PER_GROUP]), ALU.add))
                first_max(em[:], EXPERTS, iota_e, e32[:], a1[:, :, 2], a1[:, :, 3], oh[:, 0])
                done(stt(out=em[:], in0=oh[:, 0], scalar=-3.0 * FAR, in1=em[:], op0=ALU.mult, op1=ALU.add))
                first_max(em[:], EXPERTS, iota_e, e32[:], a1[:, :, 4], a1[:, :, 6], oh[:, 1])
                tt(a1[:, :, 5], a1[:, :, 4], a1[:, :, 2], ALU.subtract).then_inc(exp_in, 1)
                tt(both[:], oh[:, 0], oh[:, 1], ALU.add).then_inc(both_ready, 1)
                dve.wait_ge(exps, 1)
                done(red(a1[:, :, 7], g4[:, 1], AX.X, ALU.add))
                dve.wait_ge(exps, 2)
                done(ts(a1[:, :, 8], a1[:, :, 5], 1.0, None, ALU.add))
                done(tt(a1[:, :, 7], a1[:, :, 7], a1[:, :, 8], ALU.mult))
                done(nc.vector.reciprocal(wgt[:, 0, :], a1[:, :, 7]))
                done(tt(wgt[:, 1, :], wgt[:, 0, :], a1[:, :, 5], ALU.mult))
                dve.wait_ge(mm, 2)
                done(nc.vector.tensor_copy(row[:, 0, :], pn[:]))
                done(tt(more[:], row[:, 0, :].unsqueeze(2).to_broadcast([P, EXPERTS, MAX_MORE]),
                        cnt[:, IJ:IJ + MAX_MORE].unsqueeze(1).to_broadcast([P, EXPERTS, MAX_MORE]), ALU.is_gt))
                done(red(row[:, 1, :], more[:], AX.X, ALU.add))
                done(nc.vector.memset(row[:, 2, :], 1.0))
                done(nc.vector.tensor_tensor_scan(row[:, 3, :], row[:, 2, :], row[:, 1, :], 0.0, ALU.mult, ALU.add))
                done(tt(row[:, 4, :], row[:, 3, :], row[:, 1, :], ALU.subtract))
                done(ts(row[:, 5, :], row[:, 4, :], float(P), float((EXPERTS - 1) * P), ALU.mult, ALU.add))
                done(tt(ble[:], row[:, 3, :].unsqueeze(1).to_broadcast([P, OVERFLOW, EXPERTS]),
                        cnt[:, IB:IB + OVERFLOW].unsqueeze(2).to_broadcast([P, OVERFLOW, EXPERTS]), ALU.is_le))
                done(red(blk[:, 0:OVERFLOW], ble[:], AX.X, ALU.add))
                done(ts(blk[:, 0:OVERFLOW], blk[:, 0:OVERFLOW], float(EXPERTS - 1), None, ALU.min))
                done(nc.vector.tensor_copy(blk[:, OVERFLOW:], row[:, 3, EXPERTS - 1:]))
                done(nc.vector.tensor_copy(over[:], blk[0:1, :]))
                done(nc.vector.tensor_copy(cum[:], pc[:]))
                for c in range(2):
                    e = a1[:, :, 3] if c == 0 else a1[:, :, 6]
                    done(tt(e32[:], oh[:, c], cum[:], ALU.mult))
                    done(red(a1[:, :, 9], e32[:], AX.X, ALU.add))
                    done(ts(a1[:, :, 9], a1[:, :, 9], -1.0, None, ALU.add))
                    done(tt(e32[:], oh[:, c], over_tokens(row[:, 5, :], EXPERTS), ALU.mult))
                    done(red(a1[:, :, 10], e32[:], AX.X, ALU.add))
                    done(stt(out=a1[:, :, 10], in0=e, scalar=-float(P), in1=a1[:, :, 10], op0=ALU.mult, op1=ALU.add))
                    done(ts(a1[:, :, 11], a1[:, :, 9], float(P), None, ALU.is_ge))
                    done(tt(a1[:, :, 10], a1[:, :, 10], a1[:, :, 11], ALU.mult))
                    done(stt(out=a1[:, :, 9], in0=e, scalar=float(P), in1=a1[:, :, 9], op0=ALU.mult, op1=ALU.add))
                    done(tt(dst[:, c, :], a1[:, :, 9], a1[:, :, 10], ALU.add))
                nc.vector.tensor_copy(dest[:], dst[:]).then_inc(placed, 1)
                dve.wait_ge(back_in, 16)
                nc.vector.tensor_copy(backf[:], back[:]).then_inc(backf_ready, 1)
                dve.wait_ge(turned, 1)
                nc.vector.tensor_copy(tok_of_row[:], pt[:]).then_inc(ready, 1)
                dve.wait_ge(ready, 1)


def stage_experts(nc, h_dram, w_gu, w_d, over, tok_of_row, y_dram, ident):
    NW = 4
    with Scope(nc, "ex") as s:
        gu = s.sb("gu", [P, NW, KT, 2 * D_EXP])
        dn = s.sb("dn", [P, NW, 2, D])
        idx = s.sb("idx", [P, NW], I32)
        xg = s.sb("xg", [P, NW, D])
        xT = s.sb("xT", [P, 2, KT, P])
        sil = s.sb("sil", [P, 2, D_EXP])
        hid = s.sb("hid", [P, 2, D_EXP])
        hT = s.sb("hT", [P, 2, 2, P])
        y = s.sb("y", [P, 2, D])
        px = s.ps("px", [P, 2, NB])
        pg = s.ps("pg", [P, 2, NB])
        ph = s.ps("ph", [P, 2, NB])
        py = s.ps("py", [P, 2, NB])
        names = "x_turned x_taken gated silu hidden h_turned h_taken downed y_taken_a y_taken_v"

        class Ring:
            pass

        pipe, more = Ring(), Ring()
        for ring, tag in ((pipe, "p"), (more, "o")):
            (ring.x_turned, ring.x_taken, ring.gated, ring.silu, ring.hidden, ring.h_turned, ring.h_taken, ring.downed,
             ring.y_taken_a, ring.y_taken_v) = (s.sem(f"{tag}_{n}") for n in names.split())
        w_in = [s.sem(f"w_in{n}") for n in range(NW)]
        x_in = [s.sem(f"x_in{n}") for n in range(NW)]
        y_out = [s.sem("y_out0"), s.sem("y_out1")]
        idx_ready, gate = s.sem("idx_ready"), s.sem("pool_gate")
        o_w_in, o_x_in, o_y_out, o_idx, o_stored = (s.sem(n) for n in "o_w_in o_x_in o_y_out o_idx o_stored".split())
        y_rows = y_dram.rearrange("(b p) d -> b p d", p=P)

        def number_of_overflow(eng):
            return eng.value_load(over[0:1, OVERFLOW:OVERFLOW + 1], min_val=0, max_val=OVERFLOW)

        with nc.Block() as block:
            @block.sync
            def _(sp):
                def load(b, n):
                    sp.dma_start(gu[:, n, :, :], w_gu[b]).then_inc(w_in[n], 16)
                    sp.dma_start(dn[:, n, :, :], w_d[b]).then_inc(w_in[n], 16)

                def store(b, n):
                    sp.wait_ge(pipe.y_taken_a, b + 2)
                    sp.wait_ge(pipe.y_taken_v, b + 2)
                    sp.dma_start(y_rows[b], y[:, n % 2, :]).then_inc(y_out[n % 2], 16)

                for n in range(NW):
                    load(n, n)
                with sp.Fori(0, EXPERTS // NW - 1) as j:
                    for n in range(NW):
                        store(NW * j + n, n)
                        sp.wait_ge(pipe.downed, NW * j + n + 3)
                        load(NW * j + n + NW, n)
                for b in range(EXPERTS - NW, EXPERTS):
                    store(b, b % NW)
                sp.wait_ge(pipe.downed, EXPERTS + 2)
                n_over = number_of_overflow(sp)
                with sp.Fori(0, OVERFLOW) as b:
                    with sp.If(b < n_over):
                        e = sp.value_load(over[0:1, bass.ds(b, 1)], min_val=0, max_val=EXPERTS - 1)
                        sp.wait_ge(more.downed, b + 1)
                        sp.dma_start(gu[:, 0, :, :], w_gu[e]).then_inc(o_w_in, 16)
                        sp.dma_start(dn[:, 0, :, :], w_d[e]).then_inc(o_w_in, 16)
                        sp.wait_ge(more.y_taken_a, b + 1)
                        sp.wait_ge(more.y_taken_v, b + 1)
                        sp.dma_start(y_rows[EXPERTS + b], y[:, 0, :]).then_inc(o_y_out, 16)
                        sp.wait_ge(o_y_out, 16 * b + 16)
                        sp.sem_inc(o_stored, 1)
                for n in range(2):
                    sp.wait_ge(y_out[n], 16 * (EXPERTS // 2 + 1))

            @block.gpsimd
            def _(pool):
                def gather(b, n, index):
                    nc.gpsimd.tensor_copy(idx[:, n:n + 1], tok_of_row[:, index]).then_inc(idx_ready, 1)
                    pool.wait_ge(idx_ready, b + 1)
                    pool.sem_inc(gate, 1)
                    nc.gpsimd.indirect_dma_start(out=xg[:, n, :], out_offset=None, in_=h_dram,
                                                 in_offset=bass.IndirectOffsetOnAxis(ap=idx[:, n:n + 1], axis=0)
                                                 ).then_inc(x_in[n], 16)

                for n in range(NW):
                    gather(n, n, slice(n, n + 1))
                with pool.Fori(1, EXPERTS // NW) as j:
                    for n in range(NW):
                        pool.wait_ge(pipe.x_turned, NW * j + n - NW + 1)
                        pool.sem_inc(gate, 1)
                        gather(NW * j + n, n, bass.ds(NW * j + n, 1))
                pool.wait_ge(pipe.x_turned, EXPERTS)
                n_over = number_of_overflow(pool)
                with pool.Fori(0, OVERFLOW) as b:
                    with pool.If(b < n_over):
                        pool.wait_ge(more.x_turned, b + 1)
                        pool.sem_inc(gate, 1)
                        nc.gpsimd.tensor_copy(idx[:, 0:1], tok_of_row[:, bass.ds(b + EXPERTS, 1)]).then_inc(o_idx, 1)
                        pool.wait_ge(o_idx, b + 1)
                        pool.sem_inc(gate, 1)
                        nc.gpsimd.indirect_dma_start(out=xg[:, 0, :], out_offset=None, in_=h_dram,
                                                     in_offset=bass.IndirectOffsetOnAxis(ap=idx[:, 0:1], axis=0)
                                                     ).then_inc(o_x_in, 16)

            @block.tensor
            def _(pe):
                def turn_x(ring, b, n):
                    for k in range(KT):
                        last = nc.tensor.transpose(px[:, k // 4, (k % 4) * P:(k % 4 + 1) * P], xg[:, n, k * P:(k + 1) * P],
                                                   ident[:])
                    last.then_inc(ring.x_turned, 1)

                def up(ring, b, n):
                    for k in range(KT):
                        last = nc.tensor.matmul(pg[:, n % 2, :], lhsT=xT[:, n % 2, k, :], rhs=gu[:, n, k, :], start=(k == 0),
                                                stop=(k == KT - 1))
                    last.then_inc(ring.gated, 1)

                def turn_h(ring, b, n):
                    for j in range(2):
                        last = nc.tensor.transpose(ph[:, n % 2, j * P:(j + 1) * P], hid[:, n % 2, j * P:(j + 1) * P], ident[:])
                    last.then_inc(ring.h_turned, 1)

                def down(ring, b, n):
                    for half in range(2):
                        for j in range(2):
                            last = nc.tensor.matmul(py[:, half, :], lhsT=hT[:, n % 2, j, :],
                                                    rhs=dn[:, n, j, half * NB:(half + 1) * NB], start=(j == 0), stop=(j == 1))
                    last.then_inc(ring.downed, 1)

                def p_turn_x(b, n, turn):
                    pe.wait_ge(x_in[n], 16 * turn)
                    pe.wait_ge(pipe.x_taken, b + 1)
                    turn_x(pipe, b, n)

                def p_up(b, n, turn):
                    pe.wait_ge(w_in[n], 32 * turn)
                    pe.wait_ge(pipe.x_taken, b + 2)
                    pe.wait_ge(pipe.hidden, b + 1)
                    up(pipe, b, n)

                def p_turn_h(b, n):
                    pe.wait_ge(pipe.hidden, b + 3)
                    pe.wait_ge(pipe.h_taken, b + 1)
                    turn_h(pipe, b, n)

                def p_down(b, n):
                    pe.wait_ge(pipe.h_taken, b + 3)
                    pe.wait_ge(pipe.y_taken_a, b + 1)
                    pe.wait_ge(pipe.y_taken_v, b + 1)
                    down(pipe, b, n)

                pe.sem_inc(pipe.gated, 2)
                pe.sem_inc(pipe.h_turned, 2)
                pe.sem_inc(pipe.downed, 2)
                pe.sem_inc(more.downed, 1)
                pe.sem_inc(more.x_turned, 1)
                p_turn_x(0, 0, 1)
                p_turn_x(1, 1, 1)
                p_up(0, 0, 1)
                with pe.Fori(0, EXPERTS // NW - 1) as j:
                    for n in range(NW):
                        b = NW * j + n
                        p_up(b + 1, (n + 1) % NW, j + 1 + (n + 1) // NW)
                        p_turn_h(b, n)
                        p_turn_x(b + 2, (n + 2) % NW, j + 1 + (n + 2) // NW)
                        p_down(b, n)
                for b in range(EXPERTS - NW, EXPERTS):
                    if b + 1 < EXPERTS:
                        p_up(b + 1, (b + 1) % NW, EXPERTS // NW)
                    p_turn_h(b, b % NW)
                    if b + 2 < EXPERTS:
                        p_turn_x(b + 2, (b + 2) % NW, EXPERTS // NW)
                    p_down(b, b % NW)
                pe.wait_ge(pipe.y_taken_a, EXPERTS + 1)
                pe.wait_ge(pipe.y_taken_v, EXPERTS + 1)
                n_over = number_of_overflow(pe)
                with pe.Fori(0, OVERFLOW) as b:
                    with pe.If(b < n_over):
                        pe.wait_ge(o_x_in, 16 * b + 16)
                        turn_x(more, b, 0)
                        pe.wait_ge(o_w_in, 32 * b + 32)
                        pe.wait_ge(more.x_taken, b + 1)
                        up(more, b, 0)
                        pe.wait_ge(more.hidden, b + 1)
                        turn_h(more, b, 0)
                        pe.wait_ge(more.h_taken, b + 1)
                        down(more, b, 0)

            @block.scalar
            def _(act):
                def take_x(ring, b, n):
                    nc.scalar.copy(xT[:, n % 2, :, :].rearrange("p a b -> p (a b)"),
                                   px[:].rearrange("p a b -> p (a b)")).then_inc(ring.x_taken, 1)

                def silu(ring, b, n):
                    nc.scalar.activation(sil[:, n % 2, :], pg[:, n % 2, 0:D_EXP], ACT.Silu).then_inc(ring.silu, 1)

                def take_y(ring, b, n):
                    nc.scalar.copy(y[:, n % 2, NB:], py[:, 1, :]).then_inc(ring.y_taken_a, 1)

                def p_take_x(b, n):
                    act.wait_ge(pipe.x_turned, b + 1)
                    act.wait_ge(pipe.gated, b + 1)
                    take_x(pipe, b, n)

                def p_silu(b, n):
                    act.wait_ge(pipe.gated, b + 3)
                    act.wait_ge(pipe.hidden, b + 1)
                    silu(pipe, b, n)

                def p_take_y(b, n, turn):
                    act.wait_ge(pipe.downed, b + 3)
                    act.wait_ge(y_out[n % 2], 16 * turn)
                    take_y(pipe, b, n)

                act.sem_inc(pipe.x_taken, 1)
                act.sem_inc(pipe.y_taken_a, 1)
                p_take_x(0, 0)
                p_take_x(1, 1)
                p_silu(0, 0)
                with act.Fori(0, EXPERTS // NW - 1) as j:
                    for n in range(NW):
                        b = NW * j + n
                        p_silu(b + 1, n + 1)
                        p_take_x(b + 2, n)
                        p_take_y(b, n, 2 * j + n // 2 + 1)
                for b in range(EXPERTS - NW, EXPERTS):
                    if b + 1 < EXPERTS:
                        p_silu(b + 1, b + 1)
                    if b + 2 < EXPERTS:
                        p_take_x(b + 2, b)
                    p_take_y(b, b, b // 2 + 1)
                act.wait_ge(y_out[0], 16 * (EXPERTS // 2 + 1))
                n_over = number_of_overflow(act)
                with act.Fori(0, OVERFLOW) as b:
                    with act.If(b < n_over):
                        act.wait_ge(more.x_turned, b + 2)
                        take_x(more, b, 0)
                        act.wait_ge(more.gated, b + 1)
                        silu(more, b, 0)
                        act.wait_ge(more.downed, b + 2)
                        act.wait_ge(o_stored, b + 1)
                        take_y(more, b, 0)

            @block.vector
            def _(dve):
                def hidden(ring, b, n):
                    nc.vector.tensor_tensor(hid[:, n % 2, :], pg[:, n % 2, D_EXP:], sil[:, n % 2, :], ALU.mult
                                            ).then_inc(ring.hidden, 1)

                def take_h(ring, b, n):
                    nc.vector.tensor_copy(hT[:, n % 2, :, :].rearrange("p a b -> p (a b)"), ph[:, n % 2, 0:2 * P]
                                          ).then_inc(ring.h_taken, 1)

                def take_y(ring, b, n):
                    nc.vector.tensor_copy(y[:, n % 2, 0:NB], py[:, 0, :]).then_inc(ring.y_taken_v, 1)

                def p_hidden(b, n):
                    dve.wait_ge(pipe.silu, b + 1)
                    dve.wait_ge(pipe.h_turned, b + 1)
                    hidden(pipe, b, n)

                def p_take_h(b, n):
                    dve.wait_ge(pipe.h_turned, b + 3)
                    dve.wait_ge(pipe.downed, b + 1)
                    take_h(pipe, b, n)

                def p_take_y(b, n, turn):
                    dve.wait_ge(pipe.downed, b + 3)
                    dve.wait_ge(y_out[n % 2], 16 * turn)
                    take_y(pipe, b, n)

                dve.sem_inc(pipe.hidden, 2)
                dve.sem_inc(pipe.h_taken, 2)
                dve.sem_inc(pipe.y_taken_v, 1)
                dve.sem_inc(y_out[0], 16)
                dve.sem_inc(y_out[1], 16)
                dve.sem_inc(o_stored, 1)
                p_hidden(0, 0)
                with dve.Fori(0, EXPERTS // NW - 1) as j:
                    for n in range(NW):
                        b = NW * j + n
                        p_hidden(b + 1, n + 1)
                        p_take_h(b, n)
                        p_take_y(b, n, 2 * j + n // 2 + 1)
                for b in range(EXPERTS - NW, EXPERTS):
                    if b + 1 < EXPERTS:
                        p_hidden(b + 1, b + 1)
                    p_take_h(b, b)
                    p_take_y(b, b, b // 2 + 1)
                dve.wait_ge(y_out[0], 16 * (EXPERTS // 2 + 1))
                n_over = number_of_overflow(dve)
                with dve.Fori(0, OVERFLOW) as b:
                    with dve.If(b < n_over):
                        dve.wait_ge(more.silu, b + 1)
                        hidden(more, b, 0)
                        dve.wait_ge(more.h_turned, b + 1)
                        take_h(more, b, 0)
                        dve.wait_ge(more.downed, b + 2)
                        dve.wait_ge(o_stored, b + 1)
                        take_y(more, b, 0)


def stage_combine(nc, hres, y_dram, dest, wgt, ln_rows, out_rows):
    with Scope(nc, "cmb") as s:
        rows = s.sb("rows", [P, 2, D])
        yg = s.sb("yg", [P, 4, 2, D])
        stats = s.sb("stats", [P, TT, 2, 6])
        mv = s.sb("mv", [P, TT, 4])
        r_in, g_in = s.sem("r_in"), [s.sem(f"g_in{n}") for n in range(4)]
        v, scaled, summed, root_ready, rooted, norm_ready, normed, gained, ready, stored = (s.sem(n) for n in (
            "vector_step scaled summed root_ready rooted norm_ready normed gained ready stored".split()))
        with nc.Block() as block:
            @block.sync
            def _(sp):
                for n in range(2):
                    sp.dma_start(rows[:, n, :], ln_rows[n].partition_broadcast(P)).then_inc(r_in, 16)
                for t in range(TT):
                    sp.wait_ge(ready, t + 1)
                    sp.dma_start(out_rows[t * P:(t + 1) * P, :], hres[:, t, :]).then_inc(stored, 16)
                sp.wait_ge(stored, 16 * TT)

            @block.gpsimd
            def _(pool):
                def gather(t):
                    if t >= 4:
                        pool.wait_ge(summed, t - 3)
                    for c in range(2):
                        nc.gpsimd.indirect_dma_start(out=yg[:, t % 4, c, :], out_offset=None, in_=y_dram,
                                                     in_offset=bass.IndirectOffsetOnAxis(ap=dest[:, c, t:t + 1], axis=0)
                                                     ).then_inc(g_in[t % 4], 16)

                for t in range(4):
                    gather(t)
                pool.wait_ge(r_in, 32)
                for t in range(TT):
                    if t + 4 < TT:
                        gather(t + 4)
                    pool.wait_ge(gained, t + 1)
                    nc.gpsimd.tensor_tensor(hres[:, t, :], hres[:, t, :], rows[:, 1, :], ALU.add).then_inc(ready, 1)

            @block.scalar
            def _(act):
                for t in range(TT):
                    nc.scalar.activation(hres[:, t, :], hres[:, t, :], ACT.Identity, scale=ALPHA).then_inc(scaled, 1)
                for t in range(TT):
                    act.wait_ge(root_ready, t + 1)
                    nc.scalar.activation(mv[:, t, 2:3], mv[:, t, 2:3], ACT.Sqrt).then_inc(rooted, 1)
                    act.wait_ge(norm_ready, t + 1)
                    nc.scalar.activation(hres[:, t, :], hres[:, t, :], ACT.Identity, scale=mv[:, t, 2:3],
                                         bias=mv[:, t, 3:4]).then_inc(normed, 1)

            @block.vector
            def _(dve):
                step = [0]

                def done(ins):
                    step[0] += 1
                    ins.then_inc(v, 1)
                    dve.wait_ge(v, step[0])

                def gain(t):
                    dve.wait_ge(normed, t + 1)
                    nc.vector.tensor_tensor(hres[:, t, :], hres[:, t, :], rows[:, 0, :], ALU.mult).then_inc(gained, 1)

                dve.wait_ge(r_in, 32)
                for t in range(TT):
                    h = hres[:, t, :]
                    dve.wait_ge(scaled, t + 1)
                    dve.wait_ge(g_in[t % 4], 32 * (t // 4 + 1))
                    done(nc.vector.scalar_tensor_tensor(out=h, in0=yg[:, t % 4, 0, :], scalar=wgt[:, 0, t:t + 1], in1=h,
                                                        op0=ALU.mult, op1=ALU.add))
                    nc.vector.scalar_tensor_tensor(out=h, in0=yg[:, t % 4, 1, :], scalar=wgt[:, 1, t:t + 1], in1=h,
                                                   op0=ALU.mult, op1=ALU.add).then_inc(summed, 1)
                    dve.wait_ge(summed, t + 1)
                    for c in range(2):
                        done(nc.vector.bn_stats(stats[:, t, c, :], h[:, c * NB:(c + 1) * NB]))
                    done(nc.vector.bn_aggr(mv[:, t, 0:2], stats[:, t, :, :].rearrange("p a b -> p (a b)")))
                    nc.vector.tensor_scalar(mv[:, t, 2:3], mv[:, t, 1:2], LN_EPS, None, ALU.add).then_inc(root_ready, 1)
                    if t:
                        gain(t - 1)
                    dve.wait_ge(rooted, t + 1)
                    done(nc.vector.reciprocal(mv[:, t, 2:3], mv[:, t, 2:3]))
                    nc.vector.scalar_tensor_tensor(out=mv[:, t, 3:4], in0=mv[:, t, 0:1], scalar=-1.0, in1=mv[:, t, 2:3],
                                                   op0=ALU.mult, op1=ALU.mult).then_inc(norm_ready, 1)
                gain(TT - 1)


def first_program(nc, A, xres, consts):
    ident, ones, cumul, ident16, future16 = consts
    with Scope(nc, "b1") as b:
        gates = b.sb("gates", [P, 2, D])
        modc = b.sb("modc", [P, 2, 2, KT])
        cols = b.sb("cols", [P, 9 * KT])
        silu = b.sb("silu", [P, KT])
        stage_modulation(nc, A["x"], A["cols1"], A["w_ada"], xres, modc, cols, silu, ones)
        with Scope(nc, "att_data") as a:
            qkv = a.sb("qkv", [P, TT, QKV])
            ss = a.sb("ss", [P, TT, 3 * HEADS])
            neg_f = a.sb("neg_f", [P, TT, HEADS])
            with Scope(nc, "h1") as h:
                hT = h.sb("hT", [P, KT, S])
                stage_norm(nc, "norm1", xres, hT, modc[:, 0], ident)
                stage_qkv(nc, hT, A["w_qkv"], A["w_f"], A["b_f"], qkv, ss, neg_f, cumul, ones)
            o_all = qkv[:, :, 0:D]
            with Scope(nc, "ada") as d:
                ada_sum = d.sb("ada_sum", [P, 4 * D])
                stage_attention(nc, qkv, ss, neg_f, A["qk_gain"], o_all, A["w_ada"], silu, ada_sum, ident, ident16,
                                future16)
                stage_modulation_rest(nc, ada_sum, A["b_ada"], cols, modc, gates, ones)
            stage_out(nc, "out1", o_all, A["w_o"], xres, gates[:, 0, :], ident,
                      qkv[:, 0, D:2 * D].rearrange("p (a c) -> p a c", a=2))
        with Scope(nc, "h2") as h:
            hT = h.sb("hT", [P, KT, S])
            stage_norm(nc, "norm2", xres, hT, modc[:, 1], ident)
            stage_mlp(nc, hT, A["w1"], A["w2"], xres, gates[:, 1, :], ident)



def second_program(nc, A, xres, h_dram, row_tok, y_dram, out_rows, consts):
    ident, ones, cumul = consts[:3]
    with Scope(nc, "b2") as b:
        dest = b.sb("dest", [P, 2, TT], I32)
        wgt = b.sb("wgt", [P, 2, TT])
        over = b.sb("over", [1, OVERFLOW + 1], I32)
        tok_of_row = b.sb("tok_of_row", [P, BLOCKS], I32)
        with Scope(nc, "mx") as m:
            mixT = m.sb("mixT", [P, KT, S])
            with Scope(nc, "x2") as x2:
                xT = x2.sb("xT", [P, KT, S])
                lora_in = x2.sb("lora_in", [P, 2, S])
                stage_turn(nc, "turn2", xres, xT, ident)
                stage_pool(nc, xT, A["w_head"], A["head_cols"], A["pool_w"], A["inv_count"], mixT, lora_in)
                stage_rwkv(nc, xT, A["w_rkv"], A["lora_up"], A["unit_cols"], A["window_consts"], A["scan_keep"], lora_in,
                           mixT, ident)
            hT = m.sb("hT", [P, KT, S])
            stage_mix_out(nc, mixT, A["w_mix"], A["ln1"], xres, hT, h_dram, ident)
            stage_router(nc, hT, A["w_router"], A["b_router"], A["counts"], dest, wgt, over, row_tok, tok_of_row, y_dram, ones,
                         cumul, ident)
        stage_experts(nc, h_dram, A["w_gu"], A["w_d"], over, tok_of_row, y_dram, ident)
        stage_combine(nc, xres, y_dram, dest, wgt, A["ln2"], out_rows)


def col(v):
    return v.reshape(-1, P).T


def chunks(w, n):
    k, m = w.shape
    return w.reshape(k // P, P, m // n, n).transpose(2, 1, 0, 3)


def layouts_second(np, I):
    wi = I["w_in_2"][0]
    pool, rw = wi[:, :256], wi[:, 256:]
    dr = PAIRS * P
    r, k, v = (rw[:, n * dr:(n + 1) * dr] for n in range(3))
    head = np.concatenate([pool, rw[:, 3 * dr:]], axis=1)
    mu = I["mu_shift_2"][0]
    windows = (2, 4, 8, 16)
    t = np.arange(S)
    w_of = np.repeat(np.array(windows), 64).reshape(2, P)
    inv_count = (1.0 / np.minimum(t[None, None, :16] + 1, w_of[:, :, None])).astype(np.float32).transpose(1, 0, 2)
    head_cols = np.concatenate([col(mu[3 * dr:]), col(I["pool_scale_2"][0]), (1.0 / w_of).astype(np.float32).T], axis=1)
    pool_w = np.zeros((P, 2, P), np.float32)
    for g in range(4):
        h = slice(64 * (g % 2), 64 * (g % 2) + 64)
        pool_w[h, g // 2, h] = I["pool_w_2"][0, g]
    rkv = np.stack([np.stack([chunks(w, P)[p] for w in (r, k, v)], axis=1) for p in range(PAIRS)])
    up = np.zeros((PAIRS, P, 3, P), np.float32)
    for p in range(PAIRS):
        c = slice(p * P, (p + 1) * P)
        up[p, :64, 0], up[p, 64:, 1], up[p, :, 2] = I["w_up_2"][0][:, c], I["a_up_2"][0][:, c], I["g_up_2"][0][:, c]
    per = [mu[0:dr], mu[dr:2 * dr], mu[2 * dr:3 * dr], I["w0_2"][0], I["a0_2"][0], I["k_k_2"][0], I["k_a_2"][0],
           I["r_k_2"][0].reshape(-1), I["lnx_g_2"][0], I["lnx_b_2"][0]]
    unit_cols = np.repeat(np.stack([col(a) for a in per], axis=2), WPAIRS, axis=1).reshape(P, PAIRS * WPAIRS * NPAR)
    a = np.arange(P)
    src, dst = a[:, None], a[None, :]
    masks = [src < dst, src <= dst, src < dst, src <= dst]
    for l in range(LEVELS):
        n = 1 << l
        masks.append((src // (2 * n) == dst // (2 * n)) & (src // n < dst // n))
    same = src // 64 == dst // 64
    cst = np.stack([m.astype(np.float32) for m in masks + [same]] + [same.astype(np.float32) / 64], axis=1)
    keep = np.broadcast_to((t[:2 * WIN] % WIN != 0).astype(np.float32), (P, 2 * WIN))
    return {
        "w_head": chunks(head, P).transpose(1, 0, 2, 3), "head_cols": head_cols, "pool_w": pool_w, "inv_count": inv_count,
        "w_rkv": rkv, "lora_up": up, "unit_cols": unit_cols, "window_consts": cst, "scan_keep": keep,
        "w_mix": chunks(I["w_out_2"][0], NB), "ln1": np.stack([I["ln1_g_2"][0], I["ln1_b_2"][0]]),
    }


def layouts_third(np, I):
    gu = np.concatenate([I["exp_gate_2"][0], I["exp_up_2"][0]], axis=2)
    counts = np.concatenate([np.arange(GROUPS), np.arange(EXPERTS), np.arange(OVERFLOW), P * np.arange(1, MAX_MORE + 1)])
    return {
        "w_router": np.concatenate([I["router_group_2"][0], I["router_expert_2"][0]], axis=1).reshape(KT, P, LOGITS)
        .transpose(1, 0, 2),
        "b_router": np.concatenate([I["router_group_b_2"][0], I["router_expert_b_2"][0]]),
        "counts": counts.astype(np.float32),
        "w_gu": gu.reshape(EXPERTS, KT, P, 2 * D_EXP).transpose(0, 2, 1, 3),
        "w_d": I["exp_down_2"][0].reshape(EXPERTS, 2, P, D).transpose(0, 2, 1, 3),
        "ln2": np.stack([I["ln2_g_2"][0], I["ln2_b_2"][0]]),
    }


def layouts_first(np, I):
    wi = I["fox_w_in"][0]
    return {
        "x": I["x"][0],
        "cols1": np.concatenate([col(I["c"][0]), col(I["b_ada"][0]), col(I["norm_mix"][0]), col(I["norm_mlp"][0])], axis=1),
        "w_ada": I["w_ada"][0],
        "b_ada": I["b_ada"][0],
        "w_qkv": chunks(wi[:, :QKV], QN),
        "w_f": wi[:, QKV:].reshape(KT, P, HEADS).transpose(1, 0, 2),
        "b_f": I["fox_b_f"][0],
        "qk_gain": np.stack([I["fox_q_norm"][0], I["fox_k_norm"][0]], axis=1),
        "w_o": chunks(I["fox_w_out"][0], NB),
        "w1": chunks(I["w_mlp_in"][0], P),
        "w2": I["w_mlp_out"][0].reshape(FT, P, D),
    }


def kernel(**inputs):
    import numpy as np
    import concourse.bacc as _bacc
    from concourse.bass_utils import run_bass_kernel_spmd as _run

    I = {k: np.asarray(v) for k, v in inputs.items()}
    L = {**layouts_first(np, I), **layouts_second(np, I), **layouts_third(np, I)}
    nc = _bacc.Bacc("TRN2", target_bir_lowering=False, num_devices=1)
    arrays, A = {}, {}
    for name, a in L.items():
        a = np.ascontiguousarray(a)
        arrays[f"in_{name}"] = a
        A[name] = nc.dram_tensor(f"in_{name}", a.shape, mybir.dt.from_np(a.dtype), kind="ExternalInput").ap()
    out = nc.dram_tensor("out_0", (1, S, D), F32, kind="ExternalOutput").ap()
    h_rows = nc.dram_tensor("h_rows", (S, D), F32, kind="Internal").ap()
    row_tok = nc.dram_tensor("row_tok", (ROWS, 1), I32, kind="Internal").ap()
    y_rows = nc.dram_tensor("y_rows", (ROWS, D), F32, kind="Internal").ap()
    USED.clear()
    with Scope(nc, "all") as g:
        consts = constants(nc, g)
        xres = g.sb("xres", [P, TT, D])
        first_program(nc, A, xres, consts)
        clear_semaphores(nc)
        second_program(nc, A, xres, h_rows, row_tok, y_rows, out.rearrange("b s d -> (b s) d"), consts)
    r = _run(nc, [arrays], core_ids=[0])
    return r.results[0]["out_0"]
```
